# Optimizing a Trainium2 kernel written in Bass

```python
import math, functools
import jax, jax.numpy as jnp
from jax import lax
import numpy as np

D_MODEL = 1024
BATCH = 1
SEQ = 512
DEPTH = 1
DEC_BATCH = 8
DEC_SEQ = 8
PAST_LEN = 2048
PAGE_SIZE = 128

MLA_HEADS = 8
MLA_Q_RANK = 256
MLA_KV_RANK = 128
MLA_NOPE = 64
MLA_ROPE = 32
MLA_V = 64
DSA_HEADS = 8
DSA_KV_HEADS = 2
DSA_HEAD_DIM = 64
IDX_HEADS = 8
IDX_DIM = 64
DSA_TOPK_MAX = 256
MIX_WIDTH = MLA_HEADS * MLA_V + DSA_HEADS * DSA_HEAD_DIM
IN_SPLITS = (MLA_Q_RANK, MLA_KV_RANK, MLA_ROPE, DSA_HEADS * DSA_HEAD_DIM, DSA_KV_HEADS * DSA_HEAD_DIM,
             DSA_KV_HEADS * DSA_HEAD_DIM, IDX_HEADS * IDX_DIM, IDX_HEADS, IDX_DIM)
IN_WIDTH = sum(IN_SPLITS)
N_MEM = 256
X_HEADS = 4
X_HEAD_DIM = 64
PEER_HEADS = 8
PEER_N_KEYS = 128
PEER_N_EXPERTS = PEER_N_KEYS * PEER_N_KEYS
PEER_KEY_DIM = 256
PEER_TOPK = 16
PEER_TOKEN_BLOCK = 256
ROPE_THETA = 10000.0
NORM_EPS = 1e-6
Q_BLOCK = 128

kernel_name = 'mla_dsa_peer_hybrid_step'

def rms_norm(x, g):
    xf = x.astype(jnp.float32)
    y = xf * lax.rsqrt(jnp.mean(xf * xf, axis=-1, keepdims=True) + NORM_EPS)
    return (y * g.astype(jnp.float32)).astype(x.dtype)

def rope(x, pos):
    half = x.shape[-1] // 2
    inv = ROPE_THETA ** (-jnp.arange(half, dtype=jnp.float32) / half)
    ang = pos.astype(jnp.float32)[:, None] * inv[None, :]
    ang = ang.reshape((pos.shape[0],) + (1,) * (x.ndim - 3) + (half,))
    cos, sin = jnp.cos(ang), jnp.sin(ang)
    xf = x.astype(jnp.float32)
    x1, x2 = xf[..., :half], xf[..., half:]
    return jnp.concatenate([x1 * cos - x2 * sin, x2 * cos + x1 * sin], axis=-1).astype(x.dtype)

def map_query_blocks(fn, *xs):
    t = xs[0].shape[1]
    qb = Q_BLOCK if t % Q_BLOCK == 0 else t
    nb = t // qb
    if nb == 1:
        return fn(*xs)
    blocks = tuple(x.reshape((x.shape[0], nb, qb) + x.shape[2:]).swapaxes(0, 1) for x in xs)
    out = lax.map(lambda bl: fn(*bl), blocks)
    return out.swapaxes(0, 1).reshape((out.shape[1], t) + out.shape[3:])

def gather_pages(pool, page_table):
    rows = pool[page_table]
    return rows.reshape((rows.shape[0], rows.shape[1] * rows.shape[2]) + rows.shape[3:])

def gather_rows(kv, idx):
    return jax.vmap(lambda a, i: a[i])(kv, idx)

def gather_paged_rows(pool, page_table, new, idx):
    flat = pool.reshape((-1,) + pool.shape[2:])
    past_len = page_table.shape[1] * pool.shape[1]
    def one(pt, nw, i):
        sp = jnp.minimum(i, past_len - 1)
        phys = pt[sp // PAGE_SIZE] * PAGE_SIZE + sp % PAGE_SIZE
        from_new = nw[jnp.clip(i - past_len, 0, nw.shape[0] - 1)]
        is_past = (i < past_len).reshape(i.shape + (1,) * (flat.ndim - 1))
        return jnp.where(is_past, flat[phys], from_new)
    return jax.vmap(one)(page_table, new, idx)

def mixer_inputs(xn, pos, w_in, mla_q_norm, w_uq, mla_kv_norm, w_uk):
    b, t, _ = xn.shape
    offs = [int(v) for v in np.cumsum(IN_SPLITS)[:-1]]
    cq, ckv, kr, dq, dk, dv, iq, iw, ik = jnp.split(xn @ w_in, offs, axis=-1)
    q = (rms_norm(cq, mla_q_norm) @ w_uq).reshape(b, t, MLA_HEADS, MLA_NOPE + MLA_ROPE)
    q_lat = jnp.einsum('bthn,chn->bthc', q[..., :MLA_NOPE], w_uk)
    q_r = rope(q[..., MLA_NOPE:], pos)
    ckv = rms_norm(ckv, mla_kv_norm)
    kr = rope(kr, pos)
    dq = rope(dq.reshape(b, t, DSA_HEADS, DSA_HEAD_DIM), pos)
    dk = rope(dk.reshape(b, t, DSA_KV_HEADS, DSA_HEAD_DIM), pos)
    kv = jnp.stack([dk, dv.reshape(b, t, DSA_KV_HEADS, DSA_HEAD_DIM)], axis=2)
    iq = rope(iq.reshape(b, t, IDX_HEADS, IDX_DIM), pos)
    ik = rope(ik, pos)
    return q_lat, q_r, ckv, kr, dq, kv, iq, iw, ik

def mla_attend(q_lat, q_r, q_pos, ckv, kr):
    scale = (MLA_NOPE + MLA_ROPE) ** -0.5
    k_pos = jnp.arange(ckv.shape[1])
    def block(ql, qr, qp):
        s = (jnp.einsum('bthc,bsc->bhts', ql, ckv).astype(jnp.float32)
             + jnp.einsum('bthr,bsr->bhts', qr, kr).astype(jnp.float32)) * scale
        causal = k_pos[None, :] <= qp[0][:, None]
        p = jax.nn.softmax(jnp.where(causal[None, None], s, -jnp.inf), axis=-1).astype(ckv.dtype)
        return jnp.einsum('bhts,bsc->bthc', p, ckv)
    return map_query_blocks(block, q_lat, q_r, q_pos)

def dsa_attend(q, iq, iw, q_pos, ik, topk, fetch_kv):
    k_pos = jnp.arange(ik.shape[1])
    group = DSA_HEADS // DSA_KV_HEADS
    def block(qb, iqb, iwb, qp):
        b, t = qb.shape[:2]
        dots = jnp.einsum('bthd,bsd->bths', iqb, ik).astype(jnp.float32)
        score = jnp.einsum('bth,bths->bts', iwb.astype(jnp.float32), jax.nn.relu(dots))
        causal = k_pos[None, :] <= qp[0][:, None]
        _, idx = lax.top_k(jnp.where(causal[None], score, -jnp.inf), topk)
        valid = idx <= qp[0][None, :, None]
        kv = fetch_kv(idx)
        kg, vg = kv[:, :, :, 0], kv[:, :, :, 1]
        qg = qb.reshape(b, t, DSA_KV_HEADS, group, DSA_HEAD_DIM)
        s = jnp.einsum('btgnd,btkgd->btgnk', qg, kg).astype(jnp.float32) * DSA_HEAD_DIM ** -0.5
        p = jax.nn.softmax(jnp.where(valid[:, :, None, None, :], s, -jnp.inf), axis=-1).astype(vg.dtype)
        return jnp.einsum('btgnk,btkgd->btgnd', p, vg).reshape(b, t, DSA_HEADS, DSA_HEAD_DIM)
    return map_query_blocks(block, q, iq, iw, q_pos)

def mixer_output(o_lat, o_dsa, w_uv, w_o):
    b, t = o_lat.shape[:2]
    o_mla = jnp.einsum('bthc,chv->bthv', o_lat, w_uv).reshape(b, t, MLA_HEADS * MLA_V)
    return jnp.concatenate([o_mla, o_dsa.reshape(b, t, DSA_HEADS * DSA_HEAD_DIM)], axis=-1) @ w_o

def memory_kv(mem, mem_norm, wk_x, wv_x):
    b, m, _ = mem.shape
    mn = rms_norm(mem, mem_norm)
    return ((mn @ wk_x).reshape(b, m, X_HEADS, X_HEAD_DIM), (mn @ wv_x).reshape(b, m, X_HEADS, X_HEAD_DIM))

def cross_attend(hn, k, v, wq_x, wo_x):
    b, t, _ = hn.shape
    q = (hn @ wq_x).reshape(b, t, X_HEADS, X_HEAD_DIM)
    s = jnp.einsum('bthd,bmhd->bhtm', q, k).astype(jnp.float32) * X_HEAD_DIM ** -0.5
    p = jax.nn.softmax(s, axis=-1).astype(v.dtype)
    return jnp.einsum('bhtm,bmhd->bthd', p, v).reshape(b, t, X_HEADS * X_HEAD_DIM) @ wo_x

def peer(xn, w_pq, peer_keys, peer_u, peer_v):
    b, t, d = xn.shape
    n = b * t
    blk = min(PEER_TOKEN_BLOCK, n)
    nb = -(-n // blk)
    flat = jnp.pad(xn.reshape(n, d), ((0, nb * blk - n), (0, 0)))
    def block(xb):
        q = (xb @ w_pq).reshape(blk, PEER_HEADS, 2, PEER_KEY_DIM // 2)
        s = jnp.einsum('nhpd,hpkd->nhpk', q, peer_keys).astype(jnp.float32)
        s_top, i_top = lax.top_k(s, PEER_TOPK)
        cand = (s_top[:, :, 0, :, None] + s_top[:, :, 1, None, :]).reshape(blk, PEER_HEADS, -1)
        cand_idx = (i_top[:, :, 0, :, None] * PEER_N_KEYS + i_top[:, :, 1, None, :]).reshape(blk, PEER_HEADS, -1)
        g_s, g_i = lax.top_k(cand, PEER_TOPK)
        e = jnp.take_along_axis(cand_idx, g_i, axis=-1)
        g = jax.nn.softmax(g_s, axis=-1)
        act = jax.nn.gelu(jnp.einsum('nd,nhkd->nhk', xb, peer_u[e]).astype(jnp.float32), approximate=False)
        return jnp.einsum('nhk,nhkd->nd', (g * act).astype(xb.dtype), peer_v[e])
    out = lax.map(block, flat.reshape(nb, blk, d))
    return out.reshape(nb * blk, d)[:n].reshape(b, t, d)

def setup_inputs(seed: int = 0) -> dict:
    key = jax.random.key(seed)
    ks = jax.random.split(key, 40)
    cnt = [0]
    def nxt():
        k = ks[cnt[0]]
        cnt[0] += 1
        return k
    def nrm(shape, scale=1.0):
        return jax.random.normal(nxt(), shape, jnp.float32) * scale
    def gain(shape):
        return 1.0 + 0.01 * nrm(shape)
    n_pages = PAST_LEN // PAGE_SIZE
    n_pool = (DEC_BATCH * n_pages * 5) // 4
    L, D = DEPTH, D_MODEL
    inp = {}
    inp['x_prompt'] = nrm((BATCH, SEQ, D))
    inp['x_sample'] = nrm((DEC_BATCH, DEC_SEQ, D))
    inp['cache_mla_ckv'] = nrm((L, n_pool, PAGE_SIZE, MLA_KV_RANK))
    inp['cache_mla_kr'] = nrm((L, n_pool, PAGE_SIZE, MLA_ROPE))
    inp['cache_dsa_kv'] = nrm((L, n_pool, PAGE_SIZE, 2, DSA_KV_HEADS, DSA_HEAD_DIM))
    inp['cache_dsa_idx'] = nrm((L, n_pool, PAGE_SIZE, IDX_DIM))
    inp['cache_mem_k'] = nrm((L, DEC_BATCH, N_MEM, X_HEADS, X_HEAD_DIM))
    inp['cache_mem_v'] = nrm((L, DEC_BATCH, N_MEM, X_HEADS, X_HEAD_DIM))
    inp['page_table'] = jax.random.permutation(nxt(), n_pool)[:DEC_BATCH * n_pages].reshape(DEC_BATCH, n_pages).astype(jnp.int32)
    inp['mem_prompt'] = nrm((BATCH, N_MEM, D))
    inp['norm_mix'] = gain((L, D))
    inp['w_in'] = nrm((L, D, IN_WIDTH), D ** -0.5)
    inp['mla_q_norm'] = gain((L, MLA_Q_RANK))
    inp['w_uq'] = nrm((L, MLA_Q_RANK, MLA_HEADS * (MLA_NOPE + MLA_ROPE)), MLA_Q_RANK ** -0.5)
    inp['mla_kv_norm'] = gain((L, MLA_KV_RANK))
    inp['w_uk'] = nrm((L, MLA_KV_RANK, MLA_HEADS, MLA_NOPE), MLA_KV_RANK ** -0.5)
    inp['w_uv'] = nrm((L, MLA_KV_RANK, MLA_HEADS, MLA_V), MLA_KV_RANK ** -0.5)
    inp['w_o'] = nrm((L, MIX_WIDTH, D), MIX_WIDTH ** -0.5)
    inp['norm_mem'] = gain((L, D))
    inp['mem_norm'] = gain((L, D))
    inp['wq_x'] = nrm((L, D, X_HEADS * X_HEAD_DIM), D ** -0.5)
    inp['wk_x'] = nrm((L, D, X_HEADS * X_HEAD_DIM), D ** -0.5)
    inp['wv_x'] = nrm((L, D, X_HEADS * X_HEAD_DIM), D ** -0.5)
    inp['wo_x'] = nrm((L, X_HEADS * X_HEAD_DIM, D), (X_HEADS * X_HEAD_DIM) ** -0.5)
    inp['norm_ffn'] = gain((L, D))
    inp['w_pq'] = nrm((L, D, PEER_HEADS * PEER_KEY_DIM), D ** -0.5)
    inp['peer_keys'] = nrm((L, PEER_HEADS, 2, PEER_N_KEYS, PEER_KEY_DIM // 2), (PEER_KEY_DIM // 2) ** -0.5)
    inp['peer_u'] = nrm((L, PEER_N_EXPERTS, D), D ** -0.5)
    inp['peer_v'] = nrm((L, PEER_N_EXPERTS, D), PEER_HEADS ** -0.5)
    inp['norm_final'] = gain((D,))
    return inp

def reference(x_prompt, x_sample, cache_mla_ckv, cache_mla_kr, cache_dsa_kv, cache_dsa_idx, cache_mem_k,
              cache_mem_v, page_table, mem_prompt, norm_mix, w_in, mla_q_norm, w_uq, mla_kv_norm, w_uk, w_uv,
              w_o, norm_mem, mem_norm, wq_x, wk_x, wv_x, wo_x, norm_ffn, w_pq, peer_keys, peer_u, peer_v,
              norm_final):
    k_prompt = min(DSA_TOPK_MAX, SEQ // 4)
    k_sample = min(DSA_TOPK_MAX, (PAST_LEN + DEC_SEQ) // 4)
    pos_p = jnp.arange(SEQ)
    pos_s = PAST_LEN + jnp.arange(DEC_SEQ)
    h_p, h_s = x_prompt, x_sample
    ckv_p_l, kr_p_l, kv_p_l, ik_p_l, mk_p_l, mv_p_l = [], [], [], [], [], []
    ckv_s_l, kr_s_l, kv_s_l, ik_s_l = [], [], [], []
    for l in range(DEPTH):
        xn = rms_norm(h_p, norm_mix[l])
        q_lat, q_r, ckv, kr, dq, kv, iq, iw, ik = mixer_inputs(xn, pos_p, w_in[l], mla_q_norm[l], w_uq[l],
                                                               mla_kv_norm[l], w_uk[l])
        o_lat = mla_attend(q_lat, q_r, pos_p[None], ckv, kr)
        o_dsa = dsa_attend(dq, iq, iw, pos_p[None], ik, k_prompt, functools.partial(gather_rows, kv))
        h_p = h_p + mixer_output(o_lat, o_dsa, w_uv[l], w_o[l])
        ckv_p_l.append(ckv); kr_p_l.append(kr); kv_p_l.append(kv); ik_p_l.append(ik)
        xn = rms_norm(h_s, norm_mix[l])
        q_lat, q_r, ckv_s, kr_s, dq, kv_s, iq, iw, ik_s = mixer_inputs(xn, pos_s, w_in[l], mla_q_norm[l], w_uq[l],
                                                                       mla_kv_norm[l], w_uk[l])
        ckv_all = jnp.concatenate([gather_pages(cache_mla_ckv[l], page_table), ckv_s], axis=1)
        kr_all = jnp.concatenate([gather_pages(cache_mla_kr[l], page_table), kr_s], axis=1)
        ik_all = jnp.concatenate([gather_pages(cache_dsa_idx[l], page_table), ik_s], axis=1)
        o_lat = mla_attend(q_lat, q_r, pos_s[None], ckv_all, kr_all)
        o_dsa = dsa_attend(dq, iq, iw, pos_s[None], ik_all, k_sample,
                           functools.partial(gather_paged_rows, cache_dsa_kv[l], page_table, kv_s))
        h_s = h_s + mixer_output(o_lat, o_dsa, w_uv[l], w_o[l])
        ckv_s_l.append(ckv_s); kr_s_l.append(kr_s); kv_s_l.append(kv_s); ik_s_l.append(ik_s)
        mk_p, mv_p = memory_kv(mem_prompt, mem_norm[l], wk_x[l], wv_x[l])
        mk_p_l.append(mk_p); mv_p_l.append(mv_p)
        h_p = h_p + cross_attend(rms_norm(h_p, norm_mem[l]), mk_p, mv_p, wq_x[l], wo_x[l])
        h_s = h_s + cross_attend(rms_norm(h_s, norm_mem[l]), cache_mem_k[l], cache_mem_v[l], wq_x[l], wo_x[l])
        h_p = h_p + peer(rms_norm(h_p, norm_ffn[l]), w_pq[l], peer_keys[l], peer_u[l], peer_v[l])
        h_s = h_s + peer(rms_norm(h_s, norm_ffn[l]), w_pq[l], peer_keys[l], peer_u[l], peer_v[l])
    y_prompt = rms_norm(h_p, norm_final)
    y_sample = rms_norm(h_s, norm_final)
    return (y_prompt, y_sample, jnp.stack(ckv_p_l), jnp.stack(kr_p_l), jnp.stack(kv_p_l), jnp.stack(ik_p_l),
            jnp.stack(mk_p_l), jnp.stack(mv_p_l), jnp.stack(ckv_s_l), jnp.stack(kr_s_l), jnp.stack(kv_s_l),
            jnp.stack(ik_s_l))


_drawn_inputs = setup_inputs


def setup_inputs(seed=0):
    import zlib

    import numpy as np

    out = dict(_drawn_inputs(seed))
    spreads = {}
    factors = {'norm_mix': 3.021,
     'mla_q_norm': 8.0,
     'mla_kv_norm': 5.698,
     'norm_mem': 8.0,
     'mem_norm': 5.676,
     'norm_ffn': 14.507,
     'norm_final': 34.445}
    for name, (base, spread) in spreads.items():
        noise = np.random.default_rng([zlib.crc32(name.encode()), seed]).standard_normal(out[name].shape)
        drawn = base * np.exp(spread * noise) if base else spread * noise
        out[name] = __import__('jax').numpy.asarray(drawn.astype(out[name].dtype))
    for name, factor in factors.items():
        out[name] = (out[name] * factor).astype(out[name].dtype)
    return out
```

```python
from contextlib import ExitStack

import numpy as np
import concourse.bass as bass
from concourse import mybir
from concourse.alu_op_type import AluOpType as ALU

F32 = mybir.dt.float32
F32R = mybir.dt.float32r
BF16 = mybir.dt.bfloat16
U32 = mybir.dt.uint32
I32 = mybir.dt.int32
ACT = mybir.ActivationFunctionType
AX = mybir.AxisListType.X

P = 128
D = 1024
KD = D // P
SEQ, NB, NQ = 512, 8, 8
NS = NB * NQ
NTOK = SEQ + NS
NBLK = SEQ // P + 1
PAGE, NPAGE = 128, 16
PAST = PAGE * NPAGE
NEWC = PAST + NS
W_IN = 1768
CQ, CKV, KR, DQ, DK, DV, IQ, IW, IK = 0, 256, 384, 416, 928, 1056, 1184, 1696, 1704
PC = W_IN // 4
EPS = 1e-6
NEG = -1e30
TAKEN = -3e38
K_PROMPT, K_SAMPLE = 128, 256
MLA_SCALE = 96 ** -0.5
DSA_SCALE = 64 ** -0.5
NKEY, PH, PK = 128, 8, 16
BANK = 512

C_ID, C_IOTA, C_CAUSAL, C_NEW, C_SAME, C_COS, C_SIN = 0, 128, 256, 384, 448, 960, 1280
C_ALL = 1600


def rows(t):
    return P if t < NBLK - 1 else NS


def toks(t):
    return slice(t * P, t * P + rows(t))


def block_a(nc, T, h, sems):
    ctx = ExitStack()
    with ctx:
        def sb(name, shape, dt=F32):
            return ctx.enter_context(nc.sbuf_tensor(name, shape, dt))

        def sem(name):
            return sems.enter_context(nc.semaphore(name))

        PS = ctx.enter_context(nc.psum_tensor("psA", [P, 8 * BANK], F32))

        def bank(b, n=BANK, at=0, p0=0, p1=P):
            return PS[p0:p1, b * BANK + at:b * BANK + at + n]

        cst = sb("cst", [P, C_ALL])
        xT = sb("xT", [P, KD, NTOK])
        gcol = sb("gcol", [P, 4 * KD + 2])
        gkv = sb("gkv", [P, P])
        st = sb("st", [P, 160])
        sm = sb("sm", [P, 4 * 100])
        ssm = sb("ssm", [P, 4, NB])
        pts = sb("pts", [1, NB * NPAGE], I32)
        qrTs = sb("qrTs", [32, NB, 64])
        bdq = sb("bdq", [P, NB, 2, 4, NQ])
        Dp = sb("Dp", [P, 4, NS])
        same16 = sb("same16", [NS, NB, 64], BF16)
        id16 = sb("id16", [P, P], BF16)
        causal16 = sb("causal16", [P, P], BF16)
        m8 = sb("m8", [P, 8])
        qlTs = sb("qlTs", [P, NB, 8, NQ])
        olT = sb("olT", [P, NB, 8, NQ])
        arena = sb("arena", [P, 37800])

        def region(at, *shape, p=P):
            n = int(np.prod(shape))
            a = arena[0:p, at:at + n]
            if len(shape) == 1:
                return a
            names = "abcd"[:len(shape)]
            spec = f"p ({' '.join(names)}) -> p {' '.join(names)}"
            return a.rearrange(spec, **{k: v for k, v in zip(names[1:], shape[1:])})

        win = region(0, KD, W_IN)
        proj = region(14144, NBLK, W_IN)
        kT = region(22984, 4, NTOK)
        dqT = region(25288, 4, NTOK)
        iqT = region(27592, 4, SEQ)
        iqTs = region(29640, NB, 8, NQ, p=64)
        cqT = region(30152, 2, NTOK)
        xs = region(31304, 2, D)
        ropeA = region(33352, 640)
        ropeM = region(33992, 640)
        kk = region(34632, 256)
        w_uqn = region(34888, 2, 512)
        w_uqr = region(35912, 2, 256)
        w_ukT = region(36424, 4, P)
        w_uv = region(36936, 512)
        qnT = region(0, 4, NTOK)
        qlT = region(2304, 8, SEQ)
        qrT = region(6400, 2, NTOK)
        Vm = region(7552, 4, 512)
        mb16 = region(9600, 4 * SEQ // 2).bitcast(BF16).rearrange("p (a b) -> p a b", a=4)
        accs = region(10624, 3, SEQ)
        relu = region(12160, 2, SEQ)
        qr = region(13184, 256)
        Pr = region(31304, 3, SEQ)
        PT = region(33352, 2, SEQ)
        Kp = region(0, 2, NPAGE, 256)
        Vp = region(8192, 2, NPAGE, 256)
        krTp = region(16384, 2, PAST, p=32)
        sw = region(8192, NEWC, p=NS)
        ikp = region(10304, 4, 512, p=64)
        relus = region(12352, 2, 512)
        selE = region(13376, NB, 8, NQ, p=NS)
        Ps = region(25288, 2, NEWC)
        mbs = region(30152, NEWC // 2, p=NS).bitcast(BF16)
        PTs = region(31304, 2, SEQ)
        w_o = region(0, KD, D)
        wqx = region(8192, KD, 256)
        wkv = region(10240, KD, 512)
        memr = region(14336, 2, D)
        mT = region(16384, KD, 256)
        mkv = region(18432, 2, 512)
        mkT = region(19456, 2, 256)
        qxT = region(19968, 2, NTOK)
        bdx = region(21120, 2, NB, 4, NQ)
        oxT = region(21632, 2, NTOK)
        xc = region(22784, NB, 4, 256)
        wox = region(34888, 2, D)
        assert 22784 + 8192 <= 31304

        ident = cst[:, C_ID:C_ID + P]
        causal = cst[:, C_CAUSAL:C_CAUSAL + P]
        same = cst[0:NS, C_SAME:C_SAME + 512]
        cosT = cst[:, C_COS:C_COS + 320].rearrange("p (t c) -> p t c", t=NBLK)
        sinT = cst[:, C_SIN:C_SIN + 320].rearrange("p (t c) -> p t c", t=NBLK)

        names = """cst_in x_in win_in wsm_in pt_in mem_in wqx_in wkv_in wox_in wo_in xc_in gk_in
            sq_done ms_done rstd_done xs_done tp_done xT_done pj_mm pj_act pj_dve
            sq2_done ms2_done rstd2_done cq_done ckv_done rp_dve rp_pool c16 half_ready ioA
            tA_mm tB_mm tA_ev tB_ev up_mm up_ev ql_mm ql_ev qr_mm qr_chain qr_done qr_tp qr_ev 
            vm_mm vm_ev ix_mm ix_relu ix_acc mask_done tk
            at_S at_nb at_exp at_P at_T at_PT at_O at_oe at_c
            bdq_done sel_E sel_T sel_D xi_mm xi_relu xi_sc sw_done mbs_done
            ss_S ss_nb ss_exp ss_P ss_T ss_PT ss_oe ss_c uv_mm uv_ev
            wo_mm h_done mkv_mm mkv_ev mkT_tp mkT_ev qx_mm qx_ev bdx_done ox_mm hx_done out_st""".split()
        S = {n: sem(n) for n in names}
        ik_in = [sem(f"ik_in{i}") for i in range(4)]
        kp_in = [sem(f"kp_in{i}") for i in range(2)]
        vp_in = [sem(f"vp_in{i}") for i in range(2)]

        SELF = [("mla", t, i) for i in range(8) for t in range(4)] + \
               [("dsa", t, i) for t in range(4) for i in range(8)]
        CROSS = [("mem", t, i) for t in range(4) for i in range(4)] + [("smp", 4, g) for g in range(2)]

        def keys_of(u):
            kind, t, i = u
            return P * (t + 1) if kind in ("mla", "dsa") else 256

        def scale_of(u):
            return MLA_SCALE if u[0] == "mla" else DSA_SCALE

        n_self, n_cross = len(SELF), len(CROSS)
        UNITS = SELF + CROSS
        NORM = {"mix": (0, 5, 0), "mem": (5, 2, 2 * KD), "xmem": (7, 5, KD)}
        STREAM_UNITS = 12

        def src_of(stage, t):
            return memr[:, t, :] if stage == "mem" else h[0:rows(t), t, :]

        def nrows(stage, t):
            return P if stage == "mem" else rows(t)

        def dst_of(stage, t):
            return mT[:, :, t * P:(t + 1) * P] if stage == "mem" else xT[:, :, toks(t)]

        block = ctx.enter_context(nc.Block())

        @block.sync
        def _(sp):
            sp.dma_start(cst[:], T["cst"]).then_inc(S["cst_in"], 16)
            for t in range(4):
                sp.dma_start(h[:, t, :], T["x_prompt"][0, t * P:(t + 1) * P, :]).then_inc(S["x_in"], 16)
            sp.dma_start(h[0:NS, 4, :], T["x_sample"].rearrange("b t d -> (b t) d")).then_inc(S["x_in"], 16)
            sp.dma_start(gcol[:], T["gcol"]).then_inc(S["gk_in"], 16)
            sp.dma_start(gkv[:], T["mla_kv_norm"].broadcast_to([P, P])).then_inc(S["gk_in"], 16)
            for k in range(KD):
                sp.dma_start(win[:, k, :], T["w_in"][:, k, :]).then_inc(S["win_in"], 16)
            sp.dma_start(pts[:], T["page_table"]).then_inc(S["pt_in"], 16)
            for dst, name in ((w_uqn, "w_uqn"), (w_uqr, "w_uqr"), (w_ukT, "w_ukT"), (w_uv, "w_uv")):
                sp.dma_start(dst, T[name]).then_inc(S["wsm_in"], 16)
            for t in range(NBLK):
                R = rows(t)
                sp.wait_ge(S["ckv_done"], t + 1)
                sp.wait_ge(S["rp_dve"], t + 1)
                sp.wait_ge(S["rp_pool"], t + 1)
                for name, c, n in (("ckv", CKV, 128), ("kr", KR, 32), ("kv", DK, 256), ("idx", IK, 64)):
                    dst = T[f"new_{name}_p"][toks(t), :] if t < 4 else T[f"new_{name}_s"]
                    sp.dma_start(dst, proj[0:R, t, c:c + n]).then_inc(S["out_st"], 16)

            sp.wait_ge(S["pt_in"], 16)

            def page(b, j):
                return sp.value_load(pts[0:1, b * NPAGE + j:b * NPAGE + j + 1], min_val=0,
                                     max_val=T["n_pool"] - 1)

            sp.wait_ge(S["out_st"], 16 * 4 * NBLK)
            sp.wait_ge(S["at_oe"], n_self)
            for u in range(4 * NB):
                b, kc = 2 * (u // 8) + u % 2, (u % 8) // 2
                if u >= 4:
                    sp.wait_ge(S["xi_mm"], 5 * ((u - 4) // 8) + (u - 4) % 8 // 2 + 1)
                for j in range(4):
                    sp.dma_start(ikp[:, u % 4, j * PAGE:(j + 1) * PAGE],
                                 T["ikT"][bass.ds(page(b, 4 * kc + j), 1), :, :]
                                 .rearrange("a d k -> (a d) k")).then_inc(ik_in[u % 4], 16)
            for p in range(NB // 2):
                for which in ("K", "V"):
                    if which == "K":
                        if p >= 1:
                            sp.wait_ge(S["ss_S"], 2 * p)
                    elif p >= 1:
                        sp.wait_ge(S["ss_c"], 5 * 2 * p)
                    else:
                        sp.wait_ge(S["mbs_done"], 1)
                    for b2 in range(2):
                        for j in range(NPAGE):
                            pg = page(2 * p + b2, j)
                            if which == "K":
                                sp.dma_start(Kp[:, b2, j, :], T["poolK"][bass.ds(pg, 1), :, :]
                                             .rearrange("a q c -> (a q) c")).then_inc(kp_in[p % 2], 16)
                                sp.dma_start(krTp[:, b2, j * PAGE:(j + 1) * PAGE],
                                             T["krT"][bass.ds(pg, 1), :, :]
                                             .rearrange("a q c -> (a q) c")).then_inc(kp_in[p % 2], 16)
                            else:
                                sp.dma_start(Vp[:, b2, j, :], T["poolV"][bass.ds(pg, 1), :, :]
                                             .rearrange("a q c -> (a q) c")).then_inc(vp_in[p % 2], 16)
            sp.wait_ge(S["ss_S"], NB)
            sp.dma_start(w_o, T["w_o"]).then_inc(S["wo_in"], 16)
            sp.wait_ge(S["ss_c"], 5 * NB)
            sp.dma_start(memr, T["mem_prompt"][0].rearrange("(a p) d -> p a d", p=P)).then_inc(S["mem_in"], 16)
            sp.dma_start(wkv, T["wkv_x"]).then_inc(S["wkv_in"], 16)
            sp.dma_start(wqx, T["wq_x"]).then_inc(S["wqx_in"], 16)
            sp.dma_start(xc, T["mem_cache"].rearrange("b p a c -> p b a c")).then_inc(S["xc_in"], 16)
            sp.wait_ge(S["uv_ev"], 8)
            sp.dma_start(wox, T["wo_x"]).then_inc(S["wox_in"], 16)
            for t in range(2):
                sp.wait_ge(S["mkv_ev"], t + 1)
                for i, name in enumerate(("new_mem_k_p", "new_mem_v_p")):
                    sp.dma_start(T[name][t * P:(t + 1) * P, :], mkv[:, t, 256 * i:256 * (i + 1)])\
                        .then_inc(S["out_st"], 16)
            sp.wait_ge(S["out_st"], 16 * (4 * NBLK + 4))

        @block.gpsimd
        def _(pool):
            pool.memset(st[:, 156:158], -0.5).then_inc(S["half_ready"], 1)
            pool.memset(bdq[:], 0.0).then_inc(S["c16"], 1)

            def norm_rstd(stage):
                base, n, _ = NORM[stage]
                for t in range(n):
                    u, R = base + t, nrows(stage, t)
                    pool.wait_ge(S["sq_done"], u + 1)
                    nc.gpsimd.tensor_scalar(st[0:R, 40 + u:41 + u], st[0:R, u:u + 1], 1.0 / D, EPS,
                                            ALU.mult, ALU.add).then_inc(S["ms_done"], 1)
                    pool.wait_ge(S["ms_done"], u + 1)
                    nc.gpsimd.tensor_tensor(st[0:R, 80 + u:81 + u], st[0:R, 40 + u:41 + u],
                                            st[0:R, 156:157], ALU.pow).then_inc(S["rstd_done"], 1)

            pool.wait_ge(S["half_ready"], 1)
            norm_rstd("mix")
            pool.wait_ge(S["cst_in"], 16)
            for t in range(NBLK):
                R = rows(t)
                pool.wait_ge(S["sq2_done"], t + 1)
                for j, n in ((0, 256), (1, 128)):
                    c = 120 + 2 * t + j
                    nc.gpsimd.tensor_scalar(st[0:R, c:c + 1], st[0:R, c:c + 1], 1.0 / n, EPS,
                                            ALU.mult, ALU.add).then_inc(S["ms2_done"], 1)
                pool.wait_ge(S["ms2_done"], 2 * t + 2)
                nc.gpsimd.tensor_tensor(st[0:R, 140 + 2 * t:142 + 2 * t], st[0:R, 120 + 2 * t:122 + 2 * t],
                                        st[0:R, 156:158], ALU.pow).then_inc(S["rstd2_done"], 1)
                pool.wait_ge(S["rp_dve"], t + 1)
                if t >= 1:
                    pool.wait_ge(S["tA_mm"], 2 * t - 1)
                nc.gpsimd.tensor_copy(kk[0:R, 0:128].rearrange("p (a c) -> p a c", a=4),
                                      proj[0:R, t, KR:KR + 32].unsqueeze(1).broadcast_to([R, 4, 32]))\
                    .then_inc(S["ioA"], 1)
                nc.gpsimd.tensor_copy(kk[0:R, 128:256].rearrange("p (a c) -> p a c", a=2),
                                      proj[0:R, t, IK:IK + 64].unsqueeze(1).broadcast_to([R, 2, 64]))\
                    .then_inc(S["rp_pool"], 1)
            norm_rstd("mem")
            norm_rstd("xmem")

        @block.scalar
        def _(act):
            def norm_scale(stage):
                base, n, _ = NORM[stage]

                def square(t):
                    u, R = base + t, nrows(stage, t)
                    if stage == "mix":
                        act.wait_ge(S["x_in"], 16 * NBLK)
                    elif stage == "mem":
                        act.wait_ge(S["mem_in"], 16)
                    else:
                        act.wait_ge(S["h_done"], 2 * (t + 1))
                    if u >= 2:
                        act.wait_ge(S["tp_done"], 2 * (u - 1))
                    nc.scalar.activation(xs[0:R, u % 2, :], src_of(stage, t), ACT.Square,
                                         accum_out=st[0:R, u:u + 1]).then_inc(S["sq_done"], 1)

                square(0)
                for t in range(n):
                    u, R = base + t, nrows(stage, t)
                    if t + 1 < n:
                        square(t + 1)
                    act.wait_ge(S["rstd_done"], u + 1)
                    nc.scalar.activation(xs[0:R, u % 2, :], src_of(stage, t), ACT.Copy,
                                         scale=st[0:R, 80 + u:81 + u]).then_inc(S["xs_done"], 1)

            norm_scale("mix")
            for t in range(NBLK):
                R = rows(t)
                for c in range(2):
                    act.wait_ge(S["pj_mm"], 4 * t + c + 1)
                    nc.scalar.activation(proj[0:R, t, c * PC:(c + 1) * PC], bank(2 + c, PC, p1=R), ACT.Copy)\
                        .then_inc(S["pj_act"], 1)
                act.wait_ge(S["pj_act"], 2 * t + 1)
                act.wait_ge(S["tp_done"], 10)
                if t >= 1:
                    act.wait_ge(S["cq_done"], t)
                nc.scalar.activation(xs[0:R, 0, 0:256], proj[0:R, t, CQ:CQ + 256], ACT.Square,
                                     accum_out=st[0:R, 120 + 2 * t:121 + 2 * t])
                nc.scalar.activation(xs[0:R, 0, 256:384], proj[0:R, t, CKV:CKV + 128], ACT.Square,
                                     accum_out=st[0:R, 121 + 2 * t:122 + 2 * t]).then_inc(S["sq2_done"], 1)
                act.wait_ge(S["rstd2_done"], t + 1)
                nc.scalar.activation(proj[0:R, t, CQ:CQ + 256], proj[0:R, t, CQ:CQ + 256], ACT.Copy,
                                     scale=st[0:R, 140 + 2 * t:141 + 2 * t]).then_inc(S["cq_done"], 1)
                act.wait_ge(S["tA_mm"], 2 * t + 1)
                nc.scalar.activation(kT[:, :, toks(t)],
                                     bank(6, 4 * R).rearrange("p (a r) -> p a r", a=4), ACT.Copy)\
                    .then_inc(S["tA_ev"], 1)
                act.wait_ge(S["tA_mm"], 2 * t + 2)
                nc.scalar.activation(dqT[:, :, toks(t)],
                                     bank(6, 4 * R).rearrange("p (a r) -> p a r", a=4), ACT.Copy)\
                    .then_inc(S["tA_ev"], 1)
            act.wait_ge(S["pj_mm"], 4 * NBLK)
            for p in range(4):
                act.wait_ge(S["up_mm"], p + 1)
                nc.scalar.activation(qnT[:, p, :], bank(2 * (p % 2), NTOK), ACT.Copy).then_inc(S["up_ev"], 1)
            for t in range(4):
                act.wait_ge(S["vm_mm"], t + 1)
                nc.scalar.activation(Vm[:, t, :], bank(6 + t % 2), ACT.Copy).then_inc(S["vm_ev"], 1)
            for i in range(24):
                L = P * (i // 8 + 2)
                act.wait_ge(S["ix_mm"], i + 1)
                if i >= 2:
                    act.wait_ge(S["ix_acc"], i - 1)
                nc.scalar.activation(relu[:, i % 2, 0:L], bank(4 + i % 2, L), ACT.Relu)\
                    .then_inc(S["ix_relu"], 1)

            def softmax_exp(i, u):
                R_, L = P, keys_of(u)
                act.wait_ge(S["at_nb"], i + 1)
                if i >= 3:
                    act.wait_ge(S["at_T"], i - 2)
                nc.scalar.activation(Pr[:, i % 3, 0:L], bank(i % 2, L), ACT.Exp, bias=sm[:, 100 + i:101 + i],
                                     scale=scale_of(u), accum_out=sm[:, 200 + i:201 + i])\
                    .then_inc(S["at_exp"], 1)

            def probs_out(i, u):
                L = keys_of(u)
                act.wait_ge(S["at_T"], i + 1)
                if i >= 2:
                    act.wait_ge(S["at_O"], i - 1)
                nc.scalar.activation(PT[:, i % 2, 0:L], bank(2 + i % 2, L), ACT.Copy).then_inc(S["at_PT"], 1)

            def attention(lo, hi):
                for s in range(lo, hi + 2):
                    if s < hi:
                        softmax_exp(s, UNITS[s])
                    if s - 2 >= lo:
                        probs_out(s - 2, UNITS[s - 2])

            attention(0, n_self)
            for i in range(4 * 5):
                n = 512 if i % 5 < 4 else NS
                act.wait_ge(S["xi_mm"], i + 1)
                if i >= 2:
                    act.wait_ge(S["xi_sc"], i - 1)
                nc.scalar.activation(relus[:, i % 2, 0:n], bank(5 + i % 2, n), ACT.Relu)\
                    .then_inc(S["xi_relu"], 1)
            for i in range(NB):
                p, kind = divmod(i, 2)
                act.wait_ge(S["ss_nb"], i + 1)
                if i >= 2:
                    act.wait_ge(S["ss_T"], 5 * (i - 1))
                nc.scalar.activation(Ps[:, i % 2, :], PS[:, 0:NEWC], ACT.Exp, bias=ssm[:, 1, i:i + 1],
                                     scale=(MLA_SCALE, DSA_SCALE)[kind], accum_out=ssm[:, 2, i:i + 1])\
                    .then_inc(S["ss_exp"], 1)
                for c in range(5):
                    n = 512 if c < 4 else 128
                    k = 5 * i + c
                    act.wait_ge(S["ss_T"], k + 1)
                    if k >= 2:
                        act.wait_ge(S["ss_c"], k - 1)
                    pr = P if c < 4 else NS
                    nc.scalar.activation(PTs[0:pr, k % 2, 0:n], bank(5 + k % 2, n, p1=pr), ACT.Copy)\
                        .then_inc(S["ss_PT"], 1)
            norm_scale("mem")
            norm_scale("xmem")
            act.wait_ge(S["mkT_tp"], 1)
            nc.scalar.activation(mkT, bank(6).rearrange("p (a r) -> p a r", a=2), ACT.Copy)\
                .then_inc(S["mkT_ev"], 1)
            for c in range(2):
                act.wait_ge(S["qx_mm"], c + 1)
                nc.scalar.activation(qxT[:, c, :], bank(2 + 2 * c, NTOK), ACT.Copy).then_inc(S["qx_ev"], 1)
            attention(n_self, n_self + n_cross)

        @block.vector
        def _(dve):
            V = nc.vector
            dve.wait_ge(S["cst_in"], 16)
            V.tensor_copy(id16[:], ident).then_inc(S["c16"], 1)
            V.tensor_copy(causal16[:], causal).then_inc(S["c16"], 1)
            V.tensor_copy(same16[:].rearrange("p b c -> p (b c)"), same).then_inc(S["c16"], 1)

            def norm_gain(stage):
                base, n, g = NORM[stage]
                for t in range(n):
                    u, R = base + t, nrows(stage, t)
                    for half in range(2):
                        dve.wait_ge(S["tp_done"], 2 * u + half + 1)
                        gain = gcol[:, g + 4 * half:g + 4 * half + 4].unsqueeze(2).broadcast_to([P, 4, R])
                        V.tensor_tensor(dst_of(stage, t)[:, 4 * half:4 * half + 4, :],
                                        bank(half, 4 * R).rearrange("p (a r) -> p a r", a=4), gain, ALU.mult)\
                            .then_inc(S["xT_done"], 1)

            dve.wait_ge(S["gk_in"], 32)
            norm_gain("mix")
            chain = [0]

            def rope(eng_sem, R, t, x, out, nh, half):
                n = nh * 2 * half
                step = 32 // half
                cc = cosT[0:R, t, :].rearrange("p (a c) -> p a c", a=2)[:, :, 0:32:step]
                ss = sinT[0:R, t, :].rearrange("p (a c) -> p a c", a=2)[:, :, 0:32:step]
                x4 = x.rearrange("p (h a c) -> p h a c", h=nh, a=2)
                A = ropeA[0:R, 0:n].rearrange("p (h a c) -> p h a c", h=nh, a=2)
                M = ropeM[0:R, 0:n].rearrange("p (h a c) -> p h a c", h=nh, a=2)
                for a in range(2):
                    V.tensor_tensor(A[:, :, a, :], x4[:, :, a, :],
                                    cc[:, a, :].unsqueeze(1).broadcast_to([R, nh, half]), ALU.mult)\
                        .then_inc(S[eng_sem], 1)
                    V.tensor_tensor(M[:, :, a, :], x4[:, :, 1 - a, :],
                                    ss[:, a, :].unsqueeze(1).broadcast_to([R, nh, half]), ALU.mult)\
                        .then_inc(S[eng_sem], 1)
                chain[0] += 4
                dve.wait_ge(S[eng_sem], chain[0])
                return V.tensor_tensor(out, ropeA[0:R, 0:n], ropeM[0:R, 0:n], ALU.add)

            for t in range(NBLK):
                R = rows(t)
                for c in (2, 3):
                    dve.wait_ge(S["pj_mm"], 4 * t + c + 1)
                    V.tensor_copy(proj[0:R, t, c * PC:(c + 1) * PC], bank(2 + c, PC, p1=R))\
                        .then_inc(S["pj_dve"], 1)
                dve.wait_ge(S["pj_dve"], 2 * t + 2)
                dve.wait_ge(S["pj_act"], 2 * t + 2)
                for x0, nh, half in ((DQ, 10, 32), (IQ, 8, 32), (IK, 1, 32), (KR, 1, 16)):
                    n = nh * 2 * half
                    last = rope("qr_chain", R, t, proj[0:R, t, x0:x0 + n], proj[0:R, t, x0:x0 + n], nh, half)
                    if x0 != KR:
                        last.then_inc(S["qr_chain"], 1)
                        chain[0] += 1
                        dve.wait_ge(S["qr_chain"], chain[0])
                    else:
                        last.then_inc(S["rp_dve"], 1)
                        dve.wait_ge(S["rp_dve"], t + 1)
                dve.wait_ge(S["rstd2_done"], t + 1)
                V.scalar_tensor_tensor(out=proj[0:R, t, CKV:CKV + 128], in0=proj[0:R, t, CKV:CKV + 128],
                                       scalar=st[0:R, 141 + 2 * t:142 + 2 * t], in1=gkv[0:R, :],
                                       op0=ALU.mult, op1=ALU.mult).then_inc(S["ckv_done"], 1)
                dve.wait_ge(S["tB_mm"], 2 * t + 1)
                gain = gcol[:, 4 * KD:4 * KD + 2].unsqueeze(2).broadcast_to([P, 2, R])
                V.tensor_tensor(cqT[:, :, toks(t)], bank(7, 2 * R).rearrange("p (a r) -> p a r", a=2), gain,
                                ALU.mult).then_inc(S["tB_ev"], 1)
                dve.wait_ge(S["tB_mm"], 2 * t + 2)
                if t < 4:
                    V.tensor_copy(iqT[:, :, toks(t)], bank(7).rearrange("p (a r) -> p a r", a=4))\
                        .then_inc(S["tB_ev"], 1)
                else:
                    V.tensor_copy(iqTs.rearrange("p b h t -> p h b t"),
                                  bank(7, p1=64).rearrange("p (h b t) -> p h b t", h=8, b=NB))\
                        .then_inc(S["tB_ev"], 1)
            dve.wait_ge(S["tA_ev"], 2 * NBLK)
            dve.wait_ge(S["c16"], 4)
            for g in range(2):
                V.tensor_copy(bdq[64 * g:64 * g + 64, :, g, :, :].rearrange("p b n t -> p n b t"),
                              dqT[64 * g:64 * g + 64, :, SEQ:NTOK].rearrange("p n (b t) -> p n b t", b=NB))\
                    .then_inc(S["bdq_done"], 1)
            for hd in range(8):
                dve.wait_ge(S["ql_mm"], hd + 1)
                o = 2 * (hd % 2) * BANK
                V.tensor_copy(qlT[:, hd, :], PS[:, o:o + SEQ]).then_inc(S["ql_ev"], 1)
                V.tensor_copy(qlTs[:, :, hd, :],
                              PS[:, o + SEQ:o + NTOK].rearrange("p (b t) -> p b t", b=NB))\
                    .then_inc(S["ql_ev"], 1)
            for t in range(NBLK):
                R = rows(t)
                dve.wait_ge(S["qr_mm"], t + 1)
                if t >= 1:
                    dve.wait_ge(S["qr_tp"], t)
                rope("qr_chain", R, t, bank(4 + t % 2, 256, p1=R), qr[0:R, :], 8, 16)\
                    .then_inc(S["qr_done"], 1)
                dve.wait_ge(S["qr_done"], t + 1)
                dve.wait_ge(S["qr_tp"], t + 1)
                if t < 4:
                    V.tensor_copy(qrT[:, :, toks(t)], bank(7, 2 * R).rearrange("p (a r) -> p a r", a=2))\
                        .then_inc(S["qr_ev"], 1)
                else:
                    V.tensor_copy(qrTs[:].rearrange("p b (h t) -> p h b t", h=8),
                                  bank(7, p1=32).rearrange("p (h b t) -> p h b t", h=8, b=NB))\
                        .then_inc(S["qr_ev"], 1)
            last_mask = 0
            V.tensor_copy(mb16[:, 0, 0:P], causal).then_inc(S["mask_done"], 1)
            for i in range(24):
                t, hd = i // 8 + 1, i % 8
                L = P * (t + 1)
                acc = accs[:, t - 1, 0:L]
                iw = proj[:, t, IW + hd:IW + hd + 1]
                dve.wait_ge(S["ix_relu"], i + 1)
                if hd == 0:
                    V.tensor_scalar(acc, relu[:, i % 2, 0:L], iw, None, ALU.mult).then_inc(S["ix_acc"], 1)
                else:
                    dve.wait_ge(S["ix_acc"], i)
                    V.scalar_tensor_tensor(out=acc, in0=relu[:, i % 2, 0:L], scalar=iw, in1=acc,
                                           op0=ALU.mult, op1=ALU.add).then_inc(S["ix_acc"], 1)

            taken = [0]

            def top_k(x, m, k):
                base = taken[0]
                with dve.Fori(0, k // 8) as r:
                    V.max(m, x).then_inc(S["tk"], 1)
                    dve.wait_ge(S["tk"], base + 2 * r + 1)
                    dve.nop(nofuse=True)
                    V.match_replace(x, m, x, TAKEN).then_inc(S["tk"], 1)
                    dve.wait_ge(S["tk"], base + 2 * r + 2)
                    dve.nop(nofuse=True)
                taken[0] += 2 * (k // 8)

            for t in range(1, 4):
                L = P * (t + 1)
                acc = accs[:, t - 1, 0:L]
                dve.wait_ge(S["ix_acc"], 8 * t)
                V.tensor_tensor(acc[:, L - P:L], acc[:, L - P:L], causal, ALU.add).then_inc(S["tk"], 1)
                taken[0] += 1
                dve.wait_ge(S["tk"], taken[0])
                top_k(acc, m8[:], K_PROMPT)
                V.tensor_scalar(mb16[:, t, 0:L], acc, -2e38, NEG, ALU.is_ge, ALU.mult)\
                    .then_inc(S["mask_done"], 1)

            def softmax_max(i, u):
                L = keys_of(u)
                dve.wait_ge(S["at_S"], i + 1)
                V.reduce_max(sm[:, i:i + 1], bank(i % 2, L), AX).then_inc(S["at_c"], 1)
                dve.wait_ge(S["at_c"], at_count())
                V.tensor_scalar(sm[:, 100 + i:101 + i], sm[:, i:i + 1], -scale_of(u), None, ALU.mult)\
                    .then_inc(S["at_nb"], 1)

            counts = {"c": 0}

            def at_count():
                counts["c"] += 1
                return counts["c"]

            def softmax_norm(i, u):
                L = keys_of(u)
                dve.wait_ge(S["at_exp"], i + 1)
                V.reciprocal(sm[:, 300 + i:301 + i], sm[:, 200 + i:201 + i]).then_inc(S["at_c"], 1)
                dve.wait_ge(S["at_c"], at_count())
                V.tensor_scalar(Pr[:, i % 3, 0:L], Pr[:, i % 3, 0:L], sm[:, 300 + i:301 + i], None, ALU.mult)\
                    .then_inc(S["at_P"], 1)

            def heads_out(i, u):
                kind, t, hd = u
                dve.wait_ge(S["at_O"], i + 1)
                if kind in ("mla", "dsa"):
                    j, c = (hd % 2, hd // 2) if kind == "mla" else (hd // 4, 4 + hd % 4)
                    V.tensor_copy(xT[64 * j:64 * j + 64, c, toks(t)], bank(4 + i % 2, P, p0=64 * j, p1=64 * j + 64))\
                        .then_inc(S["at_oe"], 1)
                elif kind == "mem":
                    j, c = hd % 2, hd // 2
                    V.tensor_copy(oxT[64 * j:64 * j + 64, c, toks(t)], bank(4 + i % 2, P, p0=64 * j, p1=64 * j + 64))\
                        .then_inc(S["at_oe"], 1)
                else:
                    for c in range(2):
                        for j in range(2):
                            o = PS[64 * j:64 * j + 64, (4 + i % 2) * BANK + c * P:(4 + i % 2) * BANK + (c + 1) * P]
                            o = o.rearrange("p (b n t) -> p b n t", b=4, n=4)[:, :, 2 * c + j, :]
                            d = oxT[64 * j:64 * j + 64, c, SEQ + 32 * hd:SEQ + 32 * hd + 32]
                            last = V.tensor_copy(d.rearrange("p (b t) -> p b t", b=4), o)
                    last.then_inc(S["at_oe"], 1)

            def attention(lo, hi):
                for s in range(lo, hi + 3):
                    if s < hi:
                        softmax_max(s, UNITS[s])
                    if lo <= s - 1 < hi:
                        softmax_norm(s - 1, UNITS[s - 1])
                    if s - 3 >= lo:
                        heads_out(s - 3, UNITS[s - 3])

            dve.wait_ge(S["tA_ev"], 2 * NBLK)
            attention(0, n_self)

            dve.wait_ge(S["c16"], 4)
            V.tensor_tensor(selE, same.rearrange("p (b h t) -> p b h t", b=NB, h=8),
                            proj[0:NS, 4, IW:IW + 8].unsqueeze(1).unsqueeze(3).broadcast_to([NS, NB, 8, NQ]),
                            ALU.mult).then_inc(S["sel_E"], 1)
            dve.wait_ge(S["sel_T"], 1)
            V.tensor_copy(Dp[:], bank(7, 256).rearrange("p (a c) -> p a c", a=4)).then_inc(S["sel_D"], 1)
            dve.wait_ge(S["xi_sc"], 20)
            V.tensor_copy(sw[:, 0:PAST], PS[0:NS, 0:PAST]).then_inc(S["sw_done"], 1)
            V.tensor_tensor(sw[:, PAST:NEWC], PS[0:NS, PAST:NEWC], cst[0:NS, C_NEW:C_NEW + NS], ALU.add)\
                .then_inc(S["sw_done"], 1)
            dve.wait_ge(S["sw_done"], 2)
            top_k(sw, m8[0:NS, :], K_SAMPLE)
            dve.wait_ge(S["qr_ev"], NBLK)
            V.tensor_scalar(mbs, sw, -2e38, NEG, ALU.is_ge, ALU.mult).then_inc(S["mbs_done"], 1)

            def own_values(i, p):
                if i % 2 == 0:
                    V.tensor_copy(olT[:, 2 * p:2 * p + 2, :, :].rearrange("p b h t -> p (b h t)"), bank(7, P))\
                        .then_inc(S["ss_oe"], 1)
                else:
                    for g in range(2):
                        for b2 in range(2):
                            o = bank(7, 64, 64 * b2, p0=64 * g, p1=64 * g + 64)
                            o = o.rearrange("p (g n t) -> p g n t", g=2, n=4)[:, g, :, :]
                            c0 = SEQ + NQ * (2 * p + b2)
                            last = V.tensor_copy(xT[64 * g:64 * g + 64, 4:8, c0:c0 + NQ], o)
                    last.then_inc(S["ss_oe"], 1)

            sc = [0]
            for i in range(NB):
                p, kind = divmod(i, 2)
                dve.wait_ge(S["ss_S"], i + 1)
                V.reduce_max(ssm[:, 0, i:i + 1], PS[:, 0:NEWC], AX).then_inc(S["ss_P"], 1)
                dve.wait_ge(S["ss_P"], 3 * i + 1)
                V.tensor_scalar(ssm[:, 1, i:i + 1], ssm[:, 0, i:i + 1], -(MLA_SCALE, DSA_SCALE)[kind],
                                None, ALU.mult).then_inc(S["ss_nb"], 1)
                if i >= 1:
                    dve.wait_ge(S["ss_c"], 5 * i)
                    own_values(i - 1, (i - 1) // 2)
                dve.wait_ge(S["ss_exp"], i + 1)
                V.reciprocal(ssm[:, 3, i:i + 1], ssm[:, 2, i:i + 1])\
                    .then_inc(S["ss_P"], 1)
                dve.wait_ge(S["ss_P"], 3 * i + 2)
                V.tensor_scalar(Ps[:, i % 2, :], Ps[:, i % 2, :], ssm[:, 3, i:i + 1], None, ALU.mult)\
                    .then_inc(S["ss_P"], 1)
            dve.wait_ge(S["ss_c"], 5 * NB)
            own_values(NB - 1, NB // 2 - 1)
            for hd in range(8):
                j, c = hd % 2, hd // 2
                dve.wait_ge(S["uv_mm"], 1)
                V.tensor_copy(xT[64 * j:64 * j + 64, c, SEQ:NTOK], bank(5 + j, NS, NS * c, p0=64 * j, p1=64 * j + 64))\
                    .then_inc(S["uv_ev"], 1)
            for i in range(2 * NBLK):
                t, half = divmod(i, 2)
                R = rows(t)
                dve.wait_ge(S["wo_mm"], i + 1)
                hs = h[0:R, t, 512 * half:512 * half + 512]
                V.tensor_tensor(hs, bank(2 + i % 2, p1=R), hs, ALU.add).then_inc(S["h_done"], 1)
            norm_gain("mem")
            for t in range(2):
                dve.wait_ge(S["mkv_mm"], t + 1)
                V.tensor_copy(mkv[:, t, :], bank(4 + t)).then_inc(S["mkv_ev"], 1)
            norm_gain("xmem")
            V.memset(bdx, 0.0).then_inc(S["bdx_done"], 1)
            dve.wait_ge(S["bdx_done"], 1)
            dve.wait_ge(S["qx_ev"], 2)
            for c in range(2):
                for j in range(2):
                    V.tensor_copy(bdx[64 * j:64 * j + 64, c, :, 2 * c + j, :],
                                  qxT[64 * j:64 * j + 64, c, SEQ:NTOK].rearrange("p (b t) -> p b t", b=NB))\
                        .then_inc(S["bdx_done"], 1)
            attention(n_self, n_self + n_cross)
            for i in range(2 * NBLK):
                t, half = divmod(i, 2)
                R = rows(t)
                dve.wait_ge(S["ox_mm"], i + 1)
                hs = h[0:R, t, 512 * half:512 * half + 512]
                V.tensor_tensor(hs, bank(i % 2, p1=R), hs, ALU.add).then_inc(S["hx_done"], 1)
            dve.wait_ge(S["hx_done"], 2 * NBLK)

        @block.tensor
        def _(pe):
            M = nc.tensor.matmul
            TR = nc.tensor.transpose

            def norm_transpose(stage):
                base, n, _ = NORM[stage]
                for t in range(n):
                    u, R = base + t, nrows(stage, t)
                    pe.wait_ge(S["xs_done"], u + 1)
                    for half in range(2):
                        if u >= 1:
                            pe.wait_ge(S["xT_done"], 2 * (u - 1) + half + 1)
                        for a in range(4):
                            c = 4 * half + a
                            last = TR(bank(half, R, a * R), xs[0:R, u % 2, c * P:(c + 1) * P], ident[0:R, 0:R])
                        last.then_inc(S["tp_done"], 1)

            pe.wait_ge(S["cst_in"], 16)
            norm_transpose("mix")
            pe.wait_ge(S["win_in"], 16 * KD)

            def project(t):
                R = rows(t)
                pe.wait_ge(S["xT_done"], 2 * (t + 1))
                for c in range(4):
                    if t >= 1:
                        pe.wait_ge(S["pj_act"] if c < 2 else S["pj_dve"], 2 * (t - 1) + c % 2 + 1)
                    for k in range(KD):
                        last = M(bank(2 + c, PC, p1=R), xT[:, k, toks(t)], win[:, k, c * PC:(c + 1) * PC],
                                 start=(k == 0), stop=(k == KD - 1))
                    last.then_inc(S["pj_mm"], 1)

            def transposes(t):
                R = rows(t)
                I = ident[0:R, 0:R]
                pe.wait_ge(S["ckv_done"], t + 1)
                pe.wait_ge(S["rp_pool"], t + 1)
                pe.wait_ge(S["ioA"], t + 1)
                if t >= 1:
                    pe.wait_ge(S["tA_ev"], 2 * t)
                for a, src in enumerate((proj[0:R, t, CKV:CKV + P], kk[0:R, 0:128],
                                         proj[0:R, t, DK:DK + P], kk[0:R, 128:256])):
                    last = TR(bank(6, R, a * R), src, I)
                last.then_inc(S["tA_mm"], 1)
                pe.wait_ge(S["cq_done"], t + 1)
                if t >= 1:
                    pe.wait_ge(S["tB_ev"], 2 * t)
                for a in range(2):
                    last = TR(bank(7, R, a * R), proj[0:R, t, CQ + a * P:CQ + (a + 1) * P], I)
                last.then_inc(S["tB_mm"], 1)
                pe.wait_ge(S["tA_ev"], 2 * t + 1)
                for a in range(4):
                    last = TR(bank(6, R, a * R), proj[0:R, t, DQ + a * P:DQ + (a + 1) * P], I)
                last.then_inc(S["tA_mm"], 1)
                pe.wait_ge(S["tB_ev"], 2 * t + 1)
                if t < 4:
                    for a in range(4):
                        last = TR(bank(7, R, a * R), proj[0:R, t, IQ + a * P:IQ + (a + 1) * P], I)
                else:
                    for a in range(8):
                        last = TR(bank(7, R, a * R, p1=64), proj[0:R, t, IQ + a * 64:IQ + (a + 1) * 64], I)
                last.then_inc(S["tB_mm"], 1)

            for t in range(NBLK + 1):
                if t < NBLK:
                    project(t)
                if t >= 1:
                    transposes(t - 1)
            pe.wait_ge(S["wsm_in"], 64)
            pe.wait_ge(S["tB_ev"], 2 * NBLK)
            pe.wait_ge(S["pj_act"], 2 * NBLK)
            pe.wait_ge(S["pj_dve"], 2 * NBLK)
            for p in range(4):
                if p >= 2:
                    pe.wait_ge(S["up_ev"], p - 1)
                for lo, hi in ((0, SEQ), (SEQ, NTOK)):
                    for c in range(2):
                        o = 2 * (p % 2) * BANK
                        last = M(PS[:, o + lo:o + hi], w_uqn[:, c, p * P:(p + 1) * P], cqT[:, c, lo:hi],
                                 start=(c == 0), stop=(c == 1))
                last.then_inc(S["up_mm"], 1)
            for hd in range(8):
                j, p = hd % 2, hd // 2
                pe.wait_ge(S["up_ev"], 4)
                if hd >= 2:
                    pe.wait_ge(S["ql_ev"], 2 * (hd - 1))
                for lo, hi in ((0, SEQ), (SEQ, NTOK)):
                    o = 2 * (hd % 2) * BANK
                    last = M(PS[:, o + lo:o + hi], w_ukT[64 * j:64 * j + 64, p, :],
                             qnT[64 * j:64 * j + 64, p, lo:hi], start=True, stop=True)
                last.then_inc(S["ql_mm"], 1)
            for t in range(NBLK):
                R = rows(t)
                if t >= 2:
                    pe.wait_ge(S["qr_done"], t - 1)
                for c in range(2):
                    last = M(bank(4 + t % 2, 256, p1=R), cqT[:, c, toks(t)], w_uqr[:, c, :],
                             start=(c == 0), stop=(c == 1))
                last.then_inc(S["qr_mm"], 1)
                pe.wait_ge(S["qr_done"], t + 1)
                if t >= 1:
                    pe.wait_ge(S["qr_ev"], t)
                I = ident[0:R, 0:R]
                if t < 4:
                    for a in range(2):
                        last = TR(bank(7, R, a * R), qr[0:R, a * P:(a + 1) * P], I)
                else:
                    for a in range(8):
                        last = TR(bank(7, R, a * R, p1=32), qr[0:R, a * 32:(a + 1) * 32], I)
                last.then_inc(S["qr_tp"], 1)
            pe.wait_ge(S["qr_ev"], NBLK)
            pe.wait_ge(S["tA_ev"], 2 * NBLK)
            for t in range(4):
                if t >= 2:
                    pe.wait_ge(S["vm_ev"], t - 1)
                M(bank(6 + t % 2), kT[:, 0, toks(t)], w_uv, start=True, stop=True).then_inc(S["vm_mm"], 1)
            for i in range(24):
                t, hd = i // 8 + 1, i % 8
                L, j, p = P * (t + 1), hd % 2, hd // 2
                if i >= 2:
                    pe.wait_ge(S["ix_relu"], i - 1)
                M(bank(4 + i % 2, L), iqT[64 * j:64 * j + 64, p, toks(t)], kT[64 * j:64 * j + 64, 3, 0:L],
                  start=True, stop=True).then_inc(S["ix_mm"], 1)

            def scores(i, u):
                kind, t, hd = u
                L = keys_of(u)
                if i >= 2:
                    pe.wait_ge(S["at_exp"], i - 1)
                b = i % 2
                if kind == "mla":
                    r, c = hd % 4, hd // 4
                    M(bank(b, L), qlT[:, hd, toks(t)], kT[:, 0, 0:L], start=True, stop=False)
                    M(bank(b, L), qrT[32 * r:32 * r + 32, c, toks(t)], kT[32 * r:32 * r + 32, 1, 0:L],
                      start=False, stop=False)
                    last = M(bank(b, P, L - P), id16[:], causal16[:], start=False, stop=True)
                elif kind == "dsa":
                    g, n = hd // 4, hd % 4
                    pe.wait_ge(S["mask_done"], t + 1)
                    M(bank(b, L), dqT[64 * g:64 * g + 64, n, toks(t)], kT[64 * g:64 * g + 64, 2, 0:L],
                      start=True, stop=False)
                    last = M(bank(b, L), id16[:], mb16[:, t, 0:L], start=False, stop=True)
                elif kind == "mem":
                    j, c = hd % 2, hd // 2
                    last = M(bank(b, L), qxT[64 * j:64 * j + 64, c, toks(t)], mkT[64 * j:64 * j + 64, c, :],
                             start=True, stop=True)
                else:
                    for b4 in range(4):
                        bb = 4 * hd + b4
                        for c in range(2):
                            last = M(bank(b, L, p0=32 * b4, p1=32 * b4 + 32),
                                     bdx[:, c, bb, :, :].rearrange("p n t -> p (n t)"), xc[:, bb, c, :],
                                     start=(c == 0), stop=(c == 1))
                last.then_inc(S["at_S"], 1)

            def turn_probs(i, u):
                L = keys_of(u)
                pe.wait_ge(S["at_P"], i + 1)
                if i >= 2:
                    pe.wait_ge(S["at_PT"], i - 1)
                for a in range(L // P):
                    last = TR(bank(2 + i % 2, P, a * P), Pr[:, i % 3, a * P:(a + 1) * P], ident)
                last.then_inc(S["at_T"], 1)

            def values(i, u):
                kind, t, hd = u
                L = keys_of(u)
                nk = L // P
                pe.wait_ge(S["at_PT"], i + 1)
                if i >= 2:
                    pe.wait_ge(S["at_oe"], i - 1)
                if kind == "smp":
                    for b4 in range(4):
                        bb = 4 * hd + b4
                        for c in range(2):
                            for k in range(2):
                                last = M(bank(4 + i % 2, 32, c * P + 32 * b4), xc[:, bb, 2 + k, c * P:(c + 1) * P],
                                         PT[:, i % 2, k * P + 32 * b4:k * P + 32 * b4 + 32],
                                         start=(k == 0), stop=(k == 1))
                    last.then_inc(S["at_O"], 1)
                    return
                j = hd // 4 if kind == "dsa" else hd % 2
                for k in range(nk):
                    if kind == "mla":
                        v = Vm[:, k, hd * 64:hd * 64 + 64]
                    elif kind == "dsa":
                        v = proj[:, k, DV + 64 * j:DV + 64 * j + 64]
                    else:
                        v = mkv[:, k, 256 + 64 * hd:256 + 64 * hd + 64]
                    last = M(bank(4 + i % 2, P, p0=64 * j, p1=64 * j + 64), v, PT[:, i % 2, k * P:(k + 1) * P],
                             start=(k == 0), stop=(k == nk - 1))
                last.then_inc(S["at_O"], 1)

            def attention(lo, hi):
                for s in range(lo, hi + 3):
                    if s < hi:
                        scores(s, UNITS[s])
                    if lo <= s - 2 < hi:
                        turn_probs(s - 2, UNITS[s - 2])
                    if s - 3 >= lo:
                        values(s - 3, UNITS[s - 3])

            pe.wait_ge(S["vm_ev"], 4)
            pe.wait_ge(S["c16"], 4)
            pe.wait_ge(S["ix_relu"], 24)
            pe.wait_ge(S["ql_ev"], 16)
            attention(0, n_self)

            pe.wait_ge(S["sel_E"], 1)
            for p in range(4):
                last = TR(bank(7, NS, p * NS), selE[:, 2 * p:2 * p + 2, :, :].rearrange("p b h t -> p (b h t)"),
                          ident[0:NS, 0:NS])
            last.then_inc(S["sel_T"], 1)
            pe.wait_ge(S["sel_D"], 1)
            pe.wait_ge(S["at_oe"], n_self)
            pe.wait_ge(S["at_PT"], n_self)

            def head_sum(i):
                p, kc = divmod(i, 5)
                n = 512 if kc < 4 else NS
                pe.wait_ge(S["xi_relu"], i + 1)
                M(bank(kc, n, p1=NS), Dp[:, p, :], relus[:, i % 2, 0:n], start=(p == 0), stop=(p == 3),
                  skip_group_check=True).then_inc(S["xi_sc"], 1)

            for i in range(20):
                p, kc = divmod(i, 5)
                n = 512 if kc < 4 else NS
                if i >= 2:
                    pe.wait_ge(S["xi_relu"], i - 1)
                for b2 in range(2):
                    q = iqTs[:, 2 * p + b2, :, :].rearrange("p h t -> p (h t)")
                    if kc < 4:
                        u = 8 * p + 2 * kc + b2
                        pe.wait_ge(ik_in[u % 4], 64 * (u // 4 + 1))
                        last = M(bank(5 + i % 2, n, p0=64 * b2, p1=64 * b2 + 64), q, ikp[:, u % 4, :],
                                 start=True, stop=True)
                    else:
                        last = M(bank(5 + i % 2, n, p0=64 * b2, p1=64 * b2 + 64), q, kT[0:64, 3, SEQ:NTOK],
                                 start=True, stop=True)
                last.then_inc(S["xi_mm"], 1)
                if i >= 1:
                    head_sum(i - 1)
            head_sum(19)

            def pair_scores(i):
                p, kind = divmod(i, 2)
                if kind == 0:
                    pe.wait_ge(kp_in[p % 2], 16 * 64 * (p // 2 + 1))
                if i >= 1:
                    pe.wait_ge(S["ss_exp"], i)
                else:
                    pe.wait_ge(S["sw_done"], 2)
                if kind == 1:
                    pe.wait_ge(S["mbs_done"], 1)
                for b2 in range(2):
                    b = 2 * p + b2
                    for kc in range(5):
                        n = 512 if kc < 4 else NS
                        out = bank(kc, n, p0=64 * b2, p1=64 * b2 + 64)
                        if kind == 0:
                            ql = qlTs[:, b, :, :].rearrange("p h t -> p (h t)")
                            for a in range(4 if kc < 4 else 1):
                                if kc < 4:
                                    o = bank(kc, PAGE, a * PAGE, p0=64 * b2, p1=64 * b2 + 64)
                                    k = Kp[:, b2, 4 * kc + a, 0:128]
                                else:
                                    o, k = out, kT[:, 0, SEQ:NTOK]
                                M(o, ql, k, start=(a == 0), stop=False, skip_group_check=True)
                            k = krTp[:, b2, kc * 512:kc * 512 + 512] if kc < 4 else kT[0:32, 1, SEQ:NTOK]
                            last = M(out, qrTs[:, b, :], k, start=False, stop=(kc < 4), skip_group_check=True)
                            if kc == 4:
                                last = M(out, same[:, 64 * b:64 * b + 64], cst[0:NS, C_NEW:C_NEW + NS],
                                         start=False, stop=True, skip_group_check=True)
                        else:
                            q = bdq[:, b, :, :, :].rearrange("p g n t -> p (g n t)")
                            for a in range(4 if kc < 4 else 1):
                                if kc < 4:
                                    o = bank(kc, PAGE, a * PAGE, p0=64 * b2, p1=64 * b2 + 64)
                                    k = Kp[:, b2, 4 * kc + a, 128:256]
                                else:
                                    o, k = out, kT[:, 2, SEQ:NTOK]
                                M(o, q, k, start=(a == 0), stop=False, skip_group_check=True)
                            last = M(out, same16[:, b, :], mbs[:, kc * 512:kc * 512 + n], start=False, stop=True,
                                     skip_group_check=True)
                last.then_inc(S["ss_S"], 1)

            def turn_pair(i, c):
                k = 5 * i + c
                pe.wait_ge(S["ss_P"], 3 * i + 3)
                if k >= 2:
                    pe.wait_ge(S["ss_PT"], k - 1)
                if c < 4:
                    for a in range(4):
                        c0 = 512 * c + a * P
                        last = TR(bank(5 + k % 2, P, a * P), Ps[:, i % 2, c0:c0 + P], ident)
                else:
                    last = TR(bank(5 + k % 2, P, 0, p1=NS), Ps[:, i % 2, PAST:NEWC], ident)
                last.then_inc(S["ss_T"], 1)

            def pair_values(i, c):
                p, kind = divmod(i, 2)
                k = 5 * i + c
                pe.wait_ge(S["ss_PT"], k + 1)
                if c == 0:
                    if kind == 0:
                        pe.wait_ge(vp_in[p % 2], 16 * 32 * (p // 2 + 1))
                    if i >= 1:
                        pe.wait_ge(S["ss_oe"], i)
                for b2 in range(2):
                    out = bank(7, 64, 64 * b2)
                    first = (c == 0)
                    if c < 4:
                        for a in range(4):
                            v = Vp[:, b2, 4 * c + a, 128 * kind:128 * kind + 128]
                            last = M(out, v, PTs[:, k % 2, a * P + 64 * b2:a * P + 64 * b2 + 64],
                                     start=(first and a == 0 and b2 == 0), stop=False, skip_group_check=True)
                    else:
                        v = proj[0:NS, 4, (CKV, DV)[kind]:(CKV, DV)[kind] + P]
                        last = M(out, v, PTs[0:NS, k % 2, 64 * b2:64 * b2 + 64], start=False, stop=(b2 == 1),
                                 skip_group_check=True)
                last.then_inc(S["ss_c"], 1)

            for i in range(NB + 1):
                if i < NB:
                    pair_scores(i)
                if i >= 1:
                    for c in range(6):
                        if c < 5:
                            turn_pair(i - 1, c)
                        if c >= 1:
                            pair_values(i - 1, c - 1)
            pe.wait_ge(S["ss_oe"], NB)
            for hd in range(8):
                j, c = hd % 2, hd // 2
                last = M(bank(5 + j, NS, NS * c, p0=64 * j, p1=64 * j + 64), w_uv[:, hd * 64:hd * 64 + 64],
                         olT[:, :, hd, :], start=True, stop=True, skip_group_check=True)
            last.then_inc(S["uv_mm"], 1)
            pe.wait_ge(S["uv_ev"], 8)
            pe.wait_ge(S["wo_in"], 16)
            for i in range(2 * NBLK):
                t, half = divmod(i, 2)
                R = rows(t)
                if i >= 2:
                    pe.wait_ge(S["h_done"], i - 1)
                for k in range(KD):
                    last = M(bank(2 + i % 2, p1=R), xT[:, k, toks(t)], w_o[:, k, 512 * half:512 * half + 512],
                             start=(k == 0), stop=(k == KD - 1))
                last.then_inc(S["wo_mm"], 1)
            norm_transpose("mem")
            pe.wait_ge(S["wkv_in"], 16)
            for t in range(2):
                pe.wait_ge(S["xT_done"], 2 * (NORM["mem"][0] + t + 1))
                for k in range(KD):
                    last = M(bank(4 + t), mT[:, k, t * P:(t + 1) * P], wkv[:, k, :], start=(k == 0),
                             stop=(k == KD - 1))
                last.then_inc(S["mkv_mm"], 1)
            norm_transpose("xmem")
            pe.wait_ge(S["mkv_ev"], 2)
            for c in range(2):
                for t in range(2):
                    last = TR(bank(6, P, c * 256 + t * P), mkv[:, t, c * P:(c + 1) * P], ident)
            last.then_inc(S["mkT_tp"], 1)
            pe.wait_ge(S["wqx_in"], 16)
            pe.wait_ge(S["xT_done"], 2 * STREAM_UNITS)
            for c in range(2):
                for lo, hi in ((0, SEQ), (SEQ, NTOK)):
                    for k in range(KD):
                        o = (2 + 2 * c) * BANK
                        last = M(PS[:, o + lo:o + hi], wqx[:, k, c * P:(c + 1) * P], xT[:, k, lo:hi],
                                 start=(k == 0), stop=(k == KD - 1))
                last.then_inc(S["qx_mm"], 1)
            pe.wait_ge(S["mkT_ev"], 1)
            pe.wait_ge(S["qx_ev"], 2)
            pe.wait_ge(S["bdx_done"], 5)
            pe.wait_ge(S["xc_in"], 16)
            attention(n_self, n_self + n_cross)
            pe.wait_ge(S["wox_in"], 16)
            pe.wait_ge(S["at_oe"], n_self + n_cross)
            for i in range(2 * NBLK):
                t, half = divmod(i, 2)
                R = rows(t)
                if i >= 2:
                    pe.wait_ge(S["hx_done"], i - 1)
                for c in range(2):
                    last = M(bank(i % 2, p1=R), oxT[:, c, toks(t)], wox[:, c, 512 * half:512 * half + 512],
                             start=(c == 0), stop=(c == 1))
                last.then_inc(S["ox_mm"], 1)


def peer_select(nc, T, h, sems, xh, xl, IT, JT, ch, cl):
    ctx = ExitStack()
    with ctx:
        def sb(name, shape, dt=F32):
            return ctx.enter_context(nc.sbuf_tensor(name, shape, dt))

        PS = ctx.enter_context(nc.psum_tensor("psB", [P, 8 * BANK], F32))

        def bank(b, n=BANK, at=0, p0=0, p1=P):
            return PS[p0:p1, b * BANK + at:b * BANK + at + n]

        cst = sb("cstB", [P, 256])
        gcol = sb("gcolB", [P, KD])
        st = sb("stB", [P, 20])
        xs = sb("xsB", [P, 2, D])
        xf = sb("xfB", [P, 2, 4, P])
        keysT = sb("keysT", [P, 2 * PH, NKEY])
        wraw = sb("wraw", [P, 2, D])
        wh = sb("wh", [P, 2, D], F32R)
        wl = sb("wl", [P, 2, D], F32R)
        qT = sb("qT", [P, 2, NTOK])
        sc = sb("sc", [P, NBLK, 2 * PH, NKEY])
        mv = sb("mv", [P, 2 * PH, PK])
        mi = sb("mi", [P, 2 * PH, PK], U32)
        mf = sb("mf", [P, 2 * PH, PK])
        cand = sb("cand", [P, PH, PK, PK])
        gv = sb("gv", [P, PH, PK])
        gi = sb("gi", [P, PH, PK], U32)
        ga = sb("gaB", [P, 2, PH * PK], U32)
        gf = sb("gfB", [P, 2, PH * PK])
        hit = sb("hit", [P, PH, PK, PK])
        sel = sb("selB", [P, 3, PH * PK])
        gs = sb("gsB", [P, 2, PH])
        ident = cst[:, 0:P]
        iota16 = cst[:, P:P + PK]

        names = """cst_in key_in st_half sq_done ms_done rstd_done xs_done tp_done xf_done xh_done xl_done
            wh_done wl_done q_mm q_ev s_mm s_ev tk ex_in ex_done sel_done sT_mm sT_act ch_done cl_done""".split()
        S = {n: sems.enter_context(nc.semaphore("b_" + n)) for n in names}
        w_in = [sems.enter_context(nc.semaphore(f"b_w_in{i}")) for i in range(2)]
        NHP = 2 * PH
        block = ctx.enter_context(nc.Block())

        @block.sync
        def _(sp):
            sp.dma_start(cst[:], T["cst"][:, 0:256]).then_inc(S["cst_in"], 16)
            sp.dma_start(gcol[:], T["gcol"][:, 3 * KD:4 * KD]).then_inc(S["cst_in"], 16)
            sp.dma_start(keysT[:], T["keysT"]).then_inc(S["key_in"], 16)
            for u in range(NHP):
                if u >= 2:
                    sp.wait_ge(S["wl_done"], u - 1)
                sp.dma_start(wraw[:, u % 2, :], T["w_pq"][u]).then_inc(w_in[u % 2], 16)

        @block.gpsimd
        def _(pool):
            pool.memset(st[:, 19:20], -0.5).then_inc(S["st_half"], 1)
            pool.wait_ge(S["st_half"], 1)
            for t in range(NBLK):
                R = rows(t)
                pool.wait_ge(S["sq_done"], t + 1)
                nc.gpsimd.tensor_scalar(st[0:R, 5 + t:6 + t], st[0:R, t:t + 1], 1.0 / D, EPS, ALU.mult, ALU.add)\
                    .then_inc(S["ms_done"], 1)
                pool.wait_ge(S["ms_done"], t + 1)
                nc.gpsimd.tensor_tensor(st[0:R, 10 + t:11 + t], st[0:R, 5 + t:6 + t], st[0:R, 19:20], ALU.pow)\
                    .then_inc(S["rstd_done"], 1)

        @block.scalar
        def _(act):
            A = nc.scalar.activation

            def square(t):
                R = rows(t)
                if t >= 2:
                    act.wait_ge(S["tp_done"], 2 * (t - 1))
                A(xs[0:R, t % 2, :], h[0:R, t, :], ACT.Square, accum_out=st[0:R, t:t + 1])\
                    .then_inc(S["sq_done"], 1)

            square(0)
            for t in range(NBLK):
                R = rows(t)
                if t + 1 < NBLK:
                    square(t + 1)
                act.wait_ge(S["rstd_done"], t + 1)
                A(xs[0:R, t % 2, :], h[0:R, t, :], ACT.Copy, scale=st[0:R, 10 + t:11 + t])\
                    .then_inc(S["xs_done"], 1)
                if t >= 1:
                    for half in range(2):
                        act.wait_ge(S["xf_done"], 2 * (t - 1) + half + 1)
                        A(xh[:, 4 * half:4 * half + 4, toks(t - 1)], xf[:, half, :, 0:P], ACT.Copy)\
                            .then_inc(S["xh_done"], 1)
            for half in range(2):
                act.wait_ge(S["xf_done"], 2 * (NBLK - 1) + half + 1)
                A(xh[:, 4 * half:4 * half + 4, toks(NBLK - 1)], xf[:, half, :, 0:NS], ACT.Copy)\
                    .then_inc(S["xh_done"], 1)
            for u in range(NHP + 2):
                if u < NHP:
                    act.wait_ge(w_in[u % 2], 16 * (u // 2 + 1))
                    if u >= 2:
                        act.wait_ge(S["q_mm"], u - 1)
                    A(wh[:, u % 2, :], wraw[:, u % 2, :], ACT.Copy).then_inc(S["wh_done"], 1)
                v = u - 1
                if 0 <= v < NHP:
                    act.wait_ge(S["q_mm"], v + 1)
                    if v >= 2:
                        act.wait_ge(S["s_mm"], v - 1)
                    A(qT[:, v % 2, :], bank(2 + 2 * (v % 2), NTOK), ACT.Copy).then_inc(S["q_ev"], 1)
                v = u - 2
                if v >= 0:
                    act.wait_ge(S["s_mm"], v + 1)
                    A(sc[:, 0:4, v, :], bank(6).rearrange("p (t k) -> p t k", t=4), ACT.Copy)\
                        .then_inc(S["s_ev"], 1)
                    A(sc[0:NS, 4, v, :], bank(7, P, p1=NS), ACT.Copy).then_inc(S["s_ev"], 1)
            for t in range(NBLK):
                R = rows(t)
                act.wait_ge(S["ex_in"], t + 1)
                A(sel[0:R, 2, :], sel[0:R, 2, :], ACT.Exp).then_inc(S["ex_done"], 1)
                act.wait_ge(S["sT_mm"], t + 1)
                A(IT[:, toks(t)], bank(0, R), ACT.Copy).then_inc(S["sT_act"], 1)
                A(JT[:, toks(t)], bank(0, R, P), ACT.Copy).then_inc(S["sT_act"], 1)

        @block.vector
        def _(dve):
            V = nc.vector
            dve.wait_ge(S["cst_in"], 32)

            def low(t, half):
                R = rows(t)
                dve.wait_ge(S["xh_done"], 2 * t + half + 1)
                dst = (slice(None), slice(4 * half, 4 * half + 4), toks(t))
                V.tensor_tensor(xl[dst], xf[:, half, :, 0:R], xh[dst].bitcast(F32), ALU.subtract)\
                    .then_inc(S["xl_done"], 1)

            for t in range(NBLK):
                R = rows(t)
                for half in range(2):
                    if t >= 1:
                        low(t - 1, half)
                        dve.wait_ge(S["xl_done"], 2 * (t - 1) + half + 1)
                    dve.wait_ge(S["tp_done"], 2 * t + half + 1)
                    V.tensor_tensor(xf[:, half, :, 0:R], bank(half, 4 * R).rearrange("p (a r) -> p a r", a=4),
                                    gcol[:, 4 * half:4 * half + 4].unsqueeze(2).broadcast_to([P, 4, R]), ALU.mult)\
                        .then_inc(S["xf_done"], 1)
            for half in range(2):
                low(NBLK - 1, half)
            for u in range(NHP):
                dve.wait_ge(S["wh_done"], u + 1)
                V.tensor_tensor(wl[:, u % 2, :], wraw[:, u % 2, :], wh[:, u % 2, :].bitcast(F32), ALU.subtract)\
                    .then_inc(S["wl_done"], 1)

            done = [0]

            def then(ins):
                ins.then_inc(S["tk"], 1)
                done[0] += 1
                dve.wait_ge(S["tk"], done[0])

            def top16(xs_, val, idx):
                for first in range(2):
                    w = slice(8 * first, 8 * first + 8)
                    for k, x in enumerate(xs_):
                        last = V.max(val[:, k, w], x)
                    then(last)
                    for k, x in enumerate(xs_):
                        last = V.max_index(idx[:, k, w], val[:, k, w], x)
                    then(last)
                    if first == 0:
                        for k, x in enumerate(xs_):
                            last = V.match_replace(x, val[:, k, w], x, TAKEN)
                        then(last)

            dve.wait_ge(S["s_ev"], 2 * NHP)
            for t in range(NBLK):
                R = rows(t)
                top16([sc[0:R, t, k, :] for k in range(NHP)], mv[0:R], mi[0:R])
                V.tensor_copy(mf[0:R], mi[0:R])
                m4 = mv[0:R].rearrange("p (h a) k -> p h a k", a=2)
                f4 = mf[0:R].rearrange("p (h a) k -> p h a k", a=2)
                then(V.tensor_tensor(cand[0:R], m4[:, :, 0, :].unsqueeze(3).broadcast_to([R, PH, PK, PK]),
                                     m4[:, :, 1, :].unsqueeze(2).broadcast_to([R, PH, PK, PK]), ALU.add))
                top16([cand[0:R, k, :, :].rearrange("p a b -> p (a b)") for k in range(PH)], gv[0:R], gi[0:R])
                if t >= 1:
                    dve.wait_ge(S["sT_mm"], t)
                g3 = sel[0:R, 2, :].rearrange("p (h k) -> p h k", h=PH)
                V.tensor_tensor(g3, gv[0:R], gv[0:R, :, 0:1].broadcast_to([R, PH, PK]), ALU.subtract)\
                    .then_inc(S["ex_in"], 1)
                V.tensor_scalar(ga[0:R, 0, :], gi[0:R].rearrange("p h k -> p (h k)"), 4, None,
                                ALU.logical_shift_right)
                then(V.tensor_scalar(ga[0:R, 1, :], gi[0:R].rearrange("p h k -> p (h k)"), 15, None,
                                     ALU.bitwise_and))
                then(V.tensor_copy(gf[0:R], ga[0:R]))
                for a in range(2):
                    rank = gf[0:R, a, :].rearrange("p (h k) -> p h k", h=PH)
                    then(V.tensor_tensor(hit[0:R].rearrange("p h k c -> p (h k) c"),
                                         gf[0:R, a, :].unsqueeze(2).broadcast_to([R, PH * PK, PK]),
                                         iota16[0:R, :].unsqueeze(1).broadcast_to([R, PH * PK, PK]), ALU.is_equal))
                    then(V.tensor_tensor(hit[0:R], hit[0:R],
                                         f4[:, :, a, :].unsqueeze(2).broadcast_to([R, PH, PK, PK]), ALU.mult))
                    then(V.reduce_sum(sel[0:R, a, :], hit[0:R].rearrange("p h k c -> p (h k) c"), AX))
                dve.wait_ge(S["ex_done"], t + 1)
                then(V.reduce_sum(gs[0:R, 0, :], g3, AX))
                then(V.reciprocal(gs[0:R, 1, :], gs[0:R, 0, :]))
                V.tensor_tensor(g3, g3, gs[0:R, 1, :].unsqueeze(2).broadcast_to([R, PH, PK]), ALU.mult)\
                    .then_inc(S["sel_done"], 1)
                dve.wait_ge(S["sT_mm"], t + 1)
                V.tensor_copy(ch[:, toks(t)], bank(1, R)).then_inc(S["ch_done"], 1)
                dve.wait_ge(S["ch_done"], t + 1)
                V.tensor_tensor(cl[:, toks(t)], bank(1, R), ch[:, toks(t)].bitcast(F32), ALU.subtract)\
                    .then_inc(S["cl_done"], 1)

        @block.tensor
        def _(pe):
            M = nc.tensor.matmul
            pe.wait_ge(S["cst_in"], 32)
            for t in range(NBLK):
                R = rows(t)
                pe.wait_ge(S["xs_done"], t + 1)
                for half in range(2):
                    if t >= 1:
                        pe.wait_ge(S["xf_done"], 2 * (t - 1) + half + 1)
                    for a in range(4):
                        c = 4 * half + a
                        last = nc.tensor.transpose(bank(half, R, a * R), xs[0:R, t % 2, c * P:(c + 1) * P],
                                                   ident[0:R, 0:R])
                    last.then_inc(S["tp_done"], 1)
            pe.wait_ge(S["xl_done"], 2 * NBLK)
            pe.wait_ge(S["key_in"], 16)

            def key_scores(u):
                pe.wait_ge(S["q_ev"], u + 1)
                if u >= 1:
                    pe.wait_ge(S["s_ev"], 2 * u)
                for t in range(NBLK):
                    R = rows(t)
                    last = M(PS[0:R, 6 * BANK + t * P:6 * BANK + (t + 1) * P], qT[:, u % 2, toks(t)],
                             keysT[:, u, :], start=True, stop=True)
                last.then_inc(S["s_mm"], 1)

            for u in range(NHP):
                pe.wait_ge(S["wl_done"], u + 1)
                if u >= 2:
                    pe.wait_ge(S["q_ev"], u - 1)
                for lo, hi in ((0, SEQ), (SEQ, NTOK)):
                    o = (2 + 2 * (u % 2)) * BANK
                    for k in range(KD):
                        c = slice(k * P, (k + 1) * P)
                        for w, x in ((wh, xh), (wl, xh), (wh, xl)):
                            last = M(PS[:, o + lo:o + hi], w[:, u % 2, c], x[:, k, lo:hi],
                                     start=(k == 0 and w is wh and x is xh), stop=(k == KD - 1 and x is xl))
                last.then_inc(S["q_mm"], 1)
                if u >= 1:
                    key_scores(u - 1)
            key_scores(NHP - 1)
            for t in range(NBLK):
                R = rows(t)
                pe.wait_ge(S["sel_done"], t + 1)
                if t >= 1:
                    pe.wait_ge(S["sT_act"], 2 * t)
                    pe.wait_ge(S["cl_done"], t)
                for a in range(3):
                    last = nc.tensor.transpose(bank(a // 2, R, (a % 2) * P), sel[0:R, a, :], ident[0:R, 0:R])
                last.then_inc(S["sT_mm"], 1)


def peer_dense(nc, T, h, sems, xh, xl, IT, JT, ch, cl):
    HALF = NKEY // 2
    GROUPS = [(0, 2 * P, [0, 1]), (2 * P, NTOK, [2, 3, 4])]
    NGMAX = NTOK - 2 * P
    TG = 2
    ctx = ExitStack()
    with ctx:
        def sb(name, shape, dt=F32):
            return ctx.enter_context(nc.sbuf_tensor(name, shape, dt))

        PS = ctx.enter_context(nc.psum_tensor("psC", [P, 8 * BANK], F32))

        def bank(b, n=BANK, at=0, p0=0, p1=P):
            return PS[p0:p1, b * BANK + at:b * BANK + at + n]

        iota = sb("iotaC", [P, NKEY])
        gate = sb("gate", [P, HALF, NGMAX])
        rU = sb("rU", [P, 2, D])
        rV = sb("rV", [P, 2, D])
        Uh = sb("Uh", [P, 2, D], F32R)
        Ul = sb("Ul", [P, 2, D], F32R)
        Vh = sb("Vh", [P, 2, D], F32R)
        Vl = sb("Vl", [P, 2, D], F32R)
        ge = sb("ge", [P, NGMAX])
        wf = sb("wf", [P, NGMAX])
        Wh = sb("Wh", [P, 2, NGMAX], F32R)
        Wl = sb("Wl", [P, 2, NGMAX], F32R)
        ohI = sb("ohI", [P, 2, TG, NKEY], F32R)
        ohJ = sb("ohJ", [P, 2, TG, 2, HALF], F32R)

        names = """iota_in oh_done oh_used gt_ev hU lU hV lV u_mm ge_done w_mul w_hi w_done v_mm
            y_added""".split()
        S = {n: sems.enter_context(nc.semaphore("c_" + n)) for n in names}
        rU_in = [sems.enter_context(nc.semaphore(f"c_rU{i}")) for i in range(2)]
        rV_in = [sems.enter_context(nc.semaphore(f"c_rV{i}")) for i in range(2)]
        block = ctx.enter_context(nc.Block())
        NSTEP = 2 * NKEY
        PHASES = []
        sets = 0
        for g, (lo, hi, _) in enumerate(GROUPS):
            for jh in range(2):
                PHASES.append((g, jh, (2 * g + jh) * HALF, sets))
                sets += (hi - lo) // TG

        def pairs(eng, step, base, first, last):
            with eng.Fori(first // 2, last // 2) as i:
                for k in range(2):
                    step(base + 2 * i + k, 2 * i + k, k)

        @block.sync
        def _(sp):
            sp.dma_start(iota[:], T["cst"][:, C_IOTA:C_IOTA + NKEY]).then_inc(S["iota_in"], 16)

            def load(s, j, k):
                if not isinstance(s, int) or s >= 2:
                    sp.wait_ge(S["lU"], s - 1)
                sp.dma_start(rU[:, k, :], T["peer_uT"][bass.ds(j, 1), :, :].rearrange("a p c -> (a p) c"))\
                    .then_inc(rU_in[k], 16)
                if not isinstance(s, int) or s >= 2:
                    sp.wait_ge(S["lV"], s - 1)
                sp.dma_start(rV[:, k, :], T["peer_v"][bass.ds(j, 1), :, :].rearrange("a p c -> (a p) c"))\
                    .then_inc(rV_in[k], 16)

            load(0, 0, 0)
            load(1, 1, 1)
            pairs(sp, load, 0, 2, NKEY)
            pairs(sp, load, NKEY, 0, NKEY)

        @block.scalar
        def _(act):
            A = nc.scalar.activation

            def high_u(s, k):
                act.wait_ge(rU_in[k], 8 * (s - k) + 16)
                if not isinstance(s, int) or s >= 2:
                    act.wait_ge(S["u_mm"], s - 1)
                A(Uh[:, k, :], rU[:, k, :], ACT.Copy).then_inc(S["hU"], 1)

            def high_v(s, k):
                act.wait_ge(rV_in[k], 8 * (s - k) + 16)
                if not isinstance(s, int) or s >= 2:
                    act.wait_ge(S["v_mm"], s - 1)
                A(Vh[:, k, :], rV[:, k, :], ACT.Copy).then_inc(S["hV"], 1)

            high_u(0, 0)
            high_u(1, 1)
            high_v(0, 0)
            for g, jh, base, set0 in PHASES:
                lo, hi, _ = GROUPS[g]
                NG = hi - lo

                with act.Fori(0, NG // 16) as i:
                    for k in range(2):
                        act.wait_ge(S["oh_used"], set0 + 8 * i + 4 * k + 4)
                        act.nop(nofuse=True)
                        A(gate[:, :, bass.ds(16 * i + 8 * k, 8)].rearrange("p j n -> p n j"),
                          bank(6 + k).rearrange("p (n j) -> p n j", n=8), ACT.Copy).then_inc(S["gt_ev"], 1)

                def gelu(s, k):
                    act.wait_ge(S["u_mm"], s + 1)
                    act.wait_ge(S["w_mul"], s)
                    A(ge[:, 0:NG], bank(6 + k, NG), ACT.Gelu).then_inc(S["ge_done"], 1)

                def step(s, c, k):
                    gelu(s, k)
                    high_u(s + 2, k)
                    high_v(s + 1, 1 - k)

                if base + HALF < NSTEP:
                    if base == 0:
                        step(0, 0, 0)
                        step(1, 1, 1)
                        pairs(act, step, base, 2, HALF)
                    else:
                        pairs(act, step, base, 0, HALF)
                else:
                    pairs(act, step, base, 0, HALF - 2)
                    gelu(NSTEP - 2, 0)
                    high_v(NSTEP - 1, 1)
                    gelu(NSTEP - 1, 1)

        @block.vector
        def _(dve):
            V = nc.vector
            dve.wait_ge(S["iota_in"], 16)

            def low_u(s, k):
                dve.wait_ge(S["hU"], s + 1)
                V.tensor_tensor(Ul[:, k, :], rU[:, k, :], Uh[:, k, :].bitcast(F32), ALU.subtract)\
                    .then_inc(S["lU"], 1)

            def low_v(s, k):
                dve.wait_ge(S["hV"], s + 1)
                V.tensor_tensor(Vl[:, k, :], rV[:, k, :], Vh[:, k, :].bitcast(F32), ALU.subtract)\
                    .then_inc(S["lV"], 1)

            low_u(0, 0)
            low_u(1, 1)
            low_v(0, 0)
            for g, jh, base, set0 in PHASES:
                lo, hi, blocks = GROUPS[g]
                NG = hi - lo

                def one_hots(q, n, k):
                    if not isinstance(q, int) or q >= 2:
                        dve.wait_ge(S["oh_used"], q - 1)
                    for a in range(TG):
                        col = bass.ds(lo + n + a, 1)
                        V.tensor_scalar(ohI[:, k, a, :], iota[:], IT[:, col], None, ALU.is_equal)
                        V.tensor_scalar(ohJ[:, k, a, 0, :], iota[:, jh * HALF:(jh + 1) * HALF], JT[:, col],
                                        ch[:].bitcast(F32)[:, col], ALU.is_equal, ALU.mult)
                        last = V.tensor_scalar(ohJ[:, k, a, 1, :], iota[:, jh * HALF:(jh + 1) * HALF], JT[:, col],
                                               cl[:].bitcast(F32)[:, col], ALU.is_equal, ALU.mult)
                    last.then_inc(S["oh_done"], 1)

                if set0 == 0:
                    for q in range(4):
                        one_hots(q, TG * q, q % 2)
                with dve.Fori(1 if set0 == 0 else 0, NG // 8) as i:
                    for q in range(4):
                        one_hots(set0 + 4 * i + q, 8 * i + TG * q, q % 2)
                dve.wait_ge(S["gt_ev"], (set0 + NG // TG) // 4)

                def weigh(s, c, k):
                    dve.wait_ge(S["ge_done"], s + 1)
                    dve.wait_ge(S["w_done"], s)
                    V.tensor_tensor(wf[:, 0:NG], ge[:, 0:NG], gate[:, bass.ds(c, 1), 0:NG].rearrange("p a n -> p (a n)"),
                                    ALU.mult).then_inc(S["w_mul"], 1)
                    dve.wait_ge(S["w_mul"], s + 1)
                    if not isinstance(s, int) or s >= 2:
                        dve.wait_ge(S["v_mm"], s - 1)
                    V.tensor_copy(Wh[:, k, 0:NG], wf[:, 0:NG]).then_inc(S["w_hi"], 1)
                    dve.wait_ge(S["w_hi"], s + 1)
                    V.tensor_tensor(Wl[:, k, 0:NG], wf[:, 0:NG], Wh[:, k, 0:NG].bitcast(F32), ALU.subtract)\
                        .then_inc(S["w_done"], 1)

                def step(s, c, k):
                    weigh(s, c, k)
                    low_u(s + 2, k)
                    low_v(s + 1, 1 - k)

                if base + HALF < NSTEP:
                    if base == 0:
                        step(0, 0, 0)
                        step(1, 1, 1)
                        pairs(dve, step, base, 2, HALF)
                    else:
                        pairs(dve, step, base, 0, HALF)
                else:
                    pairs(dve, step, base, 0, HALF - 2)
                    weigh(NSTEP - 2, HALF - 2, 0)
                    low_v(NSTEP - 1, 1)
                    weigh(NSTEP - 1, HALF - 1, 1)
                if jh == 1:
                    dve.wait_ge(S["v_mm"], base + HALF)
                    for b, t in enumerate(blocks):
                        R = rows(t)
                        V.tensor_tensor(h[0:R, t, :], PS[0:R, 2 * b * BANK:2 * (b + 1) * BANK], h[0:R, t, :],
                                        ALU.add).then_inc(S["y_added"], 1)

        @block.tensor
        def _(pe):
            M = nc.tensor.matmul
            for g, jh, base, set0 in PHASES:
                lo, hi, blocks = GROUPS[g]
                NG = hi - lo
                if base > 0:
                    pe.wait_ge(S["ge_done"], base)

                def tokens8(u, k):
                    if not isinstance(u, int) or u >= 2:
                        pe.wait_ge(S["gt_ev"], u - 1)
                    for q in range(4):
                        pe.wait_ge(S["oh_done"], 4 * u + q + 1)
                        for a in range(TG):
                            o = bank(6 + k, HALF, (TG * q + a) * HALF)
                            M(o, ohI[:, q % 2, a, :], ohJ[:, q % 2, a, 0, :], start=True, stop=False)
                            last = M(o, ohI[:, q % 2, a, :], ohJ[:, q % 2, a, 1, :], start=False, stop=True)
                        last.then_inc(S["oh_used"], 1)

                if set0 == 0:
                    tokens8(0, 0)
                    tokens8(1, 1)
                with pe.Fori(1 if set0 == 0 else 0, NG // 16) as i:
                    for k in range(2):
                        tokens8(set0 // 4 + 2 * i + k, k)
                pe.wait_ge(S["gt_ev"], (set0 + NG // TG) // 4)

                def up(s, k):
                    pe.wait_ge(S["lU"], s + 1)
                    if not isinstance(s, int) or s >= 2:
                        pe.wait_ge(S["ge_done"], s - 1)
                    for d in range(KD):
                        c = slice(d * P, (d + 1) * P)
                        for a, x in ((Uh, xh), (Ul, xh), (Uh, xl)):
                            last = M(bank(6 + k, NG), a[:, k, c], x[:, d, lo:hi],
                                     start=(d == 0 and a is Uh and x is xh), stop=(d == KD - 1 and x is xl))
                    last.then_inc(S["u_mm"], 1)

                def down(s, k, first=False, final=False):
                    pe.wait_ge(S["w_done"], s + 1)
                    pe.wait_ge(S["lV"], s + 1)
                    for b, t in enumerate(blocks):
                        R = rows(t)
                        for n in range(2):
                            c = slice(n * 512, (n + 1) * 512)
                            for a, w, v in ((0, Wh, Vh), (1, Wl, Vh), (2, Wh, Vl)):
                                last = M(bank(2 * b + n, p1=R), w[:, k, b * P:b * P + R], v[:, k, c],
                                         start=(first and a == 0), stop=(final and a == 2),
                                         skip_group_check=True)
                    last.then_inc(S["v_mm"], 1)

                up(base, 0)
                if jh == 0:
                    if g == 1:
                        pe.wait_ge(S["y_added"], len(GROUPS[0][2]))
                    up(base + 1, 1)
                    down(base, 0, first=True)
                    up(base + 2, 0)
                    down(base + 1, 1)
                with pe.Fori(1 if jh == 0 else 0, HALF // 2 - 1) as i:
                    up(base + 2 * i + 1, 1)
                    down(base + 2 * i, 0)
                    up(base + 2 * i + 2, 0)
                    down(base + 2 * i + 1, 1)
                up(base + HALF - 1, 1)
                down(base + HALF - 2, 0)
                down(base + HALF - 1, 1, final=(jh == 1))


def final_norm(nc, T, h, sems):
    ctx = ExitStack()
    with ctx:
        def sb(name, shape, dt=F32):
            return ctx.enter_context(nc.sbuf_tensor(name, shape, dt))

        st = sb("stD", [P, 20])
        junk = sb("junk", [P, NBLK, D])
        gfin = sb("gfin", [P, D])
        y = sb("y", [P, NBLK, D])
        S = {n: sems.enter_context(nc.semaphore("d_" + n)) for n in "g_in st_half sq ms rstd y_done y_out".split()}
        block = ctx.enter_context(nc.Block())

        @block.sync
        def _(sp):
            sp.dma_start(gfin[:], T["norm_final"].broadcast_to([P, D])).then_inc(S["g_in"], 16)
            for t in range(NBLK):
                sp.wait_ge(S["y_done"], t + 1)
                dst = T["y_p"][toks(t), :] if t < 4 else T["y_s"]
                sp.dma_start(dst, y[0:rows(t), t, :]).then_inc(S["y_out"], 16)
            sp.wait_ge(S["y_out"], 16 * NBLK)

        @block.scalar
        def _(act):
            for t in range(NBLK):
                R = rows(t)
                nc.scalar.activation(junk[0:R, t, :], h[0:R, t, :], ACT.Square, accum_out=st[0:R, t:t + 1])\
                    .then_inc(S["sq"], 1)

        @block.gpsimd
        def _(pool):
            pool.memset(st[:, 19:20], -0.5).then_inc(S["st_half"], 1)
            pool.wait_ge(S["st_half"], 1)
            for t in range(NBLK):
                R = rows(t)
                pool.wait_ge(S["sq"], t + 1)
                nc.gpsimd.tensor_scalar(st[0:R, 5 + t:6 + t], st[0:R, t:t + 1], 1.0 / D, EPS, ALU.mult, ALU.add)\
                    .then_inc(S["ms"], 1)
                pool.wait_ge(S["ms"], t + 1)
                nc.gpsimd.tensor_tensor(st[0:R, 10 + t:11 + t], st[0:R, 5 + t:6 + t], st[0:R, 19:20], ALU.pow)\
                    .then_inc(S["rstd"], 1)

        @block.vector
        def _(dve):
            dve.wait_ge(S["g_in"], 16)
            for t in range(NBLK):
                R = rows(t)
                dve.wait_ge(S["rstd"], t + 1)
                nc.vector.scalar_tensor_tensor(out=y[0:R, t, :], in0=h[0:R, t, :], scalar=st[0:R, 10 + t:11 + t],
                                               in1=gfin[0:R, :], op0=ALU.mult, op1=ALU.mult)\
                    .then_inc(S["y_done"], 1)


def build(nc, T):
    ctx = ExitStack()
    with ctx:
        h = ctx.enter_context(nc.sbuf_tensor("h", [P, NBLK, D], F32))
        block_a(nc, T, h, ctx)
        x = [ctx.enter_context(nc.sbuf_tensor(n, [P, KD, NTOK], F32R)) for n in ("xh", "xl")]
        IJ = [ctx.enter_context(nc.sbuf_tensor(n, [P, NTOK], F32)) for n in ("IT", "JT")]
        c = [ctx.enter_context(nc.sbuf_tensor(n, [P, NTOK], F32R)) for n in ("ch", "cl")]
        peer_select(nc, T, h, ctx, *x, *IJ, *c)
        peer_dense(nc, T, h, ctx, *x, *IJ, *c)
        final_norm(nc, T, h, ctx)


HEADS = [0, 4, 1, 5, 2, 6, 3, 7]


def constants():
    c = np.zeros((P, C_ALL), np.float32)
    c[:, C_ID:C_ID + P] = np.eye(P)
    c[:, C_IOTA:C_IOTA + P] = np.arange(P)
    q, k = np.arange(P)[:, None], np.arange(P)[None, :]
    c[:, C_CAUSAL:C_CAUSAL + P] = np.where(k <= q, 0, NEG)
    q, k = np.arange(NS)[:, None], np.arange(NS)[None, :]
    c[:NS, C_NEW:C_NEW + NS] = np.where((q // NQ == k // NQ) & (k <= q), 0, NEG)
    same = np.zeros((NS, NB, 8, NQ), np.float32)
    for tok in range(NS):
        same[tok, tok // NQ, :, tok % NQ] = 1
    c[:NS, C_SAME:C_SAME + 512] = same.reshape(NS, 512)
    inv = np.float32(10000.0) ** (-np.arange(32, dtype=np.float32) / np.float32(32))
    pos = np.zeros((NBLK, P), np.float32)
    pos[:4] = np.arange(SEQ).reshape(4, P)
    pos[4, :NS] = PAST + np.arange(NS) % NQ
    ang = pos[:, :, None] * inv
    cos, sin = np.cos(ang), np.sin(ang)
    c[:, C_COS:C_COS + 320] = np.concatenate([cos, cos], -1).transpose(1, 0, 2).reshape(P, 320)
    c[:, C_SIN:C_SIN + 320] = np.concatenate([-sin, sin], -1).transpose(1, 0, 2).reshape(P, 320)
    return c


def kernel(**inputs):
    import concourse.bacc as _bacc
    from concourse.bass_utils import run_bass_kernel_spmd as _run

    x = {k: np.asarray(v) for k, v in inputs.items()}
    n_pool = x["cache_mla_ckv"].shape[1]

    def chunks(w):
        return w.reshape(-1, P, w.shape[-1]).transpose(1, 0, 2)

    w_in = x["w_in"][0]
    dq = w_in[:, DQ:DQ + 512].reshape(D, 8, 64)[:, HEADS].reshape(D, 512)
    w_in = np.concatenate([w_in[:, :DQ], dq, w_in[:, DK:]], 1)
    w_uq = x["w_uq"][0].reshape(256, 8, 96)
    w_o = x["w_o"][0]
    w_o = np.concatenate([w_o[:512], w_o[512:].reshape(8, 64, D)[HEADS].reshape(512, D)], 0)
    ckv, kr = x["cache_mla_ckv"][0], x["cache_mla_kr"][0]
    kv = x["cache_dsa_kv"][0].reshape(n_pool, PAGE, 2, 128)
    gains = [x[n][0].reshape(-1, P).T for n in ("norm_mix", "norm_mem", "mem_norm", "norm_ffn", "mla_q_norm")]
    mk = x["cache_mem_k"][0].reshape(NB, 256, 2, P).transpose(0, 3, 2, 1)
    mv = x["cache_mem_v"][0].reshape(NB, 2, P, 256).transpose(0, 2, 1, 3)
    arrays = {
        "cst": constants(),
        "x_prompt": x["x_prompt"], "x_sample": x["x_sample"], "mem_prompt": x["mem_prompt"],
        "gcol": np.concatenate(gains, 1), "mla_kv_norm": x["mla_kv_norm"], "norm_final": x["norm_final"][None],
        "page_table": x["page_table"].reshape(1, -1),
        "w_in": chunks(w_in),
        "w_uqn": chunks(w_uq[:, :, :64].reshape(256, 512)), "w_uqr": chunks(w_uq[:, :, 64:].reshape(256, 256)),
        "w_ukT": chunks(x["w_uk"][0].transpose(1, 2, 0).reshape(512, 128)),
        "w_uv": x["w_uv"][0].reshape(128, 512),
        "w_o": chunks(w_o),
        "wq_x": chunks(x["wq_x"][0]), "wkv_x": chunks(np.concatenate([x["wk_x"][0], x["wv_x"][0]], 1)),
        "wo_x": chunks(x["wo_x"][0]),
        "mem_cache": np.concatenate([mk, mv], 2),
        "ikT": x["cache_dsa_idx"][0].transpose(0, 2, 1), "krT": kr.transpose(0, 2, 1),
        "poolK": np.concatenate([ckv.transpose(0, 2, 1), kv[:, :, 0].transpose(0, 2, 1)], 2),
        "poolV": np.concatenate([ckv, kv[:, :, 1]], 2),
        "w_pq": x["w_pq"][0].reshape(KD, P, 2 * PH, P).transpose(2, 1, 0, 3).reshape(2 * PH, P, D),
        "keysT": x["peer_keys"][0].reshape(2 * PH, NKEY, P).transpose(2, 0, 1),
        "peer_uT": x["peer_u"][0].reshape(NKEY, NKEY, KD, P).transpose(1, 3, 2, 0).reshape(NKEY, P, D),
        "peer_v": x["peer_v"][0].reshape(NKEY, NKEY, D).transpose(1, 0, 2),
    }
    outs = {
        "y_p": (1, SEQ, D), "y_s": (NB, NQ, D),
        "new_ckv_p": (1, 1, SEQ, 128), "new_kr_p": (1, 1, SEQ, 32), "new_kv_p": (1, 1, SEQ, 2, 2, 64),
        "new_idx_p": (1, 1, SEQ, 64), "new_mem_k_p": (1, 1, 256, 4, 64), "new_mem_v_p": (1, 1, 256, 4, 64),
        "new_ckv_s": (1, NB, NQ, 128), "new_kr_s": (1, NB, NQ, 32), "new_kv_s": (1, NB, NQ, 2, 2, 64),
        "new_idx_s": (1, NB, NQ, 64),
    }
    flat = {"y_p": (SEQ, D), "y_s": (NS, D)}
    for n, s in outs.items():
        toks_ = int(np.prod(s[:3])) if n[:3] == "new" else flat[n][0]
        flat[n] = (toks_, int(np.prod(s)) // toks_)
    nc = _bacc.Bacc("TRN2", target_bir_lowering=False, num_devices=1)
    T = {"n_pool": n_pool}
    arrays = {n: np.ascontiguousarray(a) for n, a in arrays.items()}
    for n, a in arrays.items():
        T[n] = nc.dram_tensor("in_" + n, a.shape, mybir.dt.from_np(a.dtype), kind="ExternalInput").ap()
    for n, s in flat.items():
        T[n] = nc.dram_tensor("out_" + n, s, F32, kind="ExternalOutput").ap()
    build(nc, T)
    r = _run(nc, [{"in_" + n: a for n, a in arrays.items()}], core_ids=[0])
    return tuple(np.asarray(r.results[0]["out_" + n]).reshape(s) for n, s in outs.items())
```

```python
from contextlib import ExitStack

import numpy as np
import concourse.bass as bass
from concourse import mybir
from concourse.alu_op_type import AluOpType as ALU

F32 = mybir.dt.float32
F32R = mybir.dt.float32r
BF16 = mybir.dt.bfloat16
U32 = mybir.dt.uint32
I32 = mybir.dt.int32
ACT = mybir.ActivationFunctionType
AX = mybir.AxisListType.X

P = 128
D = 1024
KD = D // P
SEQ, NB, NQ = 512, 8, 8
NS = NB * NQ
NTOK = SEQ + NS
NBLK = SEQ // P + 1
PAGE, NPAGE = 128, 16
PAST = PAGE * NPAGE
NEWC = PAST + NS
W_IN = 1768
CQ, CKV, KR, DQ, DK, DV, IQ, IW, IK = 0, 256, 384, 416, 928, 1056, 1184, 1696, 1704
PC = W_IN // 4
EPS = 1e-6
NEG = -1e30
TAKEN = -3e38
K_PROMPT, K_SAMPLE = 128, 256
MLA_SCALE = 96 ** -0.5
DSA_SCALE = 64 ** -0.5
NKEY, PH, PK = 128, 8, 16
BANK = 512

C_ID, C_IOTA, C_CAUSAL, C_NEW, C_SAME, C_COS, C_SIN = 0, 128, 256, 384, 448, 960, 1280
C_FIRST = 1600
C_ALL = 1632

ROWS16 = []
for _a in range(PK):
    ROWS16.append((_a, PK // (_a + 1), sum(n for _, n, _ in ROWS16)))
NCAND = ROWS16[-1][2] + 1


def rows(t):
    return P if t < NBLK - 1 else NS


def toks(t):
    return slice(t * P, t * P + rows(t))


def block_a(nc, T, h, sems):
    ctx = ExitStack()
    with ctx:
        def sb(name, shape, dt=F32):
            return ctx.enter_context(nc.sbuf_tensor(name, shape, dt))

        def sem(name):
            return sems.enter_context(nc.semaphore(name))

        PS = ctx.enter_context(nc.psum_tensor("psA", [P, 8 * BANK], F32))

        def bank(b, n=BANK, at=0, p0=0, p1=P):
            return PS[p0:p1, b * BANK + at:b * BANK + at + n]

        cst = sb("cst", [P, C_ALL])
        xT = sb("xT", [P, KD, NTOK])
        gcol = sb("gcol", [P, 4 * KD + 2])
        gkv = sb("gkv", [P, P])
        st = sb("st", [P, 160])
        sm = sb("sm", [P, 4 * 100])
        ssm = sb("ssm", [P, 4, NB])
        pts = sb("pts", [1, NB * NPAGE], I32)
        qrTs = sb("qrTs", [P, 2, 64])
        bdq = sb("bdq", [P, NB, 2, 4, NQ])
        Dp = sb("Dp", [P, 4, NS])
        same16 = sb("same16", [NS, NB, 64], BF16)
        id16 = sb("id16", [P, P], BF16)
        causal16 = sb("causal16", [P, P], BF16)
        m8 = sb("m8", [P, 8])
        qlTs = sb("qlTs", [P, NB, 8, NQ])
        olT = sb("olT", [P, NB, 8, NQ])
        arena = sb("arena", [P, 37800])

        def region(at, *shape, p=P):
            n = int(np.prod(shape))
            a = arena[0:p, at:at + n]
            if len(shape) == 1:
                return a
            names = "abcd"[:len(shape)]
            spec = f"p ({' '.join(names)}) -> p {' '.join(names)}"
            return a.rearrange(spec, **{k: v for k, v in zip(names[1:], shape[1:])})

        win = region(0, KD, W_IN)
        proj = region(14144, NBLK, W_IN)
        kT = region(22984, 4, NTOK)
        dqT = region(25288, 4, NTOK)
        iqT = region(27592, 4, SEQ)
        iqTs = region(29640, NB, 8, NQ)
        cqT = region(30152, 2, NTOK)
        xs = region(31304, 2, D)
        ropeA = region(33352, 640)
        ropeM = region(33992, 640)
        kk = region(34632, 256)
        w_uqn = region(34888, 2, 512)
        w_uqr = region(35912, 2, 256)
        w_ukT = region(36424, 4, P)
        w_uv = region(36936, 512)
        qnT = region(0, 4, NTOK)
        qlT = region(2304, 8, SEQ)
        qrT = region(6400, 2, NTOK)
        Vm = region(7552, 4, 512)
        mb16 = region(9600, 4 * SEQ // 2).bitcast(BF16).rearrange("p (a b) -> p a b", a=4)
        accs = region(10624, 3, SEQ)
        relu = region(12160, 2, SEQ)
        qr = region(13184, 256)
        Pr = region(31304, 3, SEQ)
        PT = region(33352, 2, SEQ)
        ikT = region(0, NB // 2, PAST)
        KV = region(0, 2, 2, NPAGE, 256)
        krT = region(16384, 2, PAST)
        sw = region(32328, NEWC, p=NS)
        relus = region(31304, 2, 512)
        selE = region(20480, NB, 8, NQ, p=NS)
        Ps = region(25288, 2, NEWC)
        mbs = region(30152, NEWC // 2, p=NS).bitcast(BF16)
        PTs = region(31304, 2, SEQ)
        w_o = region(8192, KD, D)
        wqx = region(0, KD, 256)
        wkv = region(2048, KD, 512)
        memr = region(6144, 2, D)
        mT = region(16384, KD, 256)
        mkv = region(18432, 2, 512)
        mkT = region(19456, 2, 256)
        qxT = region(19968, 2, NTOK)
        bdx = region(21120, 2, NB, 4, NQ)
        oxT = region(21632, 2, NTOK)
        xc = region(22784, NB, 4, 256)
        wox = region(34888, 2, D)
        assert 22784 + 8192 <= 31304

        ident = cst[:, C_ID:C_ID + P]
        causal = cst[:, C_CAUSAL:C_CAUSAL + P]
        same = cst[0:NS, C_SAME:C_SAME + 512]
        cosT = cst[:, C_COS:C_COS + 320].rearrange("p (t c) -> p t c", t=NBLK)
        sinT = cst[:, C_SIN:C_SIN + 320].rearrange("p (t c) -> p t c", t=NBLK)

        names = """cst_in x_in win_in wsm_in pt_in mem_in late_in wox_in wo_in gk_in
            sq_done ms_done rstd_done xs_done tp_done xT_done pj_mm pj_act pj_dve
            sq2_done ms2_done rstd2_done cq_done ckv_done rp_dve rp_pool c16 half_ready
            tA_mm tB_mm tA_ev tB_ev up_mm up_ev ql_mm ql_ev qr_mm qr_chain qr_done qr_tp qr_ev 
            vm_mm vm_ev ix_mm ix_relu ix_acc mask_done tk
            at_S at_nb at_exp at_P at_T at_PT at_O at_oe at_c
            sel_E sel_T sel_D xi_mm xi_relu xi_sc sw_done mbs_done
            ss_S ss_nb ss_exp ss_P ss_T ss_PT ss_oe ss_c uv_mm uv_ev
            wo_mm h_done mkv_mm mkv_ev mkT_tp mkT_ev qx_mm qx_ev bdx_done ox_mm hx_done out_st""".split()
        S = {n: sem(n) for n in names}
        ik_sp, ik_pool = sem("ik_sp"), sem("ik_pool")
        kr_in = [sem(f"kr_in{i}") for i in range(4)]
        kv_sp = [sem(f"kv_sp{i}") for i in range(2)]
        kv_pool = [sem(f"kv_pool{i}") for i in range(2)]
        SMP = [(kind, p) for kind in range(2) for p in range(NB // 2)]

        IK_SP = 9

        def load_page(eng, dst, pool, b, j, done):
            pg = eng.value_load(pts[0:1, b * NPAGE + j:b * NPAGE + j + 1], min_val=0, max_val=T["n_pool"] - 1)
            eng.dma_start(dst, T[pool][bass.ds(pg, 1), :, :].rearrange("a q c -> (a q) c")).then_inc(done, 16)

        def load_index_keys(eng, j0, j1, done):
            eng.wait_ge(S["ql_ev"], 16)
            for b in range(NB):
                if b == 2:
                    eng.wait_ge(S["at_oe"], 4 * 8)
                p, b2 = divmod(b, 2)
                for j in range(j0, j1):
                    load_page(eng, ikT[64 * b2:64 * b2 + 64, p, j * PAGE:(j + 1) * PAGE], "ikT", b, j, done)

        def load_kv(eng, i, b2s, done):
            kind, p = SMP[i]
            if i == 0:
                eng.wait_ge(S["at_oe"], n_self)
                eng.wait_ge(S["out_st"], 16 * 4 * NBLK)
            elif i == 1:
                eng.wait_ge(S["xi_mm"], 20)
            else:
                eng.wait_ge(S["ss_c"], 5 * (i - 1))
            for b2 in b2s:
                for j in range(NPAGE):
                    load_page(eng, KV[:, (i + 1) % 2, b2, j, :], ("poolM", "poolD")[kind], 2 * p + b2, j,
                              done[(i + 1) % 2])

        SELF = [("mla", t, i) for i in range(8) for t in range(4)] + \
               [("dsa", t, i) for t in range(4) for i in range(8)]
        CROSS = [("mem", t, i) for t in range(4) for i in range(4)] + [("smp", 4, g) for g in range(2)]

        def keys_of(u):
            kind, t, i = u
            return P * (t + 1) if kind in ("mla", "dsa") else 256

        def scale_of(u):
            return MLA_SCALE if u[0] == "mla" else DSA_SCALE

        n_self, n_cross = len(SELF), len(CROSS)
        UNITS = SELF + CROSS
        NORM = {"mix": (0, 5, 0), "mem": (5, 2, 2 * KD), "xmem": (7, 5, KD)}
        STREAM_UNITS = 12

        def src_of(stage, t):
            return memr[:, t, :] if stage == "mem" else h[0:rows(t), t, :]

        def nrows(stage, t):
            return P if stage == "mem" else rows(t)

        def dst_of(stage, t):
            return mT[:, :, t * P:(t + 1) * P] if stage == "mem" else xT[:, :, toks(t)]

        block = ctx.enter_context(nc.Block())

        @block.sync
        def _(sp):
            sp.dma_start(cst[:], T["cst"]).then_inc(S["cst_in"], 16)
            for t in range(4):
                sp.dma_start(h[:, t, :], T["x_prompt"][0, t * P:(t + 1) * P, :]).then_inc(S["x_in"], 16)
            sp.dma_start(h[0:NS, 4, :], T["x_sample"].rearrange("b t d -> (b t) d")).then_inc(S["x_in"], 16)
            sp.dma_start(gcol[:], T["gcol"]).then_inc(S["gk_in"], 16)
            sp.dma_start(gkv[:], T["mla_kv_norm"].broadcast_to([P, P])).then_inc(S["gk_in"], 16)
            for k in range(KD):
                sp.dma_start(win[:, k, :], T["w_in"][:, k, :]).then_inc(S["win_in"], 16)
            sp.dma_start(pts[:], T["page_table"]).then_inc(S["pt_in"], 16)
            for dst, name in ((w_uqn, "w_uqn"), (w_uqr, "w_uqr"), (w_ukT, "w_ukT"), (w_uv, "w_uv")):
                sp.dma_start(dst, T[name]).then_inc(S["wsm_in"], 16)
            for t in range(NBLK):
                R = rows(t)
                sp.wait_ge(S["ckv_done"], t + 1)
                sp.wait_ge(S["rp_dve"], t + 1)
                sp.wait_ge(S["rp_pool"], t + 1)
                for name, c, n in (("ckv", CKV, 128), ("kr", KR, 32), ("kv", DK, 256), ("idx", IK, 64)):
                    dst = T[f"new_{name}_p"][toks(t), :] if t < 4 else T[f"new_{name}_s"]
                    sp.dma_start(dst, proj[0:R, t, c:c + n]).then_inc(S["out_st"], 16)

            sp.wait_ge(S["pt_in"], 16)

            load_index_keys(sp, 0, IK_SP, ik_sp)
            for i in range(NB):
                load_kv(sp, i, (0, 1) if SMP[i][0] == 0 else (0,), kv_sp)
            sp.wait_ge(S["ss_c"], 5 * (NB - 1))
            sp.dma_start(w_o, T["w_o"]).then_inc(S["wo_in"], 16)
            sp.wait_ge(S["ss_c"], 5 * NB)
            sp.dma_start(memr, T["mem_prompt"][0].rearrange("(a p) d -> p a d", p=P)).then_inc(S["mem_in"], 16)
            sp.dma_start(wkv, T["wkv_x"]).then_inc(S["late_in"], 16)
            sp.dma_start(wqx, T["wq_x"]).then_inc(S["late_in"], 16)
            sp.dma_start(xc, T["mem_cache"].rearrange("b p a c -> p b a c")).then_inc(S["late_in"], 16)
            sp.wait_ge(S["uv_ev"], 8)
            sp.dma_start(wox, T["wo_x"]).then_inc(S["wox_in"], 16)
            for t in range(2):
                sp.wait_ge(S["mkv_ev"], t + 1)
                for i, name in enumerate(("new_mem_k_p", "new_mem_v_p")):
                    sp.dma_start(T[name][t * P:(t + 1) * P, :], mkv[:, t, 256 * i:256 * (i + 1)])\
                        .then_inc(S["out_st"], 16)
            sp.wait_ge(S["out_st"], 16 * (4 * NBLK + 4))

        @block.gpsimd
        def _(pool):
            pool.memset(st[:, 156:158], -0.5).then_inc(S["half_ready"], 1)
            pool.memset(bdq[:], 0.0).then_inc(S["c16"], 1)

            def norm_rstd(stage):
                base, n, _ = NORM[stage]
                for t in range(n):
                    u, R = base + t, nrows(stage, t)
                    pool.wait_ge(S["sq_done"], u + 1)
                    nc.gpsimd.tensor_scalar(st[0:R, 40 + u:41 + u], st[0:R, u:u + 1], 1.0 / D, EPS,
                                            ALU.mult, ALU.add).then_inc(S["ms_done"], 1)
                    pool.wait_ge(S["ms_done"], u + 1)
                    nc.gpsimd.tensor_tensor(st[0:R, 80 + u:81 + u], st[0:R, 40 + u:41 + u],
                                            st[0:R, 156:157], ALU.pow).then_inc(S["rstd_done"], 1)

            pool.wait_ge(S["half_ready"], 1)
            norm_rstd("mix")
            pool.wait_ge(S["cst_in"], 16)
            for t in range(NBLK):
                R = rows(t)
                pool.wait_ge(S["sq2_done"], t + 1)
                for j, n in ((0, 256), (1, 128)):
                    c = 120 + 2 * t + j
                    nc.gpsimd.tensor_scalar(st[0:R, c:c + 1], st[0:R, c:c + 1], 1.0 / n, EPS,
                                            ALU.mult, ALU.add).then_inc(S["ms2_done"], 1)
                pool.wait_ge(S["ms2_done"], 2 * t + 2)
                nc.gpsimd.tensor_tensor(st[0:R, 140 + 2 * t:142 + 2 * t], st[0:R, 120 + 2 * t:122 + 2 * t],
                                        st[0:R, 156:158], ALU.pow).then_inc(S["rstd2_done"], 1)
                pool.wait_ge(S["rp_dve"], t + 1)
                if t >= 1:
                    pool.wait_ge(S["tA_mm"], 2 * t - 1)
                nc.gpsimd.tensor_copy(kk[0:R, 0:128].rearrange("p (a c) -> p a c", a=4),
                                      proj[0:R, t, KR:KR + 32].unsqueeze(1).broadcast_to([R, 4, 32]))
                nc.gpsimd.tensor_copy(kk[0:R, 128:256].rearrange("p (a c) -> p a c", a=2),
                                      proj[0:R, t, IK:IK + 64].unsqueeze(1).broadcast_to([R, 2, 64]))\
                    .then_inc(S["rp_pool"], 1)
            pool.wait_ge(S["pt_in"], 16)
            load_index_keys(pool, IK_SP, NPAGE, ik_pool)
            pool.wait_ge(S["at_oe"], n_self)
            pool.wait_ge(S["out_st"], 16 * 4 * NBLK)
            for b in range(NB):
                p, b2 = divmod(b, 2)
                for j in range(NPAGE):
                    load_page(pool, krT[32 * p:32 * p + 32, b2, j * PAGE:(j + 1) * PAGE], "krT", b, j, kr_in[p])
            for i in range(NB // 2, NB):
                load_kv(pool, i, (1,), kv_pool)
            norm_rstd("mem")
            norm_rstd("xmem")

        @block.scalar
        def _(act):
            def norm_scale(stage):
                base, n, _ = NORM[stage]

                def square(t):
                    u, R = base + t, nrows(stage, t)
                    if stage == "mix":
                        act.wait_ge(S["x_in"], 16 * NBLK)
                    elif stage == "mem":
                        act.wait_ge(S["mem_in"], 16)
                    else:
                        act.wait_ge(S["h_done"], 2 * (t + 1))
                    if u >= 2:
                        act.wait_ge(S["tp_done"], 2 * (u - 1))
                    nc.scalar.activation(xs[0:R, u % 2, :], src_of(stage, t), ACT.Square,
                                         accum_out=st[0:R, u:u + 1]).then_inc(S["sq_done"], 1)

                square(0)
                for t in range(n):
                    u, R = base + t, nrows(stage, t)
                    if t + 1 < n:
                        square(t + 1)
                    act.wait_ge(S["rstd_done"], u + 1)
                    nc.scalar.activation(xs[0:R, u % 2, :], src_of(stage, t), ACT.Copy,
                                         scale=st[0:R, 80 + u:81 + u]).then_inc(S["xs_done"], 1)

            norm_scale("mix")
            for t in range(NBLK):
                R = rows(t)
                for c in range(2):
                    act.wait_ge(S["pj_mm"], 4 * t + c + 1)
                    nc.scalar.activation(proj[0:R, t, c * PC:(c + 1) * PC], bank(2 + c, PC, p1=R), ACT.Copy)\
                        .then_inc(S["pj_act"], 1)
                act.wait_ge(S["pj_act"], 2 * t + 1)
                act.wait_ge(S["tp_done"], 10)
                if t >= 1:
                    act.wait_ge(S["cq_done"], t)
                nc.scalar.activation(xs[0:R, 0, 0:256], proj[0:R, t, CQ:CQ + 256], ACT.Square,
                                     accum_out=st[0:R, 120 + 2 * t:121 + 2 * t])
                nc.scalar.activation(xs[0:R, 0, 256:384], proj[0:R, t, CKV:CKV + 128], ACT.Square,
                                     accum_out=st[0:R, 121 + 2 * t:122 + 2 * t]).then_inc(S["sq2_done"], 1)
                act.wait_ge(S["rstd2_done"], t + 1)
                nc.scalar.activation(proj[0:R, t, CQ:CQ + 256], proj[0:R, t, CQ:CQ + 256], ACT.Copy,
                                     scale=st[0:R, 140 + 2 * t:141 + 2 * t]).then_inc(S["cq_done"], 1)
                act.wait_ge(S["tA_mm"], 2 * t + 1)
                nc.scalar.activation(kT[:, :, toks(t)],
                                     bank(6, 4 * R).rearrange("p (a r) -> p a r", a=4), ACT.Copy)\
                    .then_inc(S["tA_ev"], 1)
                act.wait_ge(S["tA_mm"], 2 * t + 2)
                nc.scalar.activation(dqT[:, :, toks(t)],
                                     bank(6, 4 * R).rearrange("p (a r) -> p a r", a=4), ACT.Copy)\
                    .then_inc(S["tA_ev"], 1)
            act.wait_ge(S["pj_mm"], 4 * NBLK)
            for p in range(4):
                act.wait_ge(S["up_mm"], p + 1)
                nc.scalar.activation(qnT[:, p, :], bank(2 * (p % 2), NTOK), ACT.Copy).then_inc(S["up_ev"], 1)
            for t in range(4):
                act.wait_ge(S["vm_mm"], t + 1)
                nc.scalar.activation(Vm[:, t, :], bank(6 + t % 2), ACT.Copy).then_inc(S["vm_ev"], 1)
            for i in range(24):
                L = P * (i // 8 + 2)
                act.wait_ge(S["ix_mm"], i + 1)
                if i >= 2:
                    act.wait_ge(S["ix_acc"], i - 1)
                nc.scalar.activation(relu[:, i % 2, 0:L], bank(4 + i % 2, L), ACT.Relu)\
                    .then_inc(S["ix_relu"], 1)

            def softmax_exp(i, u):
                R_, L = P, keys_of(u)
                act.wait_ge(S["at_nb"], i + 1)
                if i >= 3:
                    act.wait_ge(S["at_T"], i - 2)
                nc.scalar.activation(Pr[:, i % 3, 0:L], bank(i % 2, L), ACT.Exp, bias=sm[:, 100 + i:101 + i],
                                     scale=scale_of(u), accum_out=sm[:, 200 + i:201 + i])\
                    .then_inc(S["at_exp"], 1)

            def probs_out(i, u):
                L = keys_of(u)
                act.wait_ge(S["at_T"], i + 1)
                if i >= 2:
                    act.wait_ge(S["at_O"], i - 1)
                nc.scalar.activation(PT[:, i % 2, 0:L], bank(2 + i % 2, L), ACT.Copy).then_inc(S["at_PT"], 1)

            def attention(lo, hi):
                for s in range(lo, hi + 2):
                    if s < hi:
                        softmax_exp(s, UNITS[s])
                    if s - 2 >= lo:
                        probs_out(s - 2, UNITS[s - 2])

            attention(0, n_self)
            for i in range(4 * 5):
                n = 512 if i % 5 < 4 else NS
                act.wait_ge(S["xi_mm"], i + 1)
                if i >= 2:
                    act.wait_ge(S["xi_sc"], i - 1)
                nc.scalar.activation(relus[:, i % 2, 0:n], bank(5 + i % 2, n), ACT.Relu)\
                    .then_inc(S["xi_relu"], 1)
            for i in range(NB):
                kind, p = SMP[i]
                act.wait_ge(S["ss_nb"], i + 1)
                if i >= 2:
                    act.wait_ge(S["ss_T"], 5 * (i - 1))
                nc.scalar.activation(Ps[:, i % 2, :], PS[:, 0:NEWC], ACT.Exp, bias=ssm[:, 1, i:i + 1],
                                     scale=(MLA_SCALE, DSA_SCALE)[kind], accum_out=ssm[:, 2, i:i + 1])\
                    .then_inc(S["ss_exp"], 1)
                for c in range(5):
                    n = 512 if c < 4 else 128
                    k = 5 * i + c
                    act.wait_ge(S["ss_T"], k + 1)
                    if k >= 2:
                        act.wait_ge(S["ss_c"], k - 1)
                    pr = P if c < 4 else NS
                    nc.scalar.activation(PTs[0:pr, k % 2, 0:n], bank(5 + k % 2, n, p1=pr), ACT.Copy)\
                        .then_inc(S["ss_PT"], 1)
            norm_scale("mem")
            norm_scale("xmem")
            act.wait_ge(S["mkT_tp"], 1)
            nc.scalar.activation(mkT, bank(6).rearrange("p (a r) -> p a r", a=2), ACT.Copy)\
                .then_inc(S["mkT_ev"], 1)
            for c in range(2):
                act.wait_ge(S["qx_mm"], c + 1)
                nc.scalar.activation(qxT[:, c, :], bank(2 + 2 * c, NTOK), ACT.Copy).then_inc(S["qx_ev"], 1)
            attention(n_self, n_self + n_cross)

        @block.vector
        def _(dve):
            V = nc.vector
            dve.wait_ge(S["cst_in"], 16)
            V.tensor_copy(id16[:], ident).then_inc(S["c16"], 1)
            V.tensor_copy(causal16[:], causal).then_inc(S["c16"], 1)
            V.tensor_copy(same16[:].rearrange("p b c -> p (b c)"), same).then_inc(S["c16"], 1)

            def norm_gain(stage):
                base, n, g = NORM[stage]
                for t in range(n):
                    u, R = base + t, nrows(stage, t)
                    for half in range(2):
                        dve.wait_ge(S["tp_done"], 2 * u + half + 1)
                        gain = gcol[:, g + 4 * half:g + 4 * half + 4].unsqueeze(2).broadcast_to([P, 4, R])
                        V.tensor_tensor(dst_of(stage, t)[:, 4 * half:4 * half + 4, :],
                                        bank(half, 4 * R).rearrange("p (a r) -> p a r", a=4), gain, ALU.mult)\
                            .then_inc(S["xT_done"], 1)

            dve.wait_ge(S["gk_in"], 32)
            norm_gain("mix")
            chain = [0]

            def rope(eng_sem, R, t, x, out, nh, half):
                n = nh * 2 * half
                step = 32 // half
                cc = cosT[0:R, t, :].rearrange("p (a c) -> p a c", a=2)[:, :, 0:32:step]
                ss = sinT[0:R, t, :].rearrange("p (a c) -> p a c", a=2)[:, :, 0:32:step]
                x4 = x.rearrange("p (h a c) -> p h a c", h=nh, a=2)
                A = ropeA[0:R, 0:n].rearrange("p (h a c) -> p h a c", h=nh, a=2)
                M = ropeM[0:R, 0:n].rearrange("p (h a c) -> p h a c", h=nh, a=2)
                for a in range(2):
                    V.tensor_tensor(A[:, :, a, :], x4[:, :, a, :],
                                    cc[:, a, :].unsqueeze(1).broadcast_to([R, nh, half]), ALU.mult)\
                        .then_inc(S[eng_sem], 1)
                    V.tensor_tensor(M[:, :, a, :], x4[:, :, 1 - a, :],
                                    ss[:, a, :].unsqueeze(1).broadcast_to([R, nh, half]), ALU.mult)\
                        .then_inc(S[eng_sem], 1)
                chain[0] += 4
                dve.wait_ge(S[eng_sem], chain[0])
                return V.tensor_tensor(out, ropeA[0:R, 0:n], ropeM[0:R, 0:n], ALU.add)

            for t in range(NBLK):
                R = rows(t)
                for c in (2, 3):
                    dve.wait_ge(S["pj_mm"], 4 * t + c + 1)
                    V.tensor_copy(proj[0:R, t, c * PC:(c + 1) * PC], bank(2 + c, PC, p1=R))\
                        .then_inc(S["pj_dve"], 1)
                dve.wait_ge(S["pj_dve"], 2 * t + 2)
                dve.wait_ge(S["pj_act"], 2 * t + 2)
                for x0, nh, half in ((DQ, 10, 32), (IQ, 8, 32), (IK, 1, 32), (KR, 1, 16)):
                    n = nh * 2 * half
                    last = rope("qr_chain", R, t, proj[0:R, t, x0:x0 + n], proj[0:R, t, x0:x0 + n], nh, half)
                    if x0 != KR:
                        last.then_inc(S["qr_chain"], 1)
                        chain[0] += 1
                        dve.wait_ge(S["qr_chain"], chain[0])
                    else:
                        last.then_inc(S["rp_dve"], 1)
                        dve.wait_ge(S["rp_dve"], t + 1)
                dve.wait_ge(S["rstd2_done"], t + 1)
                V.scalar_tensor_tensor(out=proj[0:R, t, CKV:CKV + 128], in0=proj[0:R, t, CKV:CKV + 128],
                                       scalar=st[0:R, 141 + 2 * t:142 + 2 * t], in1=gkv[0:R, :],
                                       op0=ALU.mult, op1=ALU.mult).then_inc(S["ckv_done"], 1)
                dve.wait_ge(S["tB_mm"], 2 * t + 1)
                gain = gcol[:, 4 * KD:4 * KD + 2].unsqueeze(2).broadcast_to([P, 2, R])
                V.tensor_tensor(cqT[:, :, toks(t)], bank(7, 2 * R).rearrange("p (a r) -> p a r", a=2), gain,
                                ALU.mult).then_inc(S["tB_ev"], 1)
                dve.wait_ge(S["tB_mm"], 2 * t + 2)
                if t < 4:
                    V.tensor_copy(iqT[:, :, toks(t)], bank(7).rearrange("p (a r) -> p a r", a=4))\
                        .then_inc(S["tB_ev"], 1)
                else:
                    for j in range(2):
                        last = V.tensor_copy(iqTs[64 * j:64 * j + 64].rearrange("p b h t -> p h b t"),
                                             bank(7, p1=64).rearrange("p (h b t) -> p h b t", h=8, b=NB))
                    last.then_inc(S["tB_ev"], 1)
            dve.wait_ge(S["tA_ev"], 2 * NBLK)
            dve.wait_ge(S["c16"], 4)
            for g in range(2):
                V.tensor_copy(bdq[64 * g:64 * g + 64, :, g, :, :].rearrange("p b n t -> p n b t"),
                              dqT[64 * g:64 * g + 64, :, SEQ:NTOK].rearrange("p n (b t) -> p n b t", b=NB))
            for hd in range(8):
                dve.wait_ge(S["ql_mm"], hd + 1)
                o = 2 * (hd % 2) * BANK
                V.tensor_copy(qlT[:, hd, :], PS[:, o:o + SEQ]).then_inc(S["ql_ev"], 1)
                V.tensor_copy(qlTs[:, :, hd, :],
                              PS[:, o + SEQ:o + NTOK].rearrange("p (b t) -> p b t", b=NB))\
                    .then_inc(S["ql_ev"], 1)
            for t in range(NBLK):
                R = rows(t)
                dve.wait_ge(S["qr_mm"], t + 1)
                if t >= 1:
                    dve.wait_ge(S["qr_tp"], t)
                rope("qr_chain", R, t, bank(4 + t % 2, 256, p1=R), qr[0:R, :], 8, 16)\
                    .then_inc(S["qr_done"], 1)
                dve.wait_ge(S["qr_done"], t + 1)
                dve.wait_ge(S["qr_tp"], t + 1)
                if t < 4:
                    V.tensor_copy(qrT[:, :, toks(t)], bank(7, 2 * R).rearrange("p (a r) -> p a r", a=2))\
                        .then_inc(S["qr_ev"], 1)
                else:
                    for p in range(NB // 2):
                        last = V.tensor_copy(qrTs[32 * p:32 * p + 32].rearrange("p b (h t) -> p h b t", h=8),
                                             bank(7, p1=32).rearrange("p (h b t) -> p h b t", h=8, b=NB)
                                             [:, :, 2 * p:2 * p + 2, :])
                    last.then_inc(S["qr_ev"], 1)
            last_mask = 0
            V.tensor_copy(mb16[:, 0, 0:P], causal).then_inc(S["mask_done"], 1)
            for i in range(24):
                t, hd = i // 8 + 1, i % 8
                L = P * (t + 1)
                acc = accs[:, t - 1, 0:L]
                iw = proj[:, t, IW + hd:IW + hd + 1]
                dve.wait_ge(S["ix_relu"], i + 1)
                if hd == 0:
                    V.tensor_scalar(acc, relu[:, i % 2, 0:L], iw, None, ALU.mult).then_inc(S["ix_acc"], 1)
                else:
                    dve.wait_ge(S["ix_acc"], i)
                    V.scalar_tensor_tensor(out=acc, in0=relu[:, i % 2, 0:L], scalar=iw, in1=acc,
                                           op0=ALU.mult, op1=ALU.add).then_inc(S["ix_acc"], 1)

            taken = [0]

            def top_k(x, m, k):
                base = taken[0]
                with dve.Fori(0, k // 8) as r:
                    V.max(m, x).then_inc(S["tk"], 1)
                    dve.wait_ge(S["tk"], base + 2 * r + 1)
                    dve.nop(nofuse=True)
                    V.match_replace(x, m, x, TAKEN).then_inc(S["tk"], 1)
                    dve.wait_ge(S["tk"], base + 2 * r + 2)
                    dve.nop(nofuse=True)
                taken[0] += 2 * (k // 8)

            def prompt_top_k(s):
                t, part = s // 8 + 1, s % 8
                L = P * (t + 1)
                acc = accs[:, t - 1, 0:L]
                if part == 0:
                    dve.wait_ge(S["ix_acc"], 8 * t)
                    V.tensor_tensor(acc[:, L - P:L], acc[:, L - P:L], causal, ALU.add).then_inc(S["tk"], 1)
                    taken[0] += 1
                    dve.wait_ge(S["tk"], taken[0])
                for r in range(K_PROMPT // 8 // 8):
                    V.max(m8[:], acc).then_inc(S["tk"], 1)
                    dve.wait_ge(S["tk"], taken[0] + 1)
                    V.match_replace(acc, m8[:], acc, TAKEN).then_inc(S["tk"], 1)
                    dve.wait_ge(S["tk"], taken[0] + 2)
                    taken[0] += 2
                if part == 7:
                    V.tensor_scalar(mb16[:, t, 0:L], acc, -2e38, NEG, ALU.is_ge, ALU.mult)\
                        .then_inc(S["mask_done"], 1)

            def softmax_max(i, u):
                L = keys_of(u)
                dve.wait_ge(S["at_S"], i + 1)
                V.reduce_max(sm[:, i:i + 1], bank(i % 2, L), AX).then_inc(S["at_c"], 1)
                dve.wait_ge(S["at_c"], at_count())
                V.tensor_scalar(sm[:, 100 + i:101 + i], sm[:, i:i + 1], -scale_of(u), None, ALU.mult)\
                    .then_inc(S["at_nb"], 1)

            counts = {"c": 0}

            def at_count():
                counts["c"] += 1
                return counts["c"]

            def softmax_norm(i, u):
                L = keys_of(u)
                dve.wait_ge(S["at_exp"], i + 1)
                V.reciprocal(sm[:, 300 + i:301 + i], sm[:, 200 + i:201 + i]).then_inc(S["at_c"], 1)
                dve.wait_ge(S["at_c"], at_count())
                V.tensor_scalar(Pr[:, i % 3, 0:L], Pr[:, i % 3, 0:L], sm[:, 300 + i:301 + i], None, ALU.mult)\
                    .then_inc(S["at_P"], 1)

            def heads_out(i, u):
                kind, t, hd = u
                dve.wait_ge(S["at_O"], i + 1)
                if kind in ("mla", "dsa"):
                    j, c = (hd % 2, hd // 2) if kind == "mla" else (hd // 4, 4 + hd % 4)
                    V.tensor_copy(xT[64 * j:64 * j + 64, c, toks(t)], bank(4 + i % 2, P, p0=64 * j, p1=64 * j + 64))\
                        .then_inc(S["at_oe"], 1)
                elif kind == "mem":
                    j, c = hd % 2, hd // 2
                    V.tensor_copy(oxT[64 * j:64 * j + 64, c, toks(t)], bank(4 + i % 2, P, p0=64 * j, p1=64 * j + 64))\
                        .then_inc(S["at_oe"], 1)
                else:
                    for c in range(2):
                        for j in range(2):
                            o = PS[64 * j:64 * j + 64, (4 + i % 2) * BANK + c * P:(4 + i % 2) * BANK + (c + 1) * P]
                            o = o.rearrange("p (b n t) -> p b n t", b=4, n=4)[:, :, 2 * c + j, :]
                            d = oxT[64 * j:64 * j + 64, c, SEQ + 32 * hd:SEQ + 32 * hd + 32]
                            last = V.tensor_copy(d.rearrange("p (b t) -> p b t", b=4), o)
                    last.then_inc(S["at_oe"], 1)

            def attention(lo, hi):
                for s in range(lo, hi + 3):
                    if s < hi:
                        softmax_max(s, UNITS[s])
                    if lo <= s - 1 < hi:
                        softmax_norm(s - 1, UNITS[s - 1])
                    if s - 3 >= lo:
                        heads_out(s - 3, UNITS[s - 3])
                    if s < 24:
                        prompt_top_k(s)

            dve.wait_ge(S["tA_ev"], 2 * NBLK)
            attention(0, n_self)

            dve.wait_ge(S["c16"], 4)
            dve.wait_ge(S["out_st"], 16 * 4 * NBLK)
            V.tensor_tensor(selE, same.rearrange("p (b h t) -> p b h t", b=NB, h=8),
                            proj[0:NS, 4, IW:IW + 8].unsqueeze(1).unsqueeze(3).broadcast_to([NS, NB, 8, NQ]),
                            ALU.mult).then_inc(S["sel_E"], 1)
            dve.wait_ge(S["sel_T"], 1)
            V.tensor_copy(Dp[:], bank(7, 256).rearrange("p (a c) -> p a c", a=4)).then_inc(S["sel_D"], 1)
            dve.wait_ge(S["xi_sc"], 20)
            V.tensor_copy(sw[:, 0:PAST], PS[0:NS, 0:PAST]).then_inc(S["sw_done"], 1)
            V.tensor_tensor(sw[:, PAST:NEWC], PS[0:NS, PAST:NEWC], cst[0:NS, C_NEW:C_NEW + NS], ALU.add)\
                .then_inc(S["sw_done"], 1)
            dve.wait_ge(S["sw_done"], 2)

            def own_values(i):
                kind, p = SMP[i]
                if kind == 0:
                    V.tensor_copy(olT[:, 2 * p:2 * p + 2, :, :].rearrange("p b h t -> p (b h t)"), bank(7, P))\
                        .then_inc(S["ss_oe"], 1)
                else:
                    for g in range(2):
                        for b2 in range(2):
                            o = bank(7, 64, 64 * b2, p0=64 * g, p1=64 * g + 64)
                            o = o.rearrange("p (g n t) -> p g n t", g=2, n=4)[:, g, :, :]
                            c0 = SEQ + NQ * (2 * p + b2)
                            last = V.tensor_copy(xT[64 * g:64 * g + 64, 4:8, c0:c0 + NQ], o)
                    last.then_inc(S["ss_oe"], 1)

            def rounds(n):
                top_k(sw, m8[0:NS, :], 8 * n)

            before, exp_time = 3, 1
            rest = K_SAMPLE // 8 - before
            for i in range(NB):
                kind, p = SMP[i]
                if i == 0:
                    rounds(before)
                if i == NB // 2:
                    dve.wait_ge(S["qr_ev"], NBLK)
                    V.tensor_scalar(mbs, sw, -2e38, NEG, ALU.is_ge, ALU.mult).then_inc(S["mbs_done"], 1)
                dve.wait_ge(S["ss_S"], i + 1)
                V.reduce_max(ssm[:, 0, i:i + 1], PS[:, 0:NEWC], AX).then_inc(S["ss_P"], 1)
                dve.wait_ge(S["ss_P"], 3 * i + 1)
                V.tensor_scalar(ssm[:, 1, i:i + 1], ssm[:, 0, i:i + 1], -(MLA_SCALE, DSA_SCALE)[kind],
                                None, ALU.mult).then_inc(S["ss_nb"], 1)
                if kind == 0:
                    rounds(exp_time)
                    rest -= exp_time
                elif i >= 1:
                    dve.wait_ge(S["ss_c"], 5 * i)
                    own_values(i - 1)
                dve.wait_ge(S["ss_exp"], i + 1)
                V.reciprocal(ssm[:, 3, i:i + 1], ssm[:, 2, i:i + 1])\
                    .then_inc(S["ss_P"], 1)
                dve.wait_ge(S["ss_P"], 3 * i + 2)
                V.tensor_scalar(Ps[:, i % 2, :], Ps[:, i % 2, :], ssm[:, 3, i:i + 1], None, ALU.mult)\
                    .then_inc(S["ss_P"], 1)
                if kind == 0:
                    if i >= 1:
                        dve.wait_ge(S["ss_c"], 5 * i)
                        own_values(i - 1)
                    n = rest // (NB // 2 - i)
                    rounds(n)
                    rest -= n
            dve.wait_ge(S["ss_c"], 5 * NB)
            own_values(NB - 1)
            for hd in range(8):
                j, c = hd % 2, hd // 2
                dve.wait_ge(S["uv_mm"], 1)
                V.tensor_copy(xT[64 * j:64 * j + 64, c, SEQ:NTOK], bank(5 + j, NS, NS * c, p0=64 * j, p1=64 * j + 64))\
                    .then_inc(S["uv_ev"], 1)
            for i in range(2 * NBLK):
                t, half = divmod(i, 2)
                R = rows(t)
                dve.wait_ge(S["wo_mm"], i + 1)
                hs = h[0:R, t, 512 * half:512 * half + 512]
                V.tensor_tensor(hs, bank(2 + i % 2, p1=R), hs, ALU.add).then_inc(S["h_done"], 1)
            norm_gain("mem")
            for t in range(2):
                dve.wait_ge(S["mkv_mm"], t + 1)
                V.tensor_copy(mkv[:, t, :], bank(4 + t)).then_inc(S["mkv_ev"], 1)
            norm_gain("xmem")
            V.memset(bdx, 0.0).then_inc(S["bdx_done"], 1)
            dve.wait_ge(S["bdx_done"], 1)
            dve.wait_ge(S["qx_ev"], 2)
            for c in range(2):
                for j in range(2):
                    V.tensor_copy(bdx[64 * j:64 * j + 64, c, :, 2 * c + j, :],
                                  qxT[64 * j:64 * j + 64, c, SEQ:NTOK].rearrange("p (b t) -> p b t", b=NB))\
                        .then_inc(S["bdx_done"], 1)
            attention(n_self, n_self + n_cross)
            for i in range(2 * NBLK):
                t, half = divmod(i, 2)
                R = rows(t)
                dve.wait_ge(S["ox_mm"], i + 1)
                hs = h[0:R, t, 512 * half:512 * half + 512]
                V.tensor_tensor(hs, bank(i % 2, p1=R), hs, ALU.add).then_inc(S["hx_done"], 1)
            dve.wait_ge(S["hx_done"], 2 * NBLK)

        @block.tensor
        def _(pe):
            M = nc.tensor.matmul
            TR = nc.tensor.transpose

            def norm_transpose(stage):
                base, n, _ = NORM[stage]
                for t in range(n):
                    u, R = base + t, nrows(stage, t)
                    pe.wait_ge(S["xs_done"], u + 1)
                    for half in range(2):
                        if u >= 1:
                            pe.wait_ge(S["xT_done"], 2 * (u - 1) + half + 1)
                        for a in range(4):
                            c = 4 * half + a
                            last = TR(bank(half, R, a * R), xs[0:R, u % 2, c * P:(c + 1) * P], ident[0:R, 0:R])
                        last.then_inc(S["tp_done"], 1)

            pe.wait_ge(S["cst_in"], 16)
            norm_transpose("mix")
            pe.wait_ge(S["win_in"], 16 * KD)

            def project(t):
                R = rows(t)
                pe.wait_ge(S["xT_done"], 2 * (t + 1))
                for c in range(4):
                    if t >= 1:
                        pe.wait_ge(S["pj_act"] if c < 2 else S["pj_dve"], 2 * (t - 1) + c % 2 + 1)
                    for k in range(KD):
                        last = M(bank(2 + c, PC, p1=R), xT[:, k, toks(t)], win[:, k, c * PC:(c + 1) * PC],
                                 start=(k == 0), stop=(k == KD - 1))
                    last.then_inc(S["pj_mm"], 1)

            def transposes(t):
                R = rows(t)
                I = ident[0:R, 0:R]
                pe.wait_ge(S["ckv_done"], t + 1)
                pe.wait_ge(S["rp_pool"], t + 1)
                if t >= 1:
                    pe.wait_ge(S["tA_ev"], 2 * t)
                for a, src in enumerate((proj[0:R, t, CKV:CKV + P], kk[0:R, 0:128],
                                         proj[0:R, t, DK:DK + P], kk[0:R, 128:256])):
                    last = TR(bank(6, R, a * R), src, I)
                last.then_inc(S["tA_mm"], 1)
                pe.wait_ge(S["cq_done"], t + 1)
                if t >= 1:
                    pe.wait_ge(S["tB_ev"], 2 * t)
                for a in range(2):
                    last = TR(bank(7, R, a * R), proj[0:R, t, CQ + a * P:CQ + (a + 1) * P], I)
                last.then_inc(S["tB_mm"], 1)
                pe.wait_ge(S["tA_ev"], 2 * t + 1)
                for a in range(4):
                    last = TR(bank(6, R, a * R), proj[0:R, t, DQ + a * P:DQ + (a + 1) * P], I)
                last.then_inc(S["tA_mm"], 1)
                pe.wait_ge(S["tB_ev"], 2 * t + 1)
                if t < 4:
                    for a in range(4):
                        last = TR(bank(7, R, a * R), proj[0:R, t, IQ + a * P:IQ + (a + 1) * P], I)
                else:
                    for a in range(8):
                        last = TR(bank(7, R, a * R, p1=64), proj[0:R, t, IQ + a * 64:IQ + (a + 1) * 64], I)
                last.then_inc(S["tB_mm"], 1)

            for t in range(NBLK + 1):
                if t < NBLK:
                    project(t)
                if t >= 1:
                    transposes(t - 1)
            pe.wait_ge(S["wsm_in"], 64)
            pe.wait_ge(S["tB_ev"], 2 * NBLK)
            pe.wait_ge(S["pj_act"], 2 * NBLK)
            pe.wait_ge(S["pj_dve"], 2 * NBLK)
            for p in range(4):
                if p >= 2:
                    pe.wait_ge(S["up_ev"], p - 1)
                for lo, hi in ((0, SEQ), (SEQ, NTOK)):
                    for c in range(2):
                        o = 2 * (p % 2) * BANK
                        last = M(PS[:, o + lo:o + hi], w_uqn[:, c, p * P:(p + 1) * P], cqT[:, c, lo:hi],
                                 start=(c == 0), stop=(c == 1))
                last.then_inc(S["up_mm"], 1)
            for hd in range(8):
                j, p = hd % 2, hd // 2
                pe.wait_ge(S["up_ev"], 4)
                if hd >= 2:
                    pe.wait_ge(S["ql_ev"], 2 * (hd - 1))
                for lo, hi in ((0, SEQ), (SEQ, NTOK)):
                    o = 2 * (hd % 2) * BANK
                    last = M(PS[:, o + lo:o + hi], w_ukT[64 * j:64 * j + 64, p, :],
                             qnT[64 * j:64 * j + 64, p, lo:hi], start=True, stop=True)
                last.then_inc(S["ql_mm"], 1)
            for t in range(NBLK):
                R = rows(t)
                if t >= 2:
                    pe.wait_ge(S["qr_done"], t - 1)
                for c in range(2):
                    last = M(bank(4 + t % 2, 256, p1=R), cqT[:, c, toks(t)], w_uqr[:, c, :],
                             start=(c == 0), stop=(c == 1))
                last.then_inc(S["qr_mm"], 1)
                pe.wait_ge(S["qr_done"], t + 1)
                if t >= 1:
                    pe.wait_ge(S["qr_ev"], t)
                I = ident[0:R, 0:R]
                if t < 4:
                    for a in range(2):
                        last = TR(bank(7, R, a * R), qr[0:R, a * P:(a + 1) * P], I)
                else:
                    for a in range(8):
                        last = TR(bank(7, R, a * R, p1=32), qr[0:R, a * 32:(a + 1) * 32], I)
                last.then_inc(S["qr_tp"], 1)
            pe.wait_ge(S["qr_ev"], NBLK)
            pe.wait_ge(S["tA_ev"], 2 * NBLK)
            for t in range(4):
                if t >= 2:
                    pe.wait_ge(S["vm_ev"], t - 1)
                M(bank(6 + t % 2), kT[:, 0, toks(t)], w_uv, start=True, stop=True).then_inc(S["vm_mm"], 1)
            for i in range(24):
                t, hd = i // 8 + 1, i % 8
                L, j, p = P * (t + 1), hd % 2, hd // 2
                if i >= 2:
                    pe.wait_ge(S["ix_relu"], i - 1)
                M(bank(4 + i % 2, L), iqT[64 * j:64 * j + 64, p, toks(t)], kT[64 * j:64 * j + 64, 3, 0:L],
                  start=True, stop=True).then_inc(S["ix_mm"], 1)

            def scores(i, u):
                kind, t, hd = u
                L = keys_of(u)
                if i >= 2:
                    pe.wait_ge(S["at_exp"], i - 1)
                b = i % 2
                if kind == "mla":
                    r, c = hd % 4, hd // 4
                    M(bank(b, L), qlT[:, hd, toks(t)], kT[:, 0, 0:L], start=True, stop=False)
                    M(bank(b, L), qrT[32 * r:32 * r + 32, c, toks(t)], kT[32 * r:32 * r + 32, 1, 0:L],
                      start=False, stop=False)
                    last = M(bank(b, P, L - P), id16[:], causal16[:], start=False, stop=True)
                elif kind == "dsa":
                    g, n = hd // 4, hd % 4
                    pe.wait_ge(S["mask_done"], t + 1)
                    M(bank(b, L), dqT[64 * g:64 * g + 64, n, toks(t)], kT[64 * g:64 * g + 64, 2, 0:L],
                      start=True, stop=False)
                    last = M(bank(b, L), id16[:], mb16[:, t, 0:L], start=False, stop=True)
                elif kind == "mem":
                    j, c = hd % 2, hd // 2
                    last = M(bank(b, L), qxT[64 * j:64 * j + 64, c, toks(t)], mkT[64 * j:64 * j + 64, c, :],
                             start=True, stop=True)
                else:
                    for b4 in range(4):
                        bb = 4 * hd + b4
                        for c in range(2):
                            last = M(bank(b, L, p0=32 * b4, p1=32 * b4 + 32),
                                     bdx[:, c, bb, :, :].rearrange("p n t -> p (n t)"), xc[:, bb, c, :],
                                     start=(c == 0), stop=(c == 1))
                last.then_inc(S["at_S"], 1)

            def turn_probs(i, u):
                L = keys_of(u)
                pe.wait_ge(S["at_P"], i + 1)
                if i >= 2:
                    pe.wait_ge(S["at_PT"], i - 1)
                for a in range(L // P):
                    last = TR(bank(2 + i % 2, P, a * P), Pr[:, i % 3, a * P:(a + 1) * P], ident)
                last.then_inc(S["at_T"], 1)

            def values(i, u):
                kind, t, hd = u
                L = keys_of(u)
                nk = L // P
                pe.wait_ge(S["at_PT"], i + 1)
                if i >= 2:
                    pe.wait_ge(S["at_oe"], i - 1)
                if kind == "smp":
                    for b4 in range(4):
                        bb = 4 * hd + b4
                        for c in range(2):
                            for k in range(2):
                                last = M(bank(4 + i % 2, 32, c * P + 32 * b4), xc[:, bb, 2 + k, c * P:(c + 1) * P],
                                         PT[:, i % 2, k * P + 32 * b4:k * P + 32 * b4 + 32],
                                         start=(k == 0), stop=(k == 1))
                    last.then_inc(S["at_O"], 1)
                    return
                j = hd // 4 if kind == "dsa" else hd % 2
                for k in range(nk):
                    if kind == "mla":
                        v = Vm[:, k, hd * 64:hd * 64 + 64]
                    elif kind == "dsa":
                        v = proj[:, k, DV + 64 * j:DV + 64 * j + 64]
                    else:
                        v = mkv[:, k, 256 + 64 * hd:256 + 64 * hd + 64]
                    last = M(bank(4 + i % 2, P, p0=64 * j, p1=64 * j + 64), v, PT[:, i % 2, k * P:(k + 1) * P],
                             start=(k == 0), stop=(k == nk - 1))
                last.then_inc(S["at_O"], 1)

            def attention(lo, hi):
                for s in range(lo, hi + 3):
                    if s < hi:
                        scores(s, UNITS[s])
                    if lo <= s - 2 < hi:
                        turn_probs(s - 2, UNITS[s - 2])
                    if s - 3 >= lo:
                        values(s - 3, UNITS[s - 3])

            pe.wait_ge(S["vm_ev"], 4)
            pe.wait_ge(S["c16"], 4)
            pe.wait_ge(S["ix_relu"], 24)
            pe.wait_ge(S["ql_ev"], 16)
            attention(0, n_self)

            pe.wait_ge(S["sel_E"], 1)
            for p in range(4):
                last = TR(bank(7, NS, p * NS), selE[:, 2 * p:2 * p + 2, :, :].rearrange("p b h t -> p (b h t)"),
                          ident[0:NS, 0:NS])
            last.then_inc(S["sel_T"], 1)
            pe.wait_ge(S["sel_D"], 1)
            pe.wait_ge(S["at_oe"], n_self)
            pe.wait_ge(S["at_PT"], n_self)

            def head_sum(i):
                p, kc = divmod(i, 5)
                n = 512 if kc < 4 else NS
                pe.wait_ge(S["xi_relu"], i + 1)
                M(bank(kc, n, p1=NS), Dp[:, p, :], relus[:, i % 2, 0:n], start=(p == 0), stop=(p == 3),
                  skip_group_check=True).then_inc(S["xi_sc"], 1)

            pe.wait_ge(ik_sp, 16 * NB * IK_SP)
            pe.wait_ge(ik_pool, 16 * NB * (NPAGE - IK_SP))
            for i in range(20):
                p, kc = divmod(i, 5)
                n = 512 if kc < 4 else NS
                if i >= 2:
                    pe.wait_ge(S["xi_relu"], i - 1)
                for b2 in range(2):
                    H = slice(64 * b2, 64 * b2 + 64)
                    q = iqTs[H, 2 * p + b2, :, :].rearrange("p h t -> p (h t)")
                    k = ikT[H, p, kc * 512:kc * 512 + 512] if kc < 4 else kT[H, 3, SEQ:NTOK]
                    last = M(bank(5 + i % 2, n, p0=64 * b2, p1=64 * b2 + 64), q, k, start=True, stop=True)
                last.then_inc(S["xi_mm"], 1)
                if i >= 1:
                    head_sum(i - 1)
            head_sum(19)

            def pair_scores(i):
                kind, p = SMP[i]
                slot = (i + 1) % 2
                pe.wait_ge(kv_sp[slot], 16 * NPAGE * (2 * (i // 2 + 1) if kind == 0 else 4 + (i // 2 - 1)))
                if kind == 0:
                    pe.wait_ge(kr_in[p], 16 * 2 * NPAGE)
                else:
                    pe.wait_ge(kv_pool[slot], 16 * NPAGE * (i // 2 - 1))
                if i >= 1:
                    pe.wait_ge(S["ss_exp"], i)
                else:
                    pe.wait_ge(S["sw_done"], 2)
                if kind == 1:
                    pe.wait_ge(S["mbs_done"], 1)
                for b2 in range(2):
                    b = 2 * p + b2
                    for kc in range(5):
                        n = 512 if kc < 4 else NS
                        out = bank(kc, n, p0=64 * b2, p1=64 * b2 + 64)
                        if kind == 0:
                            ql = qlTs[:, b, :, :].rearrange("p h t -> p (h t)")
                            for a in range(4 if kc < 4 else 1):
                                if kc < 4:
                                    o = bank(kc, PAGE, a * PAGE, p0=64 * b2, p1=64 * b2 + 64)
                                    k = KV[:, slot, b2, 4 * kc + a, 0:128]
                                else:
                                    o, k = out, kT[:, 0, SEQ:NTOK]
                                M(o, ql, k, start=(a == 0), stop=False, skip_group_check=True)
                            G = slice(32 * p, 32 * p + 32)
                            k = krT[G, b2, kc * 512:kc * 512 + 512] if kc < 4 else kT[G, 1, SEQ:NTOK]
                            last = M(out, qrTs[G, b2, :], k, start=False, stop=(kc < 4), skip_group_check=True)
                            if kc == 4:
                                last = M(out, same[:, 64 * b:64 * b + 64], cst[0:NS, C_NEW:C_NEW + NS],
                                         start=False, stop=True, skip_group_check=True)
                        else:
                            q = bdq[:, b, :, :, :].rearrange("p g n t -> p (g n t)")
                            for a in range(4 if kc < 4 else 1):
                                if kc < 4:
                                    o = bank(kc, PAGE, a * PAGE, p0=64 * b2, p1=64 * b2 + 64)
                                    k = KV[:, slot, b2, 4 * kc + a, 0:128]
                                else:
                                    o, k = out, kT[:, 2, SEQ:NTOK]
                                M(o, q, k, start=(a == 0), stop=False, skip_group_check=True)
                            last = M(out, same16[:, b, :], mbs[:, kc * 512:kc * 512 + n], start=False, stop=True,
                                     skip_group_check=True)
                last.then_inc(S["ss_S"], 1)

            def turn_pair(i, c):
                k = 5 * i + c
                pe.wait_ge(S["ss_P"], 3 * i + 3)
                if k >= 2:
                    pe.wait_ge(S["ss_PT"], k - 1)
                if c < 4:
                    for a in range(4):
                        c0 = 512 * c + a * P
                        last = TR(bank(5 + k % 2, P, a * P), Ps[:, i % 2, c0:c0 + P], ident)
                else:
                    last = TR(bank(5 + k % 2, P, 0, p1=NS), Ps[:, i % 2, PAST:NEWC], ident)
                last.then_inc(S["ss_T"], 1)

            def pair_values(i, c):
                kind, p = SMP[i]
                k = 5 * i + c
                pe.wait_ge(S["ss_PT"], k + 1)
                if c == 0 and i >= 1:
                    pe.wait_ge(S["ss_oe"], i)
                for b2 in range(2):
                    out = bank(7, 64, 64 * b2)
                    first = (c == 0)
                    if c < 4:
                        for a in range(4):
                            v = KV[:, (i + 1) % 2, b2, 4 * c + a, 128:256]
                            last = M(out, v, PTs[:, k % 2, a * P + 64 * b2:a * P + 64 * b2 + 64],
                                     start=(first and a == 0 and b2 == 0), stop=False, skip_group_check=True)
                    else:
                        v = proj[0:NS, 4, (CKV, DV)[kind]:(CKV, DV)[kind] + P]
                        last = M(out, v, PTs[0:NS, k % 2, 64 * b2:64 * b2 + 64], start=False, stop=(b2 == 1),
                                 skip_group_check=True)
                last.then_inc(S["ss_c"], 1)

            for i in range(NB):
                pair_scores(i)
                for c in range(6):
                    if c < 5:
                        turn_pair(i, c)
                    if c >= 1:
                        pair_values(i, c - 1)
            pe.wait_ge(S["ss_oe"], NB)
            for hd in range(8):
                j, c = hd % 2, hd // 2
                last = M(bank(5 + j, NS, NS * c, p0=64 * j, p1=64 * j + 64), w_uv[:, hd * 64:hd * 64 + 64],
                         olT[:, :, hd, :], start=True, stop=True, skip_group_check=True)
            last.then_inc(S["uv_mm"], 1)
            pe.wait_ge(S["uv_ev"], 8)
            pe.wait_ge(S["wo_in"], 16)
            for i in range(2 * NBLK):
                t, half = divmod(i, 2)
                R = rows(t)
                if i >= 2:
                    pe.wait_ge(S["h_done"], i - 1)
                for k in range(KD):
                    last = M(bank(2 + i % 2, p1=R), xT[:, k, toks(t)], w_o[:, k, 512 * half:512 * half + 512],
                             start=(k == 0), stop=(k == KD - 1))
                last.then_inc(S["wo_mm"], 1)
            norm_transpose("mem")
            pe.wait_ge(S["late_in"], 48)
            for t in range(2):
                pe.wait_ge(S["xT_done"], 2 * (NORM["mem"][0] + t + 1))
                for k in range(KD):
                    last = M(bank(4 + t), mT[:, k, t * P:(t + 1) * P], wkv[:, k, :], start=(k == 0),
                             stop=(k == KD - 1))
                last.then_inc(S["mkv_mm"], 1)
            norm_transpose("xmem")
            pe.wait_ge(S["mkv_ev"], 2)
            for c in range(2):
                for t in range(2):
                    last = TR(bank(6, P, c * 256 + t * P), mkv[:, t, c * P:(c + 1) * P], ident)
            last.then_inc(S["mkT_tp"], 1)
            pe.wait_ge(S["xT_done"], 2 * STREAM_UNITS)
            for c in range(2):
                for lo, hi in ((0, SEQ), (SEQ, NTOK)):
                    for k in range(KD):
                        o = (2 + 2 * c) * BANK
                        last = M(PS[:, o + lo:o + hi], wqx[:, k, c * P:(c + 1) * P], xT[:, k, lo:hi],
                                 start=(k == 0), stop=(k == KD - 1))
                last.then_inc(S["qx_mm"], 1)
            pe.wait_ge(S["mkT_ev"], 1)
            pe.wait_ge(S["qx_ev"], 2)
            pe.wait_ge(S["bdx_done"], 5)
            attention(n_self, n_self + n_cross)
            pe.wait_ge(S["wox_in"], 16)
            pe.wait_ge(S["at_oe"], n_self + n_cross)
            for i in range(2 * NBLK):
                t, half = divmod(i, 2)
                R = rows(t)
                if i >= 2:
                    pe.wait_ge(S["hx_done"], i - 1)
                for c in range(2):
                    last = M(bank(i % 2, p1=R), oxT[:, c, toks(t)], wox[:, c, 512 * half:512 * half + 512],
                             start=(c == 0), stop=(c == 1))
                last.then_inc(S["ox_mm"], 1)


def peer_select(nc, T, h, sems, xh, xl, IT, JT, cT):
    ctx = ExitStack()
    with ctx:
        def sb(name, shape, dt=F32):
            return ctx.enter_context(nc.sbuf_tensor(name, shape, dt))

        PS = ctx.enter_context(nc.psum_tensor("psB", [P, 8 * BANK], F32))

        def bank(b, n=BANK, at=0, p0=0, p1=P):
            return PS[p0:p1, b * BANK + at:b * BANK + at + n]

        cst = sb("cstB", [P, 256])
        cst2 = sb("cst2B", [P, 2 * PK])
        gcol = sb("gcolB", [P, KD])
        st = sb("stB", [P, 20])
        xs = sb("xsB", [P, 2, D])
        xf = sb("xfB", [P, 2, 4, P])
        keysT = sb("keysT", [P, 2 * PH, NKEY])
        wraw = sb("wraw", [P, 2, D])
        wh = sb("wh", [P, 2, D], F32R)
        wl = sb("wl", [P, 2, D], F32R)
        qT = sb("qT", [P, 2, NTOK])
        sc = sb("sc", [P, NBLK, 2 * PH, NKEY])
        mv = sb("mv", [P, NBLK, 2 * PH, PK])
        mi = sb("mi", [P, NBLK, 2 * PH, PK], U32)
        mf = sb("mf", [P, 2 * PH, PK])
        dI = sb("dI", [P, PH, PK])
        cand = sb("cand", [P, PH, NCAND])
        gv = sb("gv", [P, PH, PK])
        gi = sb("gi", [P, PH, PK], U32)
        gf = sb("gfB", [P, 2, PH * PK])
        off = sb("offB", [P, PH * PK])
        reached = sb("reached", [P, PH, PK, PK])
        hit = sb("hit", [P, PH, PK, PK])
        hit2 = sb("hit2", [P, PH, PK, PK])
        sel = sb("selB", [P, 3, PH * PK])
        gs = sb("gsB", [P, 2, PH])
        ident = cst[:, 0:P]
        iota16 = cst[:, P:P + PK]
        row0, step = cst2[:, 0:PK], cst2[:, PK:2 * PK]

        names = """cst_in key_in sq_done ms_done rstd_done xs_done tp_done xf_done xh_done xl_done
            wh_done wl_done q_mm q_ev s_mm s_ev tk ex_in ex_done sel_done sT_mm sT_act""".split()
        S = {n: sems.enter_context(nc.semaphore("b_" + n)) for n in names}
        w_in = [sems.enter_context(nc.semaphore(f"b_w_in{i}")) for i in range(2)]
        NHP = 2 * PH
        block = ctx.enter_context(nc.Block())

        @block.sync
        def _(sp):
            sp.dma_start(cst[:], T["cst"][:, 0:256]).then_inc(S["cst_in"], 16)
            sp.dma_start(cst2[:], T["cst"][:, C_FIRST:C_FIRST + 2 * PK]).then_inc(S["cst_in"], 16)
            sp.dma_start(gcol[:], T["gcol"][:, 3 * KD:4 * KD]).then_inc(S["cst_in"], 16)
            sp.dma_start(keysT[:], T["keysT"]).then_inc(S["key_in"], 16)
            for u in range(NHP):
                if u >= 2:
                    sp.wait_ge(S["wl_done"], u - 1)
                sp.dma_start(wraw[:, u % 2, :], T["w_pq"][u]).then_inc(w_in[u % 2], 16)

        @block.gpsimd
        def _(pool):
            pool.memset(st[:, 19:20], -0.5).then_inc(S["ms_done"], 1)
            for t in range(NBLK):
                R = rows(t)
                pool.wait_ge(S["sq_done"], t + 1)
                nc.gpsimd.tensor_scalar(st[0:R, 5 + t:6 + t], st[0:R, t:t + 1], 1.0 / D, EPS, ALU.mult, ALU.add)\
                    .then_inc(S["ms_done"], 1)
                pool.wait_ge(S["ms_done"], t + 2)
                nc.gpsimd.tensor_tensor(st[0:R, 10 + t:11 + t], st[0:R, 5 + t:6 + t], st[0:R, 19:20], ALU.pow)\
                    .then_inc(S["rstd_done"], 1)

        @block.scalar
        def _(act):
            A = nc.scalar.activation

            def square(t):
                R = rows(t)
                if t >= 2:
                    act.wait_ge(S["tp_done"], 2 * (t - 1))
                A(xs[0:R, t % 2, :], h[0:R, t, :], ACT.Square, accum_out=st[0:R, t:t + 1])\
                    .then_inc(S["sq_done"], 1)

            square(0)
            for t in range(NBLK):
                R = rows(t)
                if t + 1 < NBLK:
                    square(t + 1)
                act.wait_ge(S["rstd_done"], t + 1)
                A(xs[0:R, t % 2, :], h[0:R, t, :], ACT.Copy, scale=st[0:R, 10 + t:11 + t])\
                    .then_inc(S["xs_done"], 1)
                if t >= 1:
                    for half in range(2):
                        act.wait_ge(S["xf_done"], 2 * (t - 1) + half + 1)
                        A(xh[:, 4 * half:4 * half + 4, toks(t - 1)], xf[:, half, :, 0:P], ACT.Copy)\
                            .then_inc(S["xh_done"], 1)
            for half in range(2):
                act.wait_ge(S["xf_done"], 2 * (NBLK - 1) + half + 1)
                A(xh[:, 4 * half:4 * half + 4, toks(NBLK - 1)], xf[:, half, :, 0:NS], ACT.Copy)\
                    .then_inc(S["xh_done"], 1)
            for u in range(NHP + 2):
                if u < NHP:
                    act.wait_ge(w_in[u % 2], 16 * (u // 2 + 1))
                    if u >= 2:
                        act.wait_ge(S["q_mm"], u - 1)
                    A(wh[:, u % 2, :], wraw[:, u % 2, :], ACT.Copy).then_inc(S["wh_done"], 1)
                v = u - 1
                if 0 <= v < NHP:
                    act.wait_ge(S["q_mm"], v + 1)
                    if v >= 2:
                        act.wait_ge(S["s_mm"], v - 1)
                    A(qT[:, v % 2, :], bank(2 + 2 * (v % 2), NTOK), ACT.Copy).then_inc(S["q_ev"], 1)
                v = u - 2
                if v >= 0:
                    act.wait_ge(S["s_mm"], v + 1)
                    A(sc[:, 0:4, v, :], bank(6).rearrange("p (t k) -> p t k", t=4), ACT.Copy)\
                        .then_inc(S["s_ev"], 1)
                    A(sc[0:NS, 4, v, :], bank(7, P, p1=NS), ACT.Copy).then_inc(S["s_ev"], 1)
            for t in range(NBLK):
                R = rows(t)
                act.wait_ge(S["ex_in"], t + 1)
                A(sel[0:R, 2, :], sel[0:R, 2, :], ACT.Exp).then_inc(S["ex_done"], 1)
                act.wait_ge(S["sT_mm"], t + 1)
                A(IT[:, toks(t)], bank(0, R), ACT.Copy).then_inc(S["sT_act"], 1)
                A(JT[:, toks(t)], bank(0, R, P), ACT.Copy).then_inc(S["sT_act"], 1)
                A(cT[:, toks(t)], bank(1, R), ACT.Copy).then_inc(S["sT_act"], 1)

        @block.vector
        def _(dve):
            V = nc.vector
            dve.wait_ge(S["cst_in"], 48)

            def low(t, half):
                R = rows(t)
                dve.wait_ge(S["xh_done"], 2 * t + half + 1)
                dst = (slice(None), slice(4 * half, 4 * half + 4), toks(t))
                V.tensor_tensor(xl[dst], xf[:, half, :, 0:R], xh[dst].bitcast(F32), ALU.subtract)\
                    .then_inc(S["xl_done"], 1)

            for t in range(NBLK):
                R = rows(t)
                for half in range(2):
                    if t >= 1:
                        low(t - 1, half)
                        dve.wait_ge(S["xl_done"], 2 * (t - 1) + half + 1)
                    dve.wait_ge(S["tp_done"], 2 * t + half + 1)
                    V.tensor_tensor(xf[:, half, :, 0:R], bank(half, 4 * R).rearrange("p (a r) -> p a r", a=4),
                                    gcol[:, 4 * half:4 * half + 4].unsqueeze(2).broadcast_to([P, 4, R]), ALU.mult)\
                        .then_inc(S["xf_done"], 1)
            for half in range(2):
                low(NBLK - 1, half)
            done = [0]

            def then(ins):
                ins.then_inc(S["tk"], 1)
                done[0] += 1
                dve.wait_ge(S["tk"], done[0])

            def top16(xs_):
                for first in range(2):
                    w = slice(8 * first, 8 * first + 8)
                    for x, val, idx in xs_:
                        last = V.max(val[:, w], x)
                    then(last)
                    for x, val, idx in xs_:
                        last = V.max_index(idx[:, w], val[:, w], x)
                    then(last)
                    if first == 0:
                        for x, val, idx in xs_:
                            last = V.match_replace(x, val[:, w], x, TAKEN)
                        then(last)

            for u in range(NHP + 2):
                if u < NHP:
                    dve.wait_ge(S["wh_done"], u + 1)
                    V.tensor_tensor(wl[:, u % 2, :], wraw[:, u % 2, :], wh[:, u % 2, :].bitcast(F32), ALU.subtract)\
                        .then_inc(S["wl_done"], 1)
                if u >= 2:
                    v = u - 2
                    dve.wait_ge(S["s_ev"], 2 * (v + 1))
                    top16([(sc[0:rows(t), t, v, :], mv[0:rows(t), t, v, :], mi[0:rows(t), t, v, :])
                           for t in range(NBLK)])

            for t in range(NBLK):
                R = rows(t)
                V.tensor_copy(mf[0:R], mi[0:R, t])
                m4 = mv[0:R, t].rearrange("p (h a) k -> p h a k", a=2)
                f4 = mf[0:R].rearrange("p (h a) k -> p h a k", a=2)
                for a, n, at in ROWS16[:8]:
                    V.tensor_tensor(cand[0:R, :, at:at + n], m4[:, :, 0, a:a + 1].broadcast_to([R, PH, n]),
                                    m4[:, :, 1, 0:n], ALU.add)
                then(V.tensor_tensor(cand[0:R, :, NCAND - 8:NCAND], m4[:, :, 0, 8:16],
                                     m4[:, :, 1, 0:1].broadcast_to([R, PH, 8]), ALU.add))
                V.tensor_copy(dI[0:R, :, 0:1], f4[:, :, 0, 0:1])
                V.tensor_tensor(dI[0:R, :, 1:PK], f4[:, :, 0, 1:PK], f4[:, :, 0, 0:PK - 1], ALU.subtract)
                top16([(cand[0:R, k, :], gv[0:R, k, :], gi[0:R, k, :]) for k in range(PH)])
                if t >= 1:
                    dve.wait_ge(S["sT_mm"], t)
                g3 = sel[0:R, 2, :].rearrange("p (h k) -> p h k", h=PH)
                V.tensor_tensor(g3, gv[0:R], gv[0:R, :, 0:1].broadcast_to([R, PH, PK]), ALU.subtract)\
                    .then_inc(S["ex_in"], 1)
                then(V.tensor_copy(gf[0:R, 0, :], gi[0:R].rearrange("p h k -> p (h k)")))
                flat = "p h k c -> p (h k) c"
                then(V.tensor_tensor(reached[0:R].rearrange(flat),
                                     gf[0:R, 0, :].unsqueeze(2).broadcast_to([R, PH * PK, PK]),
                                     row0.unsqueeze(1).broadcast_to([P, PH * PK, PK])[0:R], ALU.is_ge))
                V.tensor_tensor(hit[0:R], reached[0:R], dI[0:R].unsqueeze(2).broadcast_to([R, PH, PK, PK]),
                                ALU.mult)
                then(V.tensor_tensor(hit2[0:R].rearrange(flat), reached[0:R].rearrange(flat),
                                     step.unsqueeze(1).broadcast_to([P, PH * PK, PK])[0:R], ALU.mult))
                V.reduce_sum(sel[0:R, 0, :], hit[0:R].rearrange(flat), AX)
                then(V.reduce_sum(off[0:R, :], hit2[0:R].rearrange(flat), AX))
                then(V.tensor_tensor(gf[0:R, 1, :], gf[0:R, 0, :], off[0:R, :], ALU.subtract))
                then(V.tensor_tensor(hit[0:R].rearrange(flat),
                                     gf[0:R, 1, :].unsqueeze(2).broadcast_to([R, PH * PK, PK]),
                                     iota16[0:R, :].unsqueeze(1).broadcast_to([R, PH * PK, PK]), ALU.is_equal))
                then(V.tensor_tensor(hit[0:R], hit[0:R], f4[:, :, 1, :].unsqueeze(2).broadcast_to([R, PH, PK, PK]),
                                     ALU.mult))
                then(V.reduce_sum(sel[0:R, 1, :], hit[0:R].rearrange(flat), AX))
                dve.wait_ge(S["ex_done"], t + 1)
                then(V.reduce_sum(gs[0:R, 0, :], g3, AX))
                then(V.reciprocal(gs[0:R, 1, :], gs[0:R, 0, :]))
                V.tensor_tensor(g3, g3, gs[0:R, 1, :].unsqueeze(2).broadcast_to([R, PH, PK]), ALU.mult)\
                    .then_inc(S["sel_done"], 1)

        @block.tensor
        def _(pe):
            M = nc.tensor.matmul
            pe.wait_ge(S["cst_in"], 48)
            for t in range(NBLK):
                R = rows(t)
                pe.wait_ge(S["xs_done"], t + 1)
                for half in range(2):
                    if t >= 1:
                        pe.wait_ge(S["xf_done"], 2 * (t - 1) + half + 1)
                    for a in range(4):
                        c = 4 * half + a
                        last = nc.tensor.transpose(bank(half, R, a * R), xs[0:R, t % 2, c * P:(c + 1) * P],
                                                   ident[0:R, 0:R])
                    last.then_inc(S["tp_done"], 1)
            pe.wait_ge(S["xl_done"], 2 * NBLK)
            pe.wait_ge(S["key_in"], 16)

            def key_scores(u):
                pe.wait_ge(S["q_ev"], u + 1)
                if u >= 1:
                    pe.wait_ge(S["s_ev"], 2 * u)
                for t in range(NBLK):
                    R = rows(t)
                    last = M(PS[0:R, 6 * BANK + t * P:6 * BANK + (t + 1) * P], qT[:, u % 2, toks(t)],
                             keysT[:, u, :], start=True, stop=True)
                last.then_inc(S["s_mm"], 1)

            for u in range(NHP):
                pe.wait_ge(S["wl_done"], u + 1)
                if u >= 2:
                    pe.wait_ge(S["q_ev"], u - 1)
                for lo, hi in ((0, SEQ), (SEQ, NTOK)):
                    o = (2 + 2 * (u % 2)) * BANK
                    for k in range(KD):
                        c = slice(k * P, (k + 1) * P)
                        for w, x in ((wh, xh), (wl, xh), (wh, xl)):
                            last = M(PS[:, o + lo:o + hi], w[:, u % 2, c], x[:, k, lo:hi],
                                     start=(k == 0 and w is wh and x is xh), stop=(k == KD - 1 and x is xl))
                last.then_inc(S["q_mm"], 1)
                if u >= 1:
                    key_scores(u - 1)
            key_scores(NHP - 1)
            for t in range(NBLK):
                R = rows(t)
                pe.wait_ge(S["sel_done"], t + 1)
                if t >= 1:
                    pe.wait_ge(S["sT_act"], 3 * t)
                for a in range(3):
                    last = nc.tensor.transpose(bank(a // 2, R, (a % 2) * P), sel[0:R, a, :], ident[0:R, 0:R])
                last.then_inc(S["sT_mm"], 1)


def peer_dense(nc, T, h, sems, xh, xl, IT, JT, cT):
    GROUPS = [(0, 2 * P, [0, 1]), (2 * P, NTOK, [2, 3, 4])]
    NGMAX = NTOK - 2 * P
    TU = BANK // NKEY
    CH = 32
    UC = CH // TU
    NU = NTOK // TU
    UP = 2 * P // TU
    NCH = NTOK // CH
    QG = NKEY // 4
    SPANS = [(0, 0, 1, 4), (0, 1, 8, 4), (0, 8, QG - 1, 2), (0, QG - 1, QG, 2),
             (1, 0, 1, 0), (1, 1, QG - 1, 0), (1, QG - 1, QG, 0)]
    assert UP + 8 * 4 + (QG - 8) * 2 == NU
    ctx = ExitStack()
    with ctx:
        def sb(name, shape, dt=F32):
            return ctx.enter_context(nc.sbuf_tensor(name, shape, dt))

        PS = ctx.enter_context(nc.psum_tensor("psC", [P, 8 * BANK], F32))

        def bank(b, n=BANK, at=0, p0=0, p1=P):
            return PS[p0:p1, b * BANK + at:b * BANK + at + n]

        iota = sb("iotaC", [P, NKEY])
        rU = sb("rU", [P, 2, D])
        rV = sb("rV", [P, 2, D])
        Uh = sb("Uh", [P, 2, D], F32R)
        Ul = sb("Ul", [P, 2, D], F32R)
        Vh = sb("Vh", [P, 2, D], F32R)
        Vl = sb("Vl", [P, 2, D], F32R)
        ge = sb("ge", [P, NGMAX])
        wf = sb("wf", [P, NGMAX])
        Wh = sb("Wh", [P, 2, NGMAX], F32R)
        Wl = sb("Wl", [P, 2, NGMAX], F32R)
        ohI = sb("ohI", [P, 4, TU, NKEY])
        ohJ = sb("ohJ", [P, 4, TU, NKEY])
        ohC = sb("ohC", [P, 4, TU, NKEY])
        gst = sb("gst", [P, 2, NKEY, CH])
        gr = sb("gr", [P, 2, NGMAX // CH, 4, CH])

        names = """iota_in oh_done oh_mul oh_used gt_ev gw_out gw_done hU lU hV lV u_mm ge_done w_mul w_hi
            w_done v_mm y_added""".split()
        S = {n: sems.enter_context(nc.semaphore("c_" + n)) for n in names}
        rU_in = [sems.enter_context(nc.semaphore(f"c_rU{i}")) for i in range(2)]
        rV_in = [sems.enter_context(nc.semaphore(f"c_rV{i}")) for i in range(2)]
        gr_in = sems.enter_context(nc.semaphore("c_gr"))
        block = ctx.enter_context(nc.Block())

        def known_below(x, n):
            return isinstance(x, int) and x < n

        def over_quads(eng, quad):
            for g, a, b, n in SPANS:
                if b - a == 1:
                    quad(g, a, n)
                else:
                    with eng.Fori(a, b) as i:
                        quad(g, i, n)

        def unit_of(i, n, r):
            return (UP + 4 * i if n == 4 else UP + 16 + 2 * i) + r

        def units_at(n, k):
            return [r for r in range(n) if (r // 2 if n == 4 else r) == k]

        @block.sync
        def _(sp):
            sp.dma_start(iota[:], T["cst"][:, C_IOTA:C_IOTA + NKEY]).then_inc(S["iota_in"], 16)

            def load(s, j, k):
                if not known_below(s, 2):
                    sp.wait_ge(S["lU"], s - 1)
                sp.dma_start(rU[:, k, :], T["peer_uT"][bass.ds(j, 1), :, :].rearrange("a p c -> (a p) c"))\
                    .then_inc(rU_in[k], 16)
                if not known_below(s, 2):
                    sp.wait_ge(S["lV"], s - 1)
                sp.dma_start(rV[:, k, :], T["peer_v"][bass.ds(j, 1), :, :].rearrange("a p c -> (a p) c"))\
                    .then_inc(rV_in[k], 16)

            def load_weights(g, q):
                lo, hi, _ = GROUPS[g]
                if not known_below(QG * g + q, 2):
                    sp.wait_ge(S["w_mul"], 4 * (QG * g + q - 1))
                src = T["gates"][lo // CH:hi // CH, :, bass.ds(4 * q, 4), :].rearrange("u p j n -> p u (j n)")
                dst = gr[:, bass.ds(q % 2, 1), 0:(hi - lo) // CH, :, :].rearrange("p a u j n -> p (a u) (j n)")
                sp.dma_start(dst, src).then_inc(gr_in, 16)

            def loads(g, q, ks=range(4)):
                for k in ks:
                    load(NKEY * g + 4 * q + k, 4 * q + k, k % 2)

            loads(0, 0, (0, 1))
            sp.wait_ge(S["gw_done"], UP)
            load_weights(0, 0)
            loads(0, 0, (2, 3))
            with sp.Fori(1, QG) as i:
                load_weights(0, i)
                loads(0, i)
            loads(1, 0, (0, 1))
            sp.wait_ge(S["gw_done"], NU)
            load_weights(1, 0)
            loads(1, 0, (2, 3))
            with sp.Fori(1, QG) as i:
                load_weights(1, i)
                loads(1, i)

        @block.gpsimd
        def _(pool):
            def weigh_one_hots(u, k, slots):
                pool.wait_ge(S["oh_done"], u + 1)
                if not known_below(u, 4):
                    pool.wait_ge(S["oh_used"], u + 1 - slots)
                w = cT[:, bass.ds(TU * u, TU)].unsqueeze(2).broadcast_to([P, TU, NKEY])
                nc.gpsimd.tensor_tensor(ohC[:, k, :, :], ohJ[:, k, :, :], w, ALU.mult).then_inc(S["oh_mul"], 1)

            def store(w):
                pool.wait_ge(S["gt_ev"], UC * (w + 1))
                pool.dma_start(T["gates"][bass.ds(w, 1), :, :, :].rearrange("u p j n -> (u p) (j n)"),
                               gst[:, bass.ds(w % 2, 1), :, :].rearrange("p a j n -> p (a j n)"))\
                    .then_inc(S["gw_out"], 16)

            def stored(w):
                pool.wait_ge(S["gw_out"], 16 * (w + 1))
                pool.nop(nofuse=True).then_inc(S["gw_done"], UC)

            def chunk(w, store_last=False, slots=4):
                for r in range(UC):
                    weigh_one_hots(UC * w + r, r % slots, slots)
                    if store_last and r == 2:
                        store(w - 1)
                    if store_last and r == UC - 1:
                        stored(w - 1)

            chunk(0)
            with pool.Fori(1, UP // UC) as i:
                chunk(i, store_last=True)
            store(UP // UC - 1)
            stored(UP // UC - 1)
            for a, b, slots in ((UP // UC, (UP + 4 * 8) // UC, 4), ((UP + 4 * 8) // UC, NCH, 2)):
                with pool.Fori(a, b) as i:
                    chunk(i, slots=slots)
                    store(i)
                    stored(i)

        @block.scalar
        def _(act):
            A = nc.scalar.activation

            def high_u(s, k):
                act.wait_ge(rU_in[k], 8 * (s - k) + 16)
                if not known_below(s, 2):
                    act.wait_ge(S["u_mm"], s - 1)
                A(Uh[:, k, :], rU[:, k, :], ACT.Copy).then_inc(S["hU"], 1)

            def high_v(s, k):
                act.wait_ge(rV_in[k], 8 * (s - k) + 16)
                if not known_below(s, 2):
                    act.wait_ge(S["v_mm"], s - 1)
                A(Vh[:, k, :], rV[:, k, :], ACT.Copy).then_inc(S["hV"], 1)

            def unit_out(u, k):
                if not known_below(u, 2 * UC):
                    act.wait_ge(S["gw_done"], u + 1 - 2 * UC)
                act.wait_ge(S["oh_used"], u + 1)
                act.nop(nofuse=True)
                dst = gst[:, bass.ds(u // UC % 2, 1), :, bass.ds(TU * (u % UC), TU)]
                A(dst.rearrange("p a j n -> p (a n) j"), bank(4 + k).rearrange("p (n j) -> p n j", n=TU),
                  ACT.Copy).then_inc(S["gt_ev"], 1)

            high_u(0, 0)
            high_u(1, 1)
            high_v(0, 0)
            for r in range(2 * UC):
                unit_out(r, r % 2)
            with act.Fori(1, UP // (2 * UC)) as i:
                for r in range(2 * UC):
                    unit_out(2 * UC * i + r, r % 2)

            def quad(g, i, n):
                NG = GROUPS[g][1] - GROUPS[g][0]
                end = g == 1 and isinstance(i, int) and i == QG - 1
                for k in range(4):
                    s = NKEY * g + 4 * i + k
                    act.wait_ge(S["u_mm"], s + 1)
                    if not known_below(s, 1):
                        act.wait_ge(S["w_mul"], s)
                    A(ge[:, 0:NG], bank(6 + k % 2, NG), ACT.Gelu).then_inc(S["ge_done"], 1)
                    if not (end and k >= 2):
                        high_u(s + 2, k % 2)
                    if not (end and k == 3):
                        high_v(s + 1, 1 - k % 2)
                    for r in units_at(n, k - 2):
                        unit_out(unit_of(i, n, r), r % 2)

            over_quads(act, quad)

        @block.vector
        def _(dve):
            V = nc.vector
            dve.wait_ge(S["iota_in"], 16)

            def low_u(s, k):
                dve.wait_ge(S["hU"], s + 1)
                V.tensor_tensor(Ul[:, k, :], rU[:, k, :], Uh[:, k, :].bitcast(F32), ALU.subtract)\
                    .then_inc(S["lU"], 1)

            def low_v(s, k):
                dve.wait_ge(S["hV"], s + 1)
                V.tensor_tensor(Vl[:, k, :], rV[:, k, :], Vh[:, k, :].bitcast(F32), ALU.subtract)\
                    .then_inc(S["lV"], 1)

            def one_hots(u, k, slots=4):
                if not known_below(u, 4):
                    dve.wait_ge(S["oh_used"], u + 1 - slots)
                keys = iota[:].unsqueeze(1).broadcast_to([P, TU, NKEY])
                col = bass.ds(TU * u, TU)
                V.tensor_tensor(ohJ[:, k, :, :], keys, JT[:, col].unsqueeze(2).broadcast_to([P, TU, NKEY]),
                                ALU.is_equal)
                V.tensor_tensor(ohI[:, k, :, :], keys, IT[:, col].unsqueeze(2).broadcast_to([P, TU, NKEY]),
                                ALU.is_equal).then_inc(S["oh_done"], 1)

            low_u(0, 0)
            low_u(1, 1)
            low_v(0, 0)
            for r in range(4):
                one_hots(r, r)
            with dve.Fori(1, UP // 4) as i:
                for r in range(4):
                    one_hots(4 * i + r, r)

            def quad(g, i, n):
                lo, hi, blocks = GROUPS[g]
                NG = hi - lo
                end = g == 1 and isinstance(i, int) and i == QG - 1
                dve.wait_ge(gr_in, 16 * (QG * g + i + 1))
                for k in range(4):
                    s = NKEY * g + 4 * i + k
                    dve.wait_ge(S["ge_done"], s + 1)
                    if not known_below(s, 1):
                        dve.wait_ge(S["w_done"], s)
                    w = gr[:, bass.ds(i % 2, 1), 0:NG // CH, k, :].rearrange("p a u n -> p (a u) n")
                    V.tensor_tensor(wf[:, 0:NG].rearrange("p (u n) -> p u n", n=CH),
                                    ge[:, 0:NG].rearrange("p (u n) -> p u n", n=CH), w, ALU.mult)\
                        .then_inc(S["w_mul"], 1)
                    dve.wait_ge(S["w_mul"], s + 1)
                    if not known_below(s, 2):
                        dve.wait_ge(S["v_mm"], s - 1)
                    V.tensor_copy(Wh[:, k % 2, 0:NG], wf[:, 0:NG]).then_inc(S["w_hi"], 1)
                    dve.wait_ge(S["w_hi"], s + 1)
                    V.tensor_tensor(Wl[:, k % 2, 0:NG], wf[:, 0:NG], Wh[:, k % 2, 0:NG].bitcast(F32),
                                    ALU.subtract).then_inc(S["w_done"], 1)
                    if not (end and k >= 2):
                        low_u(s + 2, k % 2)
                    if not (end and k == 3):
                        low_v(s + 1, 1 - k % 2)
                    for r in units_at(n, k):
                        one_hots(unit_of(i, n, r), r % n, n)
                if isinstance(i, int) and i == QG - 1:
                    dve.wait_ge(S["v_mm"], NKEY * (g + 1))
                    for b, t in enumerate(blocks):
                        R = rows(t)
                        V.tensor_tensor(h[0:R, t, :], PS[0:R, 2 * b * BANK:2 * (b + 1) * BANK], h[0:R, t, :],
                                        ALU.add).then_inc(S["y_added"], 1)

            over_quads(dve, quad)

        @block.tensor
        def _(pe):
            M = nc.tensor.matmul

            def weights(u, k):
                pe.wait_ge(S["oh_mul"], u + 1)
                if not known_below(u, 2):
                    pe.wait_ge(S["gt_ev"], u - 1)
                for a in range(TU):
                    last = M(bank(4 + k % 2, NKEY, a * NKEY), ohI[:, k, a, :], ohC[:, k, a, :], start=True, stop=True)
                last.then_inc(S["oh_used"], 1)

            for r in range(4):
                weights(r, r)
            with pe.Fori(1, UP // 4) as i:
                for r in range(4):
                    weights(4 * i + r, r)

            def up(g, s, k):
                lo, hi, _ = GROUPS[g]
                pe.wait_ge(S["lU"], s + 1)
                if not known_below(s, 2):
                    pe.wait_ge(S["ge_done"], s - 1)
                for d in range(KD):
                    c = slice(d * P, (d + 1) * P)
                    for a, x in ((Uh, xh), (Ul, xh), (Uh, xl)):
                        last = M(bank(6 + k, hi - lo), a[:, k, c], x[:, d, lo:hi],
                                 start=(d == 0 and a is Uh and x is xh), stop=(d == KD - 1 and x is xl))
                last.then_inc(S["u_mm"], 1)

            def down(g, s, k, first, final):
                pe.wait_ge(S["w_done"], s + 1)
                pe.wait_ge(S["lV"], s + 1)
                for b, t in enumerate(GROUPS[g][2]):
                    R = rows(t)
                    for n in range(2):
                        c = slice(n * 512, (n + 1) * 512)
                        for a, w, v in ((0, Wh, Vh), (1, Wl, Vh), (2, Wh, Vl)):
                            last = M(bank(2 * b + n, p1=R), w[:, k, b * P:b * P + R], v[:, k, c],
                                     start=(first and a == 0), stop=(final and a == 2),
                                     skip_group_check=True)
                last.then_inc(S["v_mm"], 1)

            def quad(g, i, n):
                s0 = NKEY * g + 4 * i
                first, final = (isinstance(i, int) and i == x for x in (0, QG - 1))
                if first:
                    up(g, s0, 0)
                for k in range(4):
                    if not (final and k == 3):
                        up(g, s0 + k + 1, 1 - k % 2)
                    if first and g == 1 and k == 0:
                        pe.wait_ge(S["y_added"], len(GROUPS[0][2]))
                        pe.wait_ge(S["gt_ev"], NU)
                    down(g, s0 + k, k % 2, first and k == 0, final and k == 3)
                    for r in units_at(n, k - 1):
                        weights(unit_of(i, n, r), r)

            over_quads(pe, quad)


def final_norm(nc, T, h, sems):
    ctx = ExitStack()
    with ctx:
        def sb(name, shape, dt=F32):
            return ctx.enter_context(nc.sbuf_tensor(name, shape, dt))

        st = sb("stD", [P, 20])
        junk = sb("junk", [P, NBLK, D])
        gfin = sb("gfin", [P, D])
        y = sb("y", [P, NBLK, D])
        S = {n: sems.enter_context(nc.semaphore("d_" + n)) for n in "g_in sq ms rstd y_done y_out".split()}
        block = ctx.enter_context(nc.Block())

        @block.sync
        def _(sp):
            sp.dma_start(gfin[:], T["norm_final"].broadcast_to([P, D])).then_inc(S["g_in"], 16)
            for t in range(NBLK):
                sp.wait_ge(S["y_done"], t + 1)
                dst = T["y_p"][toks(t), :] if t < 4 else T["y_s"]
                sp.dma_start(dst, y[0:rows(t), t, :]).then_inc(S["y_out"], 16)
            sp.wait_ge(S["y_out"], 16 * NBLK)

        @block.scalar
        def _(act):
            for t in range(NBLK):
                R = rows(t)
                nc.scalar.activation(junk[0:R, t, :], h[0:R, t, :], ACT.Square, accum_out=st[0:R, t:t + 1])\
                    .then_inc(S["sq"], 1)

        @block.gpsimd
        def _(pool):
            pool.memset(st[:, 19:20], -0.5).then_inc(S["ms"], 1)
            for t in range(NBLK):
                R = rows(t)
                pool.wait_ge(S["sq"], t + 1)
                nc.gpsimd.tensor_scalar(st[0:R, 5 + t:6 + t], st[0:R, t:t + 1], 1.0 / D, EPS, ALU.mult, ALU.add)\
                    .then_inc(S["ms"], 1)
                pool.wait_ge(S["ms"], t + 2)
                nc.gpsimd.tensor_tensor(st[0:R, 10 + t:11 + t], st[0:R, 5 + t:6 + t], st[0:R, 19:20], ALU.pow)\
                    .then_inc(S["rstd"], 1)

        @block.vector
        def _(dve):
            dve.wait_ge(S["g_in"], 16)
            for t in range(NBLK):
                R = rows(t)
                dve.wait_ge(S["rstd"], t + 1)
                nc.vector.scalar_tensor_tensor(out=y[0:R, t, :], in0=h[0:R, t, :], scalar=st[0:R, 10 + t:11 + t],
                                               in1=gfin[0:R, :], op0=ALU.mult, op1=ALU.mult)\
                    .then_inc(S["y_done"], 1)


def build(nc, T):
    ctx = ExitStack()
    with ctx:
        h = ctx.enter_context(nc.sbuf_tensor("h", [P, NBLK, D], F32))
        block_a(nc, T, h, ctx)
        x = [ctx.enter_context(nc.sbuf_tensor(n, [P, KD, NTOK], F32R)) for n in ("xh", "xl")]
        IJ = [ctx.enter_context(nc.sbuf_tensor(n, [P, NTOK], F32)) for n in ("IT", "JT", "cT")]
        peer_select(nc, T, h, ctx, *x, *IJ)
        peer_dense(nc, T, h, ctx, *x, *IJ)
        final_norm(nc, T, h, ctx)


HEADS = [0, 4, 1, 5, 2, 6, 3, 7]


def constants():
    c = np.zeros((P, C_ALL), np.float32)
    c[:, C_ID:C_ID + P] = np.eye(P)
    c[:, C_IOTA:C_IOTA + P] = np.arange(P)
    q, k = np.arange(P)[:, None], np.arange(P)[None, :]
    c[:, C_CAUSAL:C_CAUSAL + P] = np.where(k <= q, 0, NEG)
    q, k = np.arange(NS)[:, None], np.arange(NS)[None, :]
    c[:NS, C_NEW:C_NEW + NS] = np.where((q // NQ == k // NQ) & (k <= q), 0, NEG)
    same = np.zeros((NS, NB, 8, NQ), np.float32)
    for tok in range(NS):
        same[tok, tok // NQ, :, tok % NQ] = 1
    c[:NS, C_SAME:C_SAME + 512] = same.reshape(NS, 512)
    inv = np.float32(10000.0) ** (-np.arange(32, dtype=np.float32) / np.float32(32))
    pos = np.zeros((NBLK, P), np.float32)
    pos[:4] = np.arange(SEQ).reshape(4, P)
    pos[4, :NS] = PAST + np.arange(NS) % NQ
    first = np.array([at for _, _, at in ROWS16], np.float32)
    c[:, C_FIRST:C_FIRST + PK] = first
    c[:, C_FIRST + PK:C_FIRST + 2 * PK] = np.diff(first, prepend=0)
    ang = pos[:, :, None] * inv
    cos, sin = np.cos(ang), np.sin(ang)
    c[:, C_COS:C_COS + 320] = np.concatenate([cos, cos], -1).transpose(1, 0, 2).reshape(P, 320)
    c[:, C_SIN:C_SIN + 320] = np.concatenate([-sin, sin], -1).transpose(1, 0, 2).reshape(P, 320)
    return c


def kernel(**inputs):
    import concourse.bacc as _bacc
    from concourse.bass_utils import run_bass_kernel_spmd as _run

    x = {k: np.asarray(v) for k, v in inputs.items()}
    n_pool = x["cache_mla_ckv"].shape[1]

    def chunks(w):
        return w.reshape(-1, P, w.shape[-1]).transpose(1, 0, 2)

    w_in = x["w_in"][0]
    dq = w_in[:, DQ:DQ + 512].reshape(D, 8, 64)[:, HEADS].reshape(D, 512)
    w_in = np.concatenate([w_in[:, :DQ], dq, w_in[:, DK:]], 1)
    w_uq = x["w_uq"][0].reshape(256, 8, 96)
    w_o = x["w_o"][0]
    w_o = np.concatenate([w_o[:512], w_o[512:].reshape(8, 64, D)[HEADS].reshape(512, D)], 0)
    ckv, kr = x["cache_mla_ckv"][0], x["cache_mla_kr"][0]
    kv = x["cache_dsa_kv"][0].reshape(n_pool, PAGE, 2, 128)
    gains = [x[n][0].reshape(-1, P).T for n in ("norm_mix", "norm_mem", "mem_norm", "norm_ffn", "mla_q_norm")]
    mk = x["cache_mem_k"][0].reshape(NB, 256, 2, P).transpose(0, 3, 2, 1)
    mv = x["cache_mem_v"][0].reshape(NB, 2, P, 256).transpose(0, 2, 1, 3)
    arrays = {
        "cst": constants(),
        "x_prompt": x["x_prompt"], "x_sample": x["x_sample"], "mem_prompt": x["mem_prompt"],
        "gcol": np.concatenate(gains, 1), "mla_kv_norm": x["mla_kv_norm"], "norm_final": x["norm_final"][None],
        "page_table": x["page_table"].reshape(1, -1),
        "w_in": chunks(w_in),
        "w_uqn": chunks(w_uq[:, :, :64].reshape(256, 512)), "w_uqr": chunks(w_uq[:, :, 64:].reshape(256, 256)),
        "w_ukT": chunks(x["w_uk"][0].transpose(1, 2, 0).reshape(512, 128)),
        "w_uv": x["w_uv"][0].reshape(128, 512),
        "w_o": chunks(w_o),
        "wq_x": chunks(x["wq_x"][0]), "wkv_x": chunks(np.concatenate([x["wk_x"][0], x["wv_x"][0]], 1)),
        "wo_x": chunks(x["wo_x"][0]),
        "mem_cache": np.concatenate([mk, mv], 2),
        "ikT": x["cache_dsa_idx"][0].transpose(0, 2, 1), "krT": kr.transpose(0, 2, 1),
        "poolM": np.concatenate([ckv.transpose(0, 2, 1), ckv], 2),
        "poolD": np.concatenate([kv[:, :, 0].transpose(0, 2, 1), kv[:, :, 1]], 2),
        "w_pq": x["w_pq"][0].reshape(KD, P, 2 * PH, P).transpose(2, 1, 0, 3).reshape(2 * PH, P, D),
        "keysT": x["peer_keys"][0].reshape(2 * PH, NKEY, P).transpose(2, 0, 1),
        "peer_uT": x["peer_u"][0].reshape(NKEY, NKEY, KD, P).transpose(1, 3, 2, 0).reshape(NKEY, P, D),
        "peer_v": x["peer_v"][0].reshape(NKEY, NKEY, D).transpose(1, 0, 2),
    }
    outs = {
        "y_p": (1, SEQ, D), "y_s": (NB, NQ, D),
        "new_ckv_p": (1, 1, SEQ, 128), "new_kr_p": (1, 1, SEQ, 32), "new_kv_p": (1, 1, SEQ, 2, 2, 64),
        "new_idx_p": (1, 1, SEQ, 64), "new_mem_k_p": (1, 1, 256, 4, 64), "new_mem_v_p": (1, 1, 256, 4, 64),
        "new_ckv_s": (1, NB, NQ, 128), "new_kr_s": (1, NB, NQ, 32), "new_kv_s": (1, NB, NQ, 2, 2, 64),
        "new_idx_s": (1, NB, NQ, 64),
    }
    flat = {"y_p": (SEQ, D), "y_s": (NS, D)}
    for n, s in outs.items():
        toks_ = int(np.prod(s[:3])) if n[:3] == "new" else flat[n][0]
        flat[n] = (toks_, int(np.prod(s)) // toks_)
    nc = _bacc.Bacc("TRN2", target_bir_lowering=False, num_devices=1)
    T = {"n_pool": n_pool}
    arrays = {n: np.ascontiguousarray(a) for n, a in arrays.items()}
    for n, a in arrays.items():
        T[n] = nc.dram_tensor("in_" + n, a.shape, mybir.dt.from_np(a.dtype), kind="ExternalInput").ap()
    for n, s in flat.items():
        T[n] = nc.dram_tensor("out_" + n, s, F32, kind="ExternalOutput").ap()
    T["gates"] = nc.dram_tensor("gates", (NTOK // 32, P, NKEY, 32), F32, kind="Internal").ap()
    build(nc, T)
    r = _run(nc, [{"in_" + n: a for n, a in arrays.items()}], core_ids=[0])
    return tuple(np.asarray(r.results[0]["out_" + n]).reshape(s) for n, s in outs.items())
```

```python
from contextlib import ExitStack

import numpy as np
import concourse.bass as bass
from concourse import mybir
from concourse.alu_op_type import AluOpType as ALU

F32 = mybir.dt.float32
F32R = mybir.dt.float32r
BF16 = mybir.dt.bfloat16
U32 = mybir.dt.uint32
I32 = mybir.dt.int32
ACT = mybir.ActivationFunctionType
AX = mybir.AxisListType.X

P = 128
D = 1024
KD = D // P
SEQ, NB, NQ = 512, 8, 8
NS = NB * NQ
NTOK = SEQ + NS
NBLK = SEQ // P + 1
PAGE, NPAGE = 128, 16
PAST = PAGE * NPAGE
NEWC = PAST + NS
W_IN = 1768
CQ, CKV, KR, DQ, DK, DV, IQ, IW, IK = 0, 256, 384, 416, 928, 1056, 1184, 1696, 1704
PC = W_IN // 4
EPS = 1e-6
NEG = -1e30
TAKEN = -3e38
K_PROMPT, K_SAMPLE = 128, 256
MLA_SCALE = 96 ** -0.5
DSA_SCALE = 64 ** -0.5
NKEY, PH, PK = 128, 8, 16
BANK = 512

C_ID, C_IOTA, C_CAUSAL, C_NEW, C_SAME, C_COS, C_SIN = 0, 128, 256, 384, 448, 960, 1280
C_FIRST = 1600
C_ALL = 1632

ROWS16 = []
for _a in range(PK):
    ROWS16.append((_a, PK // (_a + 1), sum(n for _, n, _ in ROWS16)))
NCAND = ROWS16[-1][2] + 1


def rows(t):
    return P if t < NBLK - 1 else NS


def toks(t):
    return slice(t * P, t * P + rows(t))


def block_a(nc, T, h, sems):
    ctx = ExitStack()
    with ctx:
        def sb(name, shape, dt=F32):
            return ctx.enter_context(nc.sbuf_tensor(name, shape, dt))

        def sem(name):
            return sems.enter_context(nc.semaphore(name))

        PS = ctx.enter_context(nc.psum_tensor("psA", [P, 8 * BANK], F32))

        def bank(b, n=BANK, at=0, p0=0, p1=P):
            return PS[p0:p1, b * BANK + at:b * BANK + at + n]

        cst = sb("cst", [P, C_ALL])
        xT = sb("xT", [P, KD, NTOK])
        gcol = sb("gcol", [P, 4 * KD + 2])
        gkv = sb("gkv", [P, P])
        st = sb("st", [P, 160])
        sm = sb("sm", [P, 4 * 100])
        ssm = sb("ssm", [P, 4, NB])
        pts = sb("pts", [1, NB * NPAGE], I32)
        qrTs = sb("qrTs", [P, 2, 64])
        bdq = sb("bdq", [P, NB, 2, 4, NQ])
        Dp = sb("Dp", [P, 4, NS])
        same16 = sb("same16", [NS, NB, 64], BF16)
        id16 = sb("id16", [P, P], BF16)
        causal16 = sb("causal16", [P, P], BF16)
        m8 = sb("m8", [P, 8])
        qlTs = sb("qlTs", [P, NB, 8, NQ])
        olT = sb("olT", [P, NB, 8, NQ])
        arena = sb("arena", [P, 37800])

        def region(at, *shape, p=P):
            n = int(np.prod(shape))
            a = arena[0:p, at:at + n]
            if len(shape) == 1:
                return a
            names = "abcd"[:len(shape)]
            spec = f"p ({' '.join(names)}) -> p {' '.join(names)}"
            return a.rearrange(spec, **{k: v for k, v in zip(names[1:], shape[1:])})

        win = region(0, KD, W_IN)
        proj = region(14144, NBLK, W_IN)
        kT = region(22984, 4, NTOK)
        dqT = region(25288, 4, NTOK)
        iqT = region(27592, 4, SEQ)
        iqTs = region(29640, NB, 8, NQ)
        cqT = region(30152, 2, NTOK)
        xs = region(31304, 2, D)
        ropeA = region(33352, 640)
        ropeM = region(33992, 640)
        kk = region(34632, 256)
        w_uqn = region(34888, 2, 512)
        w_uqr = region(35912, 2, 256)
        w_ukT = region(36424, 4, P)
        w_uv = region(36936, 512)
        qnT = region(0, 4, NTOK)
        qlT = region(2304, 8, SEQ)
        qrT = region(6400, 2, NTOK)
        Vm = region(7552, 4, 512)
        mb16 = region(9600, 4 * SEQ // 2).bitcast(BF16).rearrange("p (a b) -> p a b", a=4)
        accs = region(10624, 3, SEQ)
        relu = region(12160, 2, SEQ)
        qr = region(13184, 256)
        Pr = region(31304, 3, SEQ)
        PT = region(33352, 2, SEQ)
        ikT = region(0, NB // 2, PAST)
        KV = region(0, 2, 2, NPAGE, 256)
        krT = region(16384, 2, PAST)
        sw = region(32328, NEWC, p=NS)
        relus = region(31304, 2, 512)
        selE = region(20480, NB, 8, NQ, p=NS)
        Ps = region(25288, 2, NEWC)
        mbs = region(30152, NEWC // 2, p=NS).bitcast(BF16)
        PTs = region(31304, 2, SEQ)
        w_o = region(8192, KD, D)
        wqx = region(0, KD, 256)
        wkv = region(2048, KD, 512)
        memr = region(6144, 2, D)
        mT = region(16384, KD, 256)
        mkv = region(18432, 2, 512)
        mkT = region(19456, 2, 256)
        qxT = region(19968, 2, NTOK)
        bdx = region(21120, 2, NB, 4, NQ)
        oxT = region(21632, 2, NTOK)
        xc = region(22784, NB, 4, 256)
        wox = region(34888, 2, D)
        assert 22784 + 8192 <= 31304

        ident = cst[:, C_ID:C_ID + P]
        causal = cst[:, C_CAUSAL:C_CAUSAL + P]
        same = cst[0:NS, C_SAME:C_SAME + 512]
        cosT = cst[:, C_COS:C_COS + 320].rearrange("p (t c) -> p t c", t=NBLK)
        sinT = cst[:, C_SIN:C_SIN + 320].rearrange("p (t c) -> p t c", t=NBLK)

        names = """cst_in x_in win_in wsm_in pt_in mem_in late_in wox_in wo_in gk_in
            sq_done ms_done rstd_done xs_done tp_done xT_done pj_mm pj_act pj_dve
            sq2_done ms2_done rstd2_done cq_done ckv_done rp_dve rp_pool c16 half_ready
            tA_mm tB_mm tA_ev tB_ev up_mm up_ev ql_mm ql_ev qr_mm qr_chain qr_done qr_tp qr_ev 
            vm_mm vm_ev ix_mm ix_relu ix_acc mask_done tk
            at_S at_nb at_exp at_P at_T at_PT at_O at_oe at_c
            sel_E sel_T sel_D xi_mm xi_relu xi_sc sw_done mbs_done
            ss_S ss_nb ss_exp ss_P ss_N ss_T ss_PT ss_oe ss_c uv_mm uv_ev
            wo_mm h_done mkv_mm mkv_ev mkT_tp mkT_ev qx_mm qx_ev bdx_done ox_mm hx_done out_st""".split()
        S = {n: sem(n) for n in names}
        ik_sp, ik_pool = sem("ik_sp"), sem("ik_pool")
        kr_in = [sem(f"kr_in{i}") for i in range(4)]
        kv_sp = [sem(f"kv_sp{i}") for i in range(2)]
        kv_pool = [sem(f"kv_pool{i}") for i in range(2)]
        kv_act = [sem(f"kv_act{i}") for i in range(2)]
        SMP = [(kind, p) for kind in range(2) for p in range(NB // 2)]

        IK_SP = 9
        PAGES = [(b2, 4 * c + a) for c in range(4) for b2 in range(2) for a in range(4)]
        SP_PAGES = [x for n, x in enumerate(PAGES) if n % 8 in (0, 1, 2)]
        POOL_PAGES = [x for n, x in enumerate(PAGES) if n % 8 in (3, 4, 5)]
        ACT_PAGES = [x for n, x in enumerate(PAGES) if n % 8 in (6, 7)]

        def load_page(eng, dst, pool, b, j, done):
            pg = eng.value_load(pts[0:1, b * NPAGE + j:b * NPAGE + j + 1], min_val=0, max_val=T["n_pool"] - 1)
            eng.dma_start(dst, T[pool][bass.ds(pg, 1), :, :].rearrange("a q c -> (a q) c")).then_inc(done, 16)

        def load_index_keys(eng, j0, j1, done):
            eng.wait_ge(S["ql_ev"], 16)
            for b in range(NB):
                if b == 2:
                    eng.wait_ge(S["at_oe"], 4 * 8)
                p, b2 = divmod(b, 2)
                for j in range(j0, j1):
                    load_page(eng, ikT[64 * b2:64 * b2 + 64, p, j * PAGE:(j + 1) * PAGE], "ikT", b, j, done)

        def load_kv(eng, i, pages, done):
            kind, p = SMP[i]
            if i == 0:
                eng.wait_ge(S["at_oe"], n_self)
                eng.wait_ge(S["out_st"], 16 * 4 * NBLK)
            elif i == 1:
                eng.wait_ge(S["xi_mm"], 20)
            for n, (b2, j) in enumerate(pages):
                if i >= 2 and (n == 0 or j // 4 != pages[n - 1][1] // 4):
                    eng.wait_ge(S["ss_c"], 5 * (i - 2) + j // 4 + 1)
                load_page(eng, KV[:, (i + 1) % 2, b2, j, :], ("poolM", "poolD")[kind], 2 * p + b2, j,
                          done[(i + 1) % 2])

        SELF = [("mla", t, i) for i in range(8) for t in range(4)] + \
               [("dsa", t, i) for t in range(4) for i in range(8)]
        CROSS = [("mem", t, i) for t in range(4) for i in range(4)] + [("smp", 4, g) for g in range(2)]

        def keys_of(u):
            kind, t, i = u
            return P * (t + 1) if kind in ("mla", "dsa") else 256

        def scale_of(u):
            return MLA_SCALE if u[0] == "mla" else DSA_SCALE

        n_self, n_cross = len(SELF), len(CROSS)
        UNITS = SELF + CROSS
        NORM = {"mix": (0, 5, 0), "mem": (5, 2, 2 * KD), "xmem": (7, 5, KD)}
        STREAM_UNITS = 12

        def src_of(stage, t):
            return memr[:, t, :] if stage == "mem" else h[0:rows(t), t, :]

        def nrows(stage, t):
            return P if stage == "mem" else rows(t)

        def dst_of(stage, t):
            return mT[:, :, t * P:(t + 1) * P] if stage == "mem" else xT[:, :, toks(t)]

        block = ctx.enter_context(nc.Block())

        @block.sync
        def _(sp):
            sp.dma_start(cst[:], T["cst"]).then_inc(S["cst_in"], 16)
            for t in range(4):
                sp.dma_start(h[:, t, :], T["x_prompt"][0, t * P:(t + 1) * P, :]).then_inc(S["x_in"], 16)
            sp.dma_start(h[0:NS, 4, :], T["x_sample"].rearrange("b t d -> (b t) d")).then_inc(S["x_in"], 16)
            sp.dma_start(gcol[:], T["gcol"]).then_inc(S["gk_in"], 16)
            sp.dma_start(gkv[:], T["mla_kv_norm"].broadcast_to([P, P])).then_inc(S["gk_in"], 16)
            for k in range(KD):
                sp.dma_start(win[:, k, :], T["w_in"][:, k, :]).then_inc(S["win_in"], 16)
            sp.dma_start(pts[:], T["page_table"]).then_inc(S["pt_in"], 16)
            for dst, name in ((w_uqn, "w_uqn"), (w_uqr, "w_uqr"), (w_ukT, "w_ukT"), (w_uv, "w_uv")):
                sp.dma_start(dst, T[name]).then_inc(S["wsm_in"], 16)
            for t in range(NBLK):
                R = rows(t)
                sp.wait_ge(S["ckv_done"], t + 1)
                sp.wait_ge(S["rp_dve"], t + 1)
                sp.wait_ge(S["rp_pool"], t + 1)
                for name, c, n in (("ckv", CKV, 128), ("kr", KR, 32), ("kv", DK, 256), ("idx", IK, 64)):
                    dst = T[f"new_{name}_p"][toks(t), :] if t < 4 else T[f"new_{name}_s"]
                    sp.dma_start(dst, proj[0:R, t, c:c + n]).then_inc(S["out_st"], 16)

            sp.wait_ge(S["pt_in"], 16)

            load_index_keys(sp, 0, IK_SP, ik_sp)
            for i in range(NB):
                load_kv(sp, i, PAGES if SMP[i][0] == 0 else SP_PAGES, kv_sp)
            sp.wait_ge(S["ss_c"], 5 * (NB - 1))
            sp.dma_start(w_o, T["w_o"]).then_inc(S["wo_in"], 16)
            sp.wait_ge(S["ss_c"], 5 * NB)
            sp.dma_start(memr, T["mem_prompt"][0].rearrange("(a p) d -> p a d", p=P)).then_inc(S["mem_in"], 16)
            sp.dma_start(wkv, T["wkv_x"]).then_inc(S["late_in"], 16)
            sp.dma_start(wqx, T["wq_x"]).then_inc(S["late_in"], 16)
            sp.dma_start(xc, T["mem_cache"].rearrange("b p a c -> p b a c")).then_inc(S["late_in"], 16)
            sp.wait_ge(S["uv_ev"], 8)
            sp.dma_start(wox, T["wo_x"]).then_inc(S["wox_in"], 16)
            for t in range(2):
                sp.wait_ge(S["mkv_ev"], t + 1)
                for i, name in enumerate(("new_mem_k_p", "new_mem_v_p")):
                    sp.dma_start(T[name][t * P:(t + 1) * P, :], mkv[:, t, 256 * i:256 * (i + 1)])\
                        .then_inc(S["out_st"], 16)
            sp.wait_ge(S["out_st"], 16 * (4 * NBLK + 4))

        @block.gpsimd
        def _(pool):
            pool.memset(st[:, 156:158], -0.5).then_inc(S["half_ready"], 1)
            pool.memset(bdq[:], 0.0).then_inc(S["c16"], 1)

            def norm_rstd(stage):
                base, n, _ = NORM[stage]
                for t in range(n):
                    u, R = base + t, nrows(stage, t)
                    pool.wait_ge(S["sq_done"], u + 1)
                    nc.gpsimd.tensor_scalar(st[0:R, 40 + u:41 + u], st[0:R, u:u + 1], 1.0 / D, EPS,
                                            ALU.mult, ALU.add).then_inc(S["ms_done"], 1)
                    pool.wait_ge(S["ms_done"], u + 1)
                    nc.gpsimd.tensor_tensor(st[0:R, 80 + u:81 + u], st[0:R, 40 + u:41 + u],
                                            st[0:R, 156:157], ALU.pow).then_inc(S["rstd_done"], 1)

            pool.wait_ge(S["half_ready"], 1)
            norm_rstd("mix")
            pool.wait_ge(S["cst_in"], 16)
            for t in range(NBLK):
                R = rows(t)
                pool.wait_ge(S["sq2_done"], t + 1)
                for j, n in ((0, 256), (1, 128)):
                    c = 120 + 2 * t + j
                    nc.gpsimd.tensor_scalar(st[0:R, c:c + 1], st[0:R, c:c + 1], 1.0 / n, EPS,
                                            ALU.mult, ALU.add).then_inc(S["ms2_done"], 1)
                pool.wait_ge(S["ms2_done"], 2 * t + 2)
                nc.gpsimd.tensor_tensor(st[0:R, 140 + 2 * t:142 + 2 * t], st[0:R, 120 + 2 * t:122 + 2 * t],
                                        st[0:R, 156:158], ALU.pow).then_inc(S["rstd2_done"], 1)
                pool.wait_ge(S["rp_dve"], t + 1)
                if t >= 1:
                    pool.wait_ge(S["tA_mm"], 2 * t - 1)
                nc.gpsimd.tensor_copy(kk[0:R, 0:128].rearrange("p (a c) -> p a c", a=4),
                                      proj[0:R, t, KR:KR + 32].unsqueeze(1).broadcast_to([R, 4, 32]))
                nc.gpsimd.tensor_copy(kk[0:R, 128:256].rearrange("p (a c) -> p a c", a=2),
                                      proj[0:R, t, IK:IK + 64].unsqueeze(1).broadcast_to([R, 2, 64]))\
                    .then_inc(S["rp_pool"], 1)
            pool.wait_ge(S["pt_in"], 16)
            load_index_keys(pool, IK_SP, NPAGE, ik_pool)
            pool.wait_ge(S["at_oe"], n_self)
            pool.wait_ge(S["out_st"], 16 * 4 * NBLK)
            for b in range(NB):
                p, b2 = divmod(b, 2)
                for j in range(NPAGE):
                    load_page(pool, krT[32 * p:32 * p + 32, b2, j * PAGE:(j + 1) * PAGE], "krT", b, j, kr_in[p])
            for i in range(NB // 2, NB):
                load_kv(pool, i, POOL_PAGES, kv_pool)
            norm_rstd("mem")
            norm_rstd("xmem")

        @block.scalar
        def _(act):
            def norm_scale(stage):
                base, n, _ = NORM[stage]

                def square(t):
                    u, R = base + t, nrows(stage, t)
                    if stage == "mix":
                        act.wait_ge(S["x_in"], 16 * NBLK)
                    elif stage == "mem":
                        act.wait_ge(S["mem_in"], 16)
                    else:
                        act.wait_ge(S["h_done"], 2 * (t + 1))
                    if u >= 2:
                        act.wait_ge(S["tp_done"], 2 * (u - 1))
                    nc.scalar.activation(xs[0:R, u % 2, :], src_of(stage, t), ACT.Square,
                                         accum_out=st[0:R, u:u + 1]).then_inc(S["sq_done"], 1)

                square(0)
                for t in range(n):
                    u, R = base + t, nrows(stage, t)
                    if t + 1 < n:
                        square(t + 1)
                    act.wait_ge(S["rstd_done"], u + 1)
                    nc.scalar.activation(xs[0:R, u % 2, :], src_of(stage, t), ACT.Copy,
                                         scale=st[0:R, 80 + u:81 + u]).then_inc(S["xs_done"], 1)

            norm_scale("mix")
            for t in range(NBLK):
                R = rows(t)
                for c in range(2):
                    act.wait_ge(S["pj_mm"], 4 * t + c + 1)
                    nc.scalar.activation(proj[0:R, t, c * PC:(c + 1) * PC], bank(2 + c, PC, p1=R), ACT.Copy)\
                        .then_inc(S["pj_act"], 1)
                act.wait_ge(S["pj_act"], 2 * t + 1)
                act.wait_ge(S["tp_done"], 10)
                if t >= 1:
                    act.wait_ge(S["cq_done"], t)
                nc.scalar.activation(xs[0:R, 0, 0:256], proj[0:R, t, CQ:CQ + 256], ACT.Square,
                                     accum_out=st[0:R, 120 + 2 * t:121 + 2 * t])
                nc.scalar.activation(xs[0:R, 0, 256:384], proj[0:R, t, CKV:CKV + 128], ACT.Square,
                                     accum_out=st[0:R, 121 + 2 * t:122 + 2 * t]).then_inc(S["sq2_done"], 1)
                act.wait_ge(S["rstd2_done"], t + 1)
                nc.scalar.activation(proj[0:R, t, CQ:CQ + 256], proj[0:R, t, CQ:CQ + 256], ACT.Copy,
                                     scale=st[0:R, 140 + 2 * t:141 + 2 * t]).then_inc(S["cq_done"], 1)
                act.wait_ge(S["tA_mm"], 2 * t + 1)
                nc.scalar.activation(kT[:, :, toks(t)],
                                     bank(6, 4 * R).rearrange("p (a r) -> p a r", a=4), ACT.Copy)\
                    .then_inc(S["tA_ev"], 1)
                act.wait_ge(S["tA_mm"], 2 * t + 2)
                nc.scalar.activation(dqT[:, :, toks(t)],
                                     bank(6, 4 * R).rearrange("p (a r) -> p a r", a=4), ACT.Copy)\
                    .then_inc(S["tA_ev"], 1)
            act.wait_ge(S["pj_mm"], 4 * NBLK)
            for p in range(4):
                act.wait_ge(S["up_mm"], p + 1)
                nc.scalar.activation(qnT[:, p, :], bank(2 * (p % 2), NTOK), ACT.Copy).then_inc(S["up_ev"], 1)
            for t in range(4):
                act.wait_ge(S["vm_mm"], t + 1)
                nc.scalar.activation(Vm[:, t, :], bank(6 + t % 2), ACT.Copy).then_inc(S["vm_ev"], 1)
            for i in range(24):
                L = P * (i // 8 + 2)
                act.wait_ge(S["ix_mm"], i + 1)
                if i >= 2:
                    act.wait_ge(S["ix_acc"], i - 1)
                nc.scalar.activation(relu[:, i % 2, 0:L], bank(4 + i % 2, L), ACT.Relu)\
                    .then_inc(S["ix_relu"], 1)

            def softmax_exp(i, u):
                L = keys_of(u)
                act.wait_ge(S["at_nb"], i + 1)
                if i >= 3:
                    act.wait_ge(S["at_T"], i - 2)
                nc.scalar.activation(Pr[:, i % 3, 0:L], bank(i % 2, L), ACT.Exp, bias=sm[:, 100 + i:101 + i],
                                     scale=scale_of(u), accum_out=sm[:, 200 + i:201 + i])\
                    .then_inc(S["at_exp"], 1)

            def probs_out(i, u):
                L = keys_of(u)
                act.wait_ge(S["at_T"], i + 1)
                if i >= 2:
                    act.wait_ge(S["at_O"], i - 1)
                nc.scalar.activation(PT[:, i % 2, 0:L], bank(2 + i % 2, L), ACT.Copy).then_inc(S["at_PT"], 1)

            def attention(lo, hi):
                for s in range(lo, hi + 2):
                    if s < hi:
                        softmax_exp(s, UNITS[s])
                    if s - 2 >= lo:
                        probs_out(s - 2, UNITS[s - 2])

            attention(0, n_self)
            for i in range(4 * 5):
                n = 512 if i % 5 < 4 else NS
                act.wait_ge(S["xi_mm"], i + 1)
                if i >= 2:
                    act.wait_ge(S["xi_sc"], i - 1)
                nc.scalar.activation(relus[:, i % 2, 0:n], bank(5 + i % 2, n), ACT.Relu)\
                    .then_inc(S["xi_relu"], 1)
            act.wait_ge(S["pt_in"], 16)
            for i in range(NB):
                kind, p = SMP[i]
                act.wait_ge(S["ss_nb"], i + 1)
                if i >= 2:
                    act.wait_ge(S["ss_T"], 5 * (i - 1))
                nc.scalar.activation(Ps[:, i % 2, :], PS[:, 0:NEWC], ACT.Exp, bias=ssm[:, 1, i:i + 1],
                                     scale=(MLA_SCALE, DSA_SCALE)[kind], accum_out=ssm[:, 2, i:i + 1])\
                    .then_inc(S["ss_exp"], 1)
                act.wait_ge(S["ss_P"], 2 * i + 2)
                nc.scalar.activation(Ps[:, i % 2, :], Ps[:, i % 2, :], ACT.Copy, scale=ssm[:, 3, i:i + 1])\
                    .then_inc(S["ss_N"], 1)
                for c in range(5):
                    n = 512 if c < 4 else 128
                    k = 5 * i + c
                    act.wait_ge(S["ss_T"], k + 1)
                    if k >= 2:
                        act.wait_ge(S["ss_c"], k - 1)
                    pr = P if c < 4 else NS
                    nc.scalar.activation(PTs[0:pr, k % 2, 0:n], bank(5 + k % 2, n, p1=pr), ACT.Copy)\
                        .then_inc(S["ss_PT"], 1)
                    if c >= 1 and i + 2 >= NB // 2 and i + 2 < NB:
                        load_kv(act, i + 2, [x for x in ACT_PAGES if x[1] // 4 == c - 1], kv_act)
            norm_scale("mem")
            norm_scale("xmem")
            act.wait_ge(S["mkT_tp"], 1)
            nc.scalar.activation(mkT, bank(6).rearrange("p (a r) -> p a r", a=2), ACT.Copy)\
                .then_inc(S["mkT_ev"], 1)
            for c in range(2):
                act.wait_ge(S["qx_mm"], c + 1)
                nc.scalar.activation(qxT[:, c, :], bank(2 + 2 * c, NTOK), ACT.Copy).then_inc(S["qx_ev"], 1)
            attention(n_self, n_self + n_cross)

        @block.vector
        def _(dve):
            V = nc.vector
            dve.wait_ge(S["cst_in"], 16)
            V.tensor_copy(id16[:], ident).then_inc(S["c16"], 1)
            V.tensor_copy(causal16[:], causal).then_inc(S["c16"], 1)
            V.tensor_copy(same16[:].rearrange("p b c -> p (b c)"), same).then_inc(S["c16"], 1)

            def norm_gain(stage):
                base, n, g = NORM[stage]
                for t in range(n):
                    u, R = base + t, nrows(stage, t)
                    for half in range(2):
                        dve.wait_ge(S["tp_done"], 2 * u + half + 1)
                        gain = gcol[:, g + 4 * half:g + 4 * half + 4].unsqueeze(2).broadcast_to([P, 4, R])
                        V.tensor_tensor(dst_of(stage, t)[:, 4 * half:4 * half + 4, :],
                                        bank(half, 4 * R).rearrange("p (a r) -> p a r", a=4), gain, ALU.mult)\
                            .then_inc(S["xT_done"], 1)

            dve.wait_ge(S["gk_in"], 32)
            norm_gain("mix")
            chain = [0]

            def rope(eng_sem, R, t, x, out, nh, half):
                n = nh * 2 * half
                step = 32 // half
                cc = cosT[0:R, t, :].rearrange("p (a c) -> p a c", a=2)[:, :, 0:32:step]
                ss = sinT[0:R, t, :].rearrange("p (a c) -> p a c", a=2)[:, :, 0:32:step]
                x4 = x.rearrange("p (h a c) -> p h a c", h=nh, a=2)
                A = ropeA[0:R, 0:n].rearrange("p (h a c) -> p h a c", h=nh, a=2)
                M = ropeM[0:R, 0:n].rearrange("p (h a c) -> p h a c", h=nh, a=2)
                for a in range(2):
                    V.tensor_tensor(A[:, :, a, :], x4[:, :, a, :],
                                    cc[:, a, :].unsqueeze(1).broadcast_to([R, nh, half]), ALU.mult)\
                        .then_inc(S[eng_sem], 1)
                    V.tensor_tensor(M[:, :, a, :], x4[:, :, 1 - a, :],
                                    ss[:, a, :].unsqueeze(1).broadcast_to([R, nh, half]), ALU.mult)\
                        .then_inc(S[eng_sem], 1)
                chain[0] += 4
                dve.wait_ge(S[eng_sem], chain[0])
                return V.tensor_tensor(out, ropeA[0:R, 0:n], ropeM[0:R, 0:n], ALU.add)

            for t in range(NBLK):
                R = rows(t)
                for c in (2, 3):
                    dve.wait_ge(S["pj_mm"], 4 * t + c + 1)
                    V.tensor_copy(proj[0:R, t, c * PC:(c + 1) * PC], bank(2 + c, PC, p1=R))\
                        .then_inc(S["pj_dve"], 1)
                dve.wait_ge(S["pj_dve"], 2 * t + 2)
                dve.wait_ge(S["pj_act"], 2 * t + 2)
                for x0, nh, half in ((DQ, 10, 32), (IQ, 8, 32), (IK, 1, 32), (KR, 1, 16)):
                    n = nh * 2 * half
                    last = rope("qr_chain", R, t, proj[0:R, t, x0:x0 + n], proj[0:R, t, x0:x0 + n], nh, half)
                    if x0 != KR:
                        last.then_inc(S["qr_chain"], 1)
                        chain[0] += 1
                        dve.wait_ge(S["qr_chain"], chain[0])
                    else:
                        last.then_inc(S["rp_dve"], 1)
                        dve.wait_ge(S["rp_dve"], t + 1)
                dve.wait_ge(S["rstd2_done"], t + 1)
                V.scalar_tensor_tensor(out=proj[0:R, t, CKV:CKV + 128], in0=proj[0:R, t, CKV:CKV + 128],
                                       scalar=st[0:R, 141 + 2 * t:142 + 2 * t], in1=gkv[0:R, :],
                                       op0=ALU.mult, op1=ALU.mult).then_inc(S["ckv_done"], 1)
                dve.wait_ge(S["tB_mm"], 2 * t + 1)
                gain = gcol[:, 4 * KD:4 * KD + 2].unsqueeze(2).broadcast_to([P, 2, R])
                V.tensor_tensor(cqT[:, :, toks(t)], bank(7, 2 * R).rearrange("p (a r) -> p a r", a=2), gain,
                                ALU.mult).then_inc(S["tB_ev"], 1)
                dve.wait_ge(S["tB_mm"], 2 * t + 2)
                if t < 4:
                    V.tensor_copy(iqT[:, :, toks(t)], bank(7).rearrange("p (a r) -> p a r", a=4))\
                        .then_inc(S["tB_ev"], 1)
                else:
                    for j in range(2):
                        last = V.tensor_copy(iqTs[64 * j:64 * j + 64].rearrange("p b h t -> p h b t"),
                                             bank(7, p1=64).rearrange("p (h b t) -> p h b t", h=8, b=NB))
                    last.then_inc(S["tB_ev"], 1)
            dve.wait_ge(S["tA_ev"], 2 * NBLK)
            dve.wait_ge(S["c16"], 4)
            for g in range(2):
                V.tensor_copy(bdq[64 * g:64 * g + 64, :, g, :, :].rearrange("p b n t -> p n b t"),
                              dqT[64 * g:64 * g + 64, :, SEQ:NTOK].rearrange("p n (b t) -> p n b t", b=NB))
            for hd in range(8):
                dve.wait_ge(S["ql_mm"], hd + 1)
                o = 2 * (hd % 2) * BANK
                V.tensor_copy(qlT[:, hd, :], PS[:, o:o + SEQ]).then_inc(S["ql_ev"], 1)
                V.tensor_copy(qlTs[:, :, hd, :],
                              PS[:, o + SEQ:o + NTOK].rearrange("p (b t) -> p b t", b=NB))\
                    .then_inc(S["ql_ev"], 1)
            for t in range(NBLK):
                R = rows(t)
                dve.wait_ge(S["qr_mm"], t + 1)
                if t >= 1:
                    dve.wait_ge(S["qr_tp"], t)
                rope("qr_chain", R, t, bank(4 + t % 2, 256, p1=R), qr[0:R, :], 8, 16)\
                    .then_inc(S["qr_done"], 1)
                dve.wait_ge(S["qr_done"], t + 1)
                dve.wait_ge(S["qr_tp"], t + 1)
                if t < 4:
                    V.tensor_copy(qrT[:, :, toks(t)], bank(7, 2 * R).rearrange("p (a r) -> p a r", a=2))\
                        .then_inc(S["qr_ev"], 1)
                else:
                    for p in range(NB // 2):
                        last = V.tensor_copy(qrTs[32 * p:32 * p + 32].rearrange("p b (h t) -> p h b t", h=8),
                                             bank(7, p1=32).rearrange("p (h b t) -> p h b t", h=8, b=NB)
                                             [:, :, 2 * p:2 * p + 2, :])
                    last.then_inc(S["qr_ev"], 1)
            V.tensor_copy(mb16[:, 0, 0:P], causal).then_inc(S["mask_done"], 1)
            for i in range(24):
                t, hd = i // 8 + 1, i % 8
                L = P * (t + 1)
                acc = accs[:, t - 1, 0:L]
                iw = proj[:, t, IW + hd:IW + hd + 1]
                dve.wait_ge(S["ix_relu"], i + 1)
                if hd == 0:
                    V.tensor_scalar(acc, relu[:, i % 2, 0:L], iw, None, ALU.mult).then_inc(S["ix_acc"], 1)
                else:
                    dve.wait_ge(S["ix_acc"], i)
                    V.scalar_tensor_tensor(out=acc, in0=relu[:, i % 2, 0:L], scalar=iw, in1=acc,
                                           op0=ALU.mult, op1=ALU.add).then_inc(S["ix_acc"], 1)

            taken = [0]

            def top_k(x, m, k):
                base = taken[0]
                with dve.Fori(0, k // 8) as r:
                    V.max(m, x).then_inc(S["tk"], 1)
                    dve.wait_ge(S["tk"], base + 2 * r + 1)
                    dve.nop(nofuse=True)
                    V.match_replace(x, m, x, TAKEN).then_inc(S["tk"], 1)
                    dve.wait_ge(S["tk"], base + 2 * r + 2)
                    dve.nop(nofuse=True)
                taken[0] += 2 * (k // 8)

            def prompt_top_k(s):
                t, part = s // 8 + 1, s % 8
                L = P * (t + 1)
                acc = accs[:, t - 1, 0:L]
                if part == 0:
                    dve.wait_ge(S["ix_acc"], 8 * t)
                    V.tensor_tensor(acc[:, L - P:L], acc[:, L - P:L], causal, ALU.add).then_inc(S["tk"], 1)
                    taken[0] += 1
                    dve.wait_ge(S["tk"], taken[0])
                for r in range(K_PROMPT // 8 // 8):
                    V.max(m8[:], acc).then_inc(S["tk"], 1)
                    dve.wait_ge(S["tk"], taken[0] + 1)
                    V.match_replace(acc, m8[:], acc, TAKEN).then_inc(S["tk"], 1)
                    dve.wait_ge(S["tk"], taken[0] + 2)
                    taken[0] += 2
                if part == 7:
                    V.tensor_scalar(mb16[:, t, 0:L], acc, -2e38, NEG, ALU.is_ge, ALU.mult)\
                        .then_inc(S["mask_done"], 1)

            def softmax_max(i, u):
                L = keys_of(u)
                dve.wait_ge(S["at_S"], i + 1)
                V.reduce_max(sm[:, i:i + 1], bank(i % 2, L), AX).then_inc(S["at_c"], 1)
                dve.wait_ge(S["at_c"], at_count())
                V.tensor_scalar(sm[:, 100 + i:101 + i], sm[:, i:i + 1], -scale_of(u), None, ALU.mult)\
                    .then_inc(S["at_nb"], 1)

            counts = {"c": 0}

            def at_count():
                counts["c"] += 1
                return counts["c"]

            def softmax_norm(i, u):
                L = keys_of(u)
                dve.wait_ge(S["at_exp"], i + 1)
                V.reciprocal(sm[:, 300 + i:301 + i], sm[:, 200 + i:201 + i]).then_inc(S["at_c"], 1)
                dve.wait_ge(S["at_c"], at_count())
                V.tensor_scalar(Pr[:, i % 3, 0:L], Pr[:, i % 3, 0:L], sm[:, 300 + i:301 + i], None, ALU.mult)\
                    .then_inc(S["at_P"], 1)

            def heads_out(i, u):
                kind, t, hd = u
                dve.wait_ge(S["at_O"], i + 1)
                if kind in ("mla", "dsa"):
                    j, c = (hd % 2, hd // 2) if kind == "mla" else (hd // 4, 4 + hd % 4)
                    V.tensor_copy(xT[64 * j:64 * j + 64, c, toks(t)], bank(4 + i % 2, P, p0=64 * j, p1=64 * j + 64))\
                        .then_inc(S["at_oe"], 1)
                elif kind == "mem":
                    j, c = hd % 2, hd // 2
                    V.tensor_copy(oxT[64 * j:64 * j + 64, c, toks(t)], bank(4 + i % 2, P, p0=64 * j, p1=64 * j + 64))\
                        .then_inc(S["at_oe"], 1)
                else:
                    for c in range(2):
                        for j in range(2):
                            o = PS[64 * j:64 * j + 64, (4 + i % 2) * BANK + c * P:(4 + i % 2) * BANK + (c + 1) * P]
                            o = o.rearrange("p (b n t) -> p b n t", b=4, n=4)[:, :, 2 * c + j, :]
                            d = oxT[64 * j:64 * j + 64, c, SEQ + 32 * hd:SEQ + 32 * hd + 32]
                            last = V.tensor_copy(d.rearrange("p (b t) -> p b t", b=4), o)
                    last.then_inc(S["at_oe"], 1)

            def attention(lo, hi):
                for s in range(lo, hi + 3):
                    if s < hi:
                        softmax_max(s, UNITS[s])
                    if lo <= s - 1 < hi:
                        softmax_norm(s - 1, UNITS[s - 1])
                    if s - 3 >= lo:
                        heads_out(s - 3, UNITS[s - 3])
                    if s < 24:
                        prompt_top_k(s)

            dve.wait_ge(S["tA_ev"], 2 * NBLK)
            attention(0, n_self)

            dve.wait_ge(S["c16"], 4)
            dve.wait_ge(S["out_st"], 16 * 4 * NBLK)
            V.tensor_tensor(selE, same.rearrange("p (b h t) -> p b h t", b=NB, h=8),
                            proj[0:NS, 4, IW:IW + 8].unsqueeze(1).unsqueeze(3).broadcast_to([NS, NB, 8, NQ]),
                            ALU.mult).then_inc(S["sel_E"], 1)
            dve.wait_ge(S["sel_T"], 1)
            V.tensor_copy(Dp[:], bank(7, 256).rearrange("p (a c) -> p a c", a=4)).then_inc(S["sel_D"], 1)
            dve.wait_ge(S["xi_sc"], 20)
            V.tensor_copy(sw[:, 0:PAST], PS[0:NS, 0:PAST]).then_inc(S["sw_done"], 1)
            V.tensor_tensor(sw[:, PAST:NEWC], PS[0:NS, PAST:NEWC], cst[0:NS, C_NEW:C_NEW + NS], ALU.add)\
                .then_inc(S["sw_done"], 1)
            dve.wait_ge(S["sw_done"], 2)

            def own_values(i):
                kind, p = SMP[i]
                if kind == 0:
                    V.tensor_copy(olT[:, 2 * p:2 * p + 2, :, :].rearrange("p b h t -> p (b h t)"), bank(7, P))\
                        .then_inc(S["ss_oe"], 1)
                else:
                    for g in range(2):
                        for b2 in range(2):
                            o = bank(7, 64, 64 * b2, p0=64 * g, p1=64 * g + 64)
                            o = o.rearrange("p (g n t) -> p g n t", g=2, n=4)[:, g, :, :]
                            c0 = SEQ + NQ * (2 * p + b2)
                            last = V.tensor_copy(xT[64 * g:64 * g + 64, 4:8, c0:c0 + NQ], o)
                    last.then_inc(S["ss_oe"], 1)

            def rounds(n):
                top_k(sw, m8[0:NS, :], 8 * n)

            before, exp_time = 3, 1
            rest = K_SAMPLE // 8 - before
            for i in range(NB):
                kind, p = SMP[i]
                if i == 0:
                    rounds(before)
                if i == NB // 2:
                    dve.wait_ge(S["qr_ev"], NBLK)
                    V.tensor_scalar(mbs, sw, -2e38, NEG, ALU.is_ge, ALU.mult).then_inc(S["mbs_done"], 1)
                dve.wait_ge(S["ss_S"], i + 1)
                V.reduce_max(ssm[:, 0, i:i + 1], PS[:, 0:NEWC], AX).then_inc(S["ss_P"], 1)
                dve.wait_ge(S["ss_P"], 2 * i + 1)
                V.tensor_scalar(ssm[:, 1, i:i + 1], ssm[:, 0, i:i + 1], -(MLA_SCALE, DSA_SCALE)[kind],
                                None, ALU.mult).then_inc(S["ss_nb"], 1)
                if kind == 0:
                    rounds(exp_time)
                    rest -= exp_time
                dve.wait_ge(S["ss_exp"], i + 1)
                V.reciprocal(ssm[:, 3, i:i + 1], ssm[:, 2, i:i + 1])\
                    .then_inc(S["ss_P"], 1)
                if i >= 1:
                    dve.wait_ge(S["ss_c"], 5 * i)
                    own_values(i - 1)
                if kind == 0:
                    n = rest // (NB // 2 - i)
                    rounds(n)
                    rest -= n
            dve.wait_ge(S["ss_c"], 5 * NB)
            own_values(NB - 1)
            for hd in range(8):
                j, c = hd % 2, hd // 2
                dve.wait_ge(S["uv_mm"], 1)
                V.tensor_copy(xT[64 * j:64 * j + 64, c, SEQ:NTOK], bank(5 + j, NS, NS * c, p0=64 * j, p1=64 * j + 64))\
                    .then_inc(S["uv_ev"], 1)
            for i in range(2 * NBLK):
                t, half = divmod(i, 2)
                R = rows(t)
                dve.wait_ge(S["wo_mm"], i + 1)
                hs = h[0:R, t, 512 * half:512 * half + 512]
                V.tensor_tensor(hs, bank(2 + i % 2, p1=R), hs, ALU.add).then_inc(S["h_done"], 1)
            norm_gain("mem")
            for t in range(2):
                dve.wait_ge(S["mkv_mm"], t + 1)
                V.tensor_copy(mkv[:, t, :], bank(4 + t)).then_inc(S["mkv_ev"], 1)
            norm_gain("xmem")
            V.memset(bdx, 0.0).then_inc(S["bdx_done"], 1)
            dve.wait_ge(S["bdx_done"], 1)
            dve.wait_ge(S["qx_ev"], 2)
            for c in range(2):
                for j in range(2):
                    V.tensor_copy(bdx[64 * j:64 * j + 64, c, :, 2 * c + j, :],
                                  qxT[64 * j:64 * j + 64, c, SEQ:NTOK].rearrange("p (b t) -> p b t", b=NB))\
                        .then_inc(S["bdx_done"], 1)
            attention(n_self, n_self + n_cross)
            for i in range(2 * NBLK):
                t, half = divmod(i, 2)
                R = rows(t)
                dve.wait_ge(S["ox_mm"], i + 1)
                hs = h[0:R, t, 512 * half:512 * half + 512]
                V.tensor_tensor(hs, bank(i % 2, p1=R), hs, ALU.add).then_inc(S["hx_done"], 1)
            dve.wait_ge(S["hx_done"], 2 * NBLK)

        @block.tensor
        def _(pe):
            M = nc.tensor.matmul
            TR = nc.tensor.transpose

            def norm_transpose(stage):
                base, n, _ = NORM[stage]
                for t in range(n):
                    u, R = base + t, nrows(stage, t)
                    pe.wait_ge(S["xs_done"], u + 1)
                    for half in range(2):
                        if u >= 1:
                            pe.wait_ge(S["xT_done"], 2 * (u - 1) + half + 1)
                        for a in range(4):
                            c = 4 * half + a
                            last = TR(bank(half, R, a * R), xs[0:R, u % 2, c * P:(c + 1) * P], ident[0:R, 0:R])
                        last.then_inc(S["tp_done"], 1)

            pe.wait_ge(S["cst_in"], 16)
            norm_transpose("mix")
            pe.wait_ge(S["win_in"], 16 * KD)

            def project(t):
                R = rows(t)
                pe.wait_ge(S["xT_done"], 2 * (t + 1))
                for c in range(4):
                    if t >= 1:
                        pe.wait_ge(S["pj_act"] if c < 2 else S["pj_dve"], 2 * (t - 1) + c % 2 + 1)
                    for k in range(KD):
                        last = M(bank(2 + c, PC, p1=R), xT[:, k, toks(t)], win[:, k, c * PC:(c + 1) * PC],
                                 start=(k == 0), stop=(k == KD - 1))
                    last.then_inc(S["pj_mm"], 1)

            def transposes(t):
                R = rows(t)
                I = ident[0:R, 0:R]
                pe.wait_ge(S["ckv_done"], t + 1)
                pe.wait_ge(S["rp_pool"], t + 1)
                if t >= 1:
                    pe.wait_ge(S["tA_ev"], 2 * t)
                for a, src in enumerate((proj[0:R, t, CKV:CKV + P], kk[0:R, 0:128],
                                         proj[0:R, t, DK:DK + P], kk[0:R, 128:256])):
                    last = TR(bank(6, R, a * R), src, I)
                last.then_inc(S["tA_mm"], 1)
                pe.wait_ge(S["cq_done"], t + 1)
                if t >= 1:
                    pe.wait_ge(S["tB_ev"], 2 * t)
                for a in range(2):
                    last = TR(bank(7, R, a * R), proj[0:R, t, CQ + a * P:CQ + (a + 1) * P], I)
                last.then_inc(S["tB_mm"], 1)
                pe.wait_ge(S["tA_ev"], 2 * t + 1)
                for a in range(4):
                    last = TR(bank(6, R, a * R), proj[0:R, t, DQ + a * P:DQ + (a + 1) * P], I)
                last.then_inc(S["tA_mm"], 1)
                pe.wait_ge(S["tB_ev"], 2 * t + 1)
                if t < 4:
                    for a in range(4):
                        last = TR(bank(7, R, a * R), proj[0:R, t, IQ + a * P:IQ + (a + 1) * P], I)
                else:
                    for a in range(8):
                        last = TR(bank(7, R, a * R, p1=64), proj[0:R, t, IQ + a * 64:IQ + (a + 1) * 64], I)
                last.then_inc(S["tB_mm"], 1)

            for t in range(NBLK + 1):
                if t < NBLK:
                    project(t)
                if t >= 1:
                    transposes(t - 1)
            pe.wait_ge(S["wsm_in"], 64)
            pe.wait_ge(S["tB_ev"], 2 * NBLK)
            pe.wait_ge(S["pj_act"], 2 * NBLK)
            pe.wait_ge(S["pj_dve"], 2 * NBLK)
            for p in range(4):
                if p >= 2:
                    pe.wait_ge(S["up_ev"], p - 1)
                for lo, hi in ((0, SEQ), (SEQ, NTOK)):
                    for c in range(2):
                        o = 2 * (p % 2) * BANK
                        last = M(PS[:, o + lo:o + hi], w_uqn[:, c, p * P:(p + 1) * P], cqT[:, c, lo:hi],
                                 start=(c == 0), stop=(c == 1))
                last.then_inc(S["up_mm"], 1)
            for hd in range(8):
                j, p = hd % 2, hd // 2
                pe.wait_ge(S["up_ev"], 4)
                if hd >= 2:
                    pe.wait_ge(S["ql_ev"], 2 * (hd - 1))
                for lo, hi in ((0, SEQ), (SEQ, NTOK)):
                    o = 2 * (hd % 2) * BANK
                    last = M(PS[:, o + lo:o + hi], w_ukT[64 * j:64 * j + 64, p, :],
                             qnT[64 * j:64 * j + 64, p, lo:hi], start=True, stop=True)
                last.then_inc(S["ql_mm"], 1)
            for t in range(NBLK):
                R = rows(t)
                if t >= 2:
                    pe.wait_ge(S["qr_done"], t - 1)
                for c in range(2):
                    last = M(bank(4 + t % 2, 256, p1=R), cqT[:, c, toks(t)], w_uqr[:, c, :],
                             start=(c == 0), stop=(c == 1))
                last.then_inc(S["qr_mm"], 1)
                pe.wait_ge(S["qr_done"], t + 1)
                if t >= 1:
                    pe.wait_ge(S["qr_ev"], t)
                I = ident[0:R, 0:R]
                if t < 4:
                    for a in range(2):
                        last = TR(bank(7, R, a * R), qr[0:R, a * P:(a + 1) * P], I)
                else:
                    for a in range(8):
                        last = TR(bank(7, R, a * R, p1=32), qr[0:R, a * 32:(a + 1) * 32], I)
                last.then_inc(S["qr_tp"], 1)
            pe.wait_ge(S["qr_ev"], NBLK)
            pe.wait_ge(S["tA_ev"], 2 * NBLK)
            for t in range(4):
                if t >= 2:
                    pe.wait_ge(S["vm_ev"], t - 1)
                M(bank(6 + t % 2), kT[:, 0, toks(t)], w_uv, start=True, stop=True).then_inc(S["vm_mm"], 1)
            for i in range(24):
                t, hd = i // 8 + 1, i % 8
                L, j, p = P * (t + 1), hd % 2, hd // 2
                if i >= 2:
                    pe.wait_ge(S["ix_relu"], i - 1)
                M(bank(4 + i % 2, L), iqT[64 * j:64 * j + 64, p, toks(t)], kT[64 * j:64 * j + 64, 3, 0:L],
                  start=True, stop=True).then_inc(S["ix_mm"], 1)

            def scores(i, u):
                kind, t, hd = u
                L = keys_of(u)
                if i >= 2:
                    pe.wait_ge(S["at_exp"], i - 1)
                b = i % 2
                if kind == "mla":
                    r, c = hd % 4, hd // 4
                    M(bank(b, L), qlT[:, hd, toks(t)], kT[:, 0, 0:L], start=True, stop=False)
                    M(bank(b, L), qrT[32 * r:32 * r + 32, c, toks(t)], kT[32 * r:32 * r + 32, 1, 0:L],
                      start=False, stop=False)
                    last = M(bank(b, P, L - P), id16[:], causal16[:], start=False, stop=True)
                elif kind == "dsa":
                    g, n = hd // 4, hd % 4
                    pe.wait_ge(S["mask_done"], t + 1)
                    M(bank(b, L), dqT[64 * g:64 * g + 64, n, toks(t)], kT[64 * g:64 * g + 64, 2, 0:L],
                      start=True, stop=False)
                    last = M(bank(b, L), id16[:], mb16[:, t, 0:L], start=False, stop=True)
                elif kind == "mem":
                    j, c = hd % 2, hd // 2
                    last = M(bank(b, L), qxT[64 * j:64 * j + 64, c, toks(t)], mkT[64 * j:64 * j + 64, c, :],
                             start=True, stop=True)
                else:
                    for b4 in range(4):
                        bb = 4 * hd + b4
                        for c in range(2):
                            last = M(bank(b, L, p0=32 * b4, p1=32 * b4 + 32),
                                     bdx[:, c, bb, :, :].rearrange("p n t -> p (n t)"), xc[:, bb, c, :],
                                     start=(c == 0), stop=(c == 1))
                last.then_inc(S["at_S"], 1)

            def turn_probs(i, u):
                L = keys_of(u)
                pe.wait_ge(S["at_P"], i + 1)
                if i >= 2:
                    pe.wait_ge(S["at_PT"], i - 1)
                for a in range(L // P):
                    last = TR(bank(2 + i % 2, P, a * P), Pr[:, i % 3, a * P:(a + 1) * P], ident)
                last.then_inc(S["at_T"], 1)

            def values(i, u):
                kind, t, hd = u
                L = keys_of(u)
                nk = L // P
                pe.wait_ge(S["at_PT"], i + 1)
                if i >= 2:
                    pe.wait_ge(S["at_oe"], i - 1)
                if kind == "smp":
                    for b4 in range(4):
                        bb = 4 * hd + b4
                        for c in range(2):
                            for k in range(2):
                                last = M(bank(4 + i % 2, 32, c * P + 32 * b4), xc[:, bb, 2 + k, c * P:(c + 1) * P],
                                         PT[:, i % 2, k * P + 32 * b4:k * P + 32 * b4 + 32],
                                         start=(k == 0), stop=(k == 1))
                    last.then_inc(S["at_O"], 1)
                    return
                j = hd // 4 if kind == "dsa" else hd % 2
                for k in range(nk):
                    if kind == "mla":
                        v = Vm[:, k, hd * 64:hd * 64 + 64]
                    elif kind == "dsa":
                        v = proj[:, k, DV + 64 * j:DV + 64 * j + 64]
                    else:
                        v = mkv[:, k, 256 + 64 * hd:256 + 64 * hd + 64]
                    last = M(bank(4 + i % 2, P, p0=64 * j, p1=64 * j + 64), v, PT[:, i % 2, k * P:(k + 1) * P],
                             start=(k == 0), stop=(k == nk - 1))
                last.then_inc(S["at_O"], 1)

            def attention(lo, hi):
                for s in range(lo, hi + 3):
                    if s < hi:
                        scores(s, UNITS[s])
                    if lo <= s - 2 < hi:
                        turn_probs(s - 2, UNITS[s - 2])
                    if s - 3 >= lo:
                        values(s - 3, UNITS[s - 3])

            pe.wait_ge(S["vm_ev"], 4)
            pe.wait_ge(S["c16"], 4)
            pe.wait_ge(S["ix_relu"], 24)
            pe.wait_ge(S["ql_ev"], 16)
            attention(0, n_self)

            pe.wait_ge(S["sel_E"], 1)
            for p in range(4):
                last = TR(bank(7, NS, p * NS), selE[:, 2 * p:2 * p + 2, :, :].rearrange("p b h t -> p (b h t)"),
                          ident[0:NS, 0:NS])
            last.then_inc(S["sel_T"], 1)
            pe.wait_ge(S["sel_D"], 1)
            pe.wait_ge(S["at_oe"], n_self)
            pe.wait_ge(S["at_PT"], n_self)

            def head_sum(i):
                p, kc = divmod(i, 5)
                n = 512 if kc < 4 else NS
                pe.wait_ge(S["xi_relu"], i + 1)
                M(bank(kc, n, p1=NS), Dp[:, p, :], relus[:, i % 2, 0:n], start=(p == 0), stop=(p == 3),
                  skip_group_check=True).then_inc(S["xi_sc"], 1)

            pe.wait_ge(ik_sp, 16 * NB * IK_SP)
            pe.wait_ge(ik_pool, 16 * NB * (NPAGE - IK_SP))
            for i in range(20):
                p, kc = divmod(i, 5)
                n = 512 if kc < 4 else NS
                if i >= 2:
                    pe.wait_ge(S["xi_relu"], i - 1)
                for b2 in range(2):
                    H = slice(64 * b2, 64 * b2 + 64)
                    q = iqTs[H, 2 * p + b2, :, :].rearrange("p h t -> p (h t)")
                    k = ikT[H, p, kc * 512:kc * 512 + 512] if kc < 4 else kT[H, 3, SEQ:NTOK]
                    last = M(bank(5 + i % 2, n, p0=64 * b2, p1=64 * b2 + 64), q, k, start=True, stop=True)
                last.then_inc(S["xi_mm"], 1)
                if i >= 1:
                    head_sum(i - 1)
            head_sum(19)

            def pair_scores(i):
                kind, p = SMP[i]
                slot = (i + 1) % 2
                pe.wait_ge(kv_sp[slot], 16 * (len(PAGES) * min(i // 2 + 1, 2) + len(SP_PAGES) * max(i // 2 - 1, 0)))
                if kind == 0:
                    pe.wait_ge(kr_in[p], 16 * 2 * NPAGE)
                else:
                    pe.wait_ge(kv_pool[slot], 16 * len(POOL_PAGES) * (i // 2 - 1))
                    pe.wait_ge(kv_act[slot], 16 * len(ACT_PAGES) * (i // 2 - 1))
                if i >= 1:
                    pe.wait_ge(S["ss_exp"], i)
                else:
                    pe.wait_ge(S["sw_done"], 2)
                if kind == 1:
                    pe.wait_ge(S["mbs_done"], 1)
                for b2 in range(2):
                    b = 2 * p + b2
                    for kc in range(5):
                        n = 512 if kc < 4 else NS
                        out = bank(kc, n, p0=64 * b2, p1=64 * b2 + 64)
                        if kind == 0:
                            ql = qlTs[:, b, :, :].rearrange("p h t -> p (h t)")
                            for a in range(4 if kc < 4 else 1):
                                if kc < 4:
                                    o = bank(kc, PAGE, a * PAGE, p0=64 * b2, p1=64 * b2 + 64)
                                    k = KV[:, slot, b2, 4 * kc + a, 0:128]
                                else:
                                    o, k = out, kT[:, 0, SEQ:NTOK]
                                M(o, ql, k, start=(a == 0), stop=False, skip_group_check=True)
                            G = slice(32 * p, 32 * p + 32)
                            k = krT[G, b2, kc * 512:kc * 512 + 512] if kc < 4 else kT[G, 1, SEQ:NTOK]
                            last = M(out, qrTs[G, b2, :], k, start=False, stop=(kc < 4), skip_group_check=True)
                            if kc == 4:
                                last = M(out, same[:, 64 * b:64 * b + 64], cst[0:NS, C_NEW:C_NEW + NS],
                                         start=False, stop=True, skip_group_check=True)
                        else:
                            q = bdq[:, b, :, :, :].rearrange("p g n t -> p (g n t)")
                            for a in range(4 if kc < 4 else 1):
                                if kc < 4:
                                    o = bank(kc, PAGE, a * PAGE, p0=64 * b2, p1=64 * b2 + 64)
                                    k = KV[:, slot, b2, 4 * kc + a, 0:128]
                                else:
                                    o, k = out, kT[:, 2, SEQ:NTOK]
                                M(o, q, k, start=(a == 0), stop=False, skip_group_check=True)
                            last = M(out, same16[:, b, :], mbs[:, kc * 512:kc * 512 + n], start=False, stop=True,
                                     skip_group_check=True)
                last.then_inc(S["ss_S"], 1)

            def turn_pair(i, c):
                k = 5 * i + c
                pe.wait_ge(S["ss_N"], i + 1)
                if k >= 2:
                    pe.wait_ge(S["ss_PT"], k - 1)
                if c < 4:
                    for a in range(4):
                        c0 = 512 * c + a * P
                        last = TR(bank(5 + k % 2, P, a * P), Ps[:, i % 2, c0:c0 + P], ident)
                else:
                    last = TR(bank(5 + k % 2, P, 0, p1=NS), Ps[:, i % 2, PAST:NEWC], ident)
                last.then_inc(S["ss_T"], 1)

            def pair_values(i, c):
                kind, p = SMP[i]
                k = 5 * i + c
                pe.wait_ge(S["ss_PT"], k + 1)
                if c == 0 and i >= 1:
                    pe.wait_ge(S["ss_oe"], i)
                for b2 in range(2):
                    out = bank(7, 64, 64 * b2)
                    first = (c == 0)
                    if c < 4:
                        for a in range(4):
                            v = KV[:, (i + 1) % 2, b2, 4 * c + a, 128:256]
                            last = M(out, v, PTs[:, k % 2, a * P + 64 * b2:a * P + 64 * b2 + 64],
                                     start=(first and a == 0 and b2 == 0), stop=False, skip_group_check=True)
                    else:
                        v = proj[0:NS, 4, (CKV, DV)[kind]:(CKV, DV)[kind] + P]
                        last = M(out, v, PTs[0:NS, k % 2, 64 * b2:64 * b2 + 64], start=False, stop=(b2 == 1),
                                 skip_group_check=True)
                last.then_inc(S["ss_c"], 1)

            for i in range(NB):
                if i <= NB // 2:
                    pair_scores(i)
                if NB // 2 <= i < NB - 1:
                    pair_scores(i + 1)
                for c in range(6):
                    if c < 5:
                        turn_pair(i, c)
                    if c >= 1:
                        pair_values(i, c - 1)
            pe.wait_ge(S["ss_oe"], NB)
            for hd in range(8):
                j, c = hd % 2, hd // 2
                last = M(bank(5 + j, NS, NS * c, p0=64 * j, p1=64 * j + 64), w_uv[:, hd * 64:hd * 64 + 64],
                         olT[:, :, hd, :], start=True, stop=True, skip_group_check=True)
            last.then_inc(S["uv_mm"], 1)
            pe.wait_ge(S["uv_ev"], 8)
            pe.wait_ge(S["wo_in"], 16)
            for i in range(2 * NBLK):
                t, half = divmod(i, 2)
                R = rows(t)
                if i >= 2:
                    pe.wait_ge(S["h_done"], i - 1)
                for k in range(KD):
                    last = M(bank(2 + i % 2, p1=R), xT[:, k, toks(t)], w_o[:, k, 512 * half:512 * half + 512],
                             start=(k == 0), stop=(k == KD - 1))
                last.then_inc(S["wo_mm"], 1)
            norm_transpose("mem")
            pe.wait_ge(S["late_in"], 48)
            for t in range(2):
                pe.wait_ge(S["xT_done"], 2 * (NORM["mem"][0] + t + 1))
                for k in range(KD):
                    last = M(bank(4 + t), mT[:, k, t * P:(t + 1) * P], wkv[:, k, :], start=(k == 0),
                             stop=(k == KD - 1))
                last.then_inc(S["mkv_mm"], 1)
            norm_transpose("xmem")
            pe.wait_ge(S["mkv_ev"], 2)
            for c in range(2):
                for t in range(2):
                    last = TR(bank(6, P, c * 256 + t * P), mkv[:, t, c * P:(c + 1) * P], ident)
            last.then_inc(S["mkT_tp"], 1)
            pe.wait_ge(S["xT_done"], 2 * STREAM_UNITS)
            for c in range(2):
                for lo, hi in ((0, SEQ), (SEQ, NTOK)):
                    for k in range(KD):
                        o = (2 + 2 * c) * BANK
                        last = M(PS[:, o + lo:o + hi], wqx[:, k, c * P:(c + 1) * P], xT[:, k, lo:hi],
                                 start=(k == 0), stop=(k == KD - 1))
                last.then_inc(S["qx_mm"], 1)
            pe.wait_ge(S["mkT_ev"], 1)
            pe.wait_ge(S["qx_ev"], 2)
            pe.wait_ge(S["bdx_done"], 5)
            attention(n_self, n_self + n_cross)
            pe.wait_ge(S["wox_in"], 16)
            pe.wait_ge(S["at_oe"], n_self + n_cross)
            for i in range(2 * NBLK):
                t, half = divmod(i, 2)
                R = rows(t)
                if i >= 2:
                    pe.wait_ge(S["hx_done"], i - 1)
                for c in range(2):
                    last = M(bank(i % 2, p1=R), oxT[:, c, toks(t)], wox[:, c, 512 * half:512 * half + 512],
                             start=(c == 0), stop=(c == 1))
                last.then_inc(S["ox_mm"], 1)


class Choice:

    def __init__(self, nc, ctx):
        def sb(name, shape, dt=F32):
            return ctx.enter_context(nc.sbuf_tensor(name, shape, dt))

        self.cst = sb("cstP", [P, 256])
        self.cst2 = sb("cst2P", [P, 2 * PK])
        self.ident, self.iota, self.iota16 = self.cst[:, 0:P], self.cst[:, P:2 * P], self.cst[:, P:P + PK]
        self.row0, self.step = self.cst2[:, 0:PK], sb("step16", [P, PK], BF16)
        self.mv = sb("mv", [P, NBLK - 2, 2 * PH, PK])
        self.mi = sb("mi", [P, NBLK - 2, 2 * PH, PK], U32)
        self.mf = sb("mf", [P, 2 * PH, PK], BF16)
        self.dI = sb("dI", [P, PH, PK], BF16)
        self.cand = sb("cand", [P, PH, NCAND])
        self.gv = sb("gv", [P, PH, PK])
        self.gi = sb("gi", [P, PH, PK], U32)
        self.gf = sb("gf", [P, 2, PH * PK])
        self.off = sb("off", [P, PH * PK])
        self.sel = sb("sel", [P, 3, PH * PK])
        self.gs = sb("gs", [P, 2, PH])
        self.sems = {n: ctx.enter_context(nc.semaphore("e_" + n))
                     for n in "tk ex_in ex_done sel_done sT_mm sT_act".split()}
        self.passes = 0


def end_pass(dve, C, ins):
    ins.then_inc(C.sems["tk"], 1)
    C.passes += 1
    dve.wait_ge(C.sems["tk"], C.passes)


def best8(V, dve, C, rows_, first):
    w = slice(0, 8) if first else slice(8, 16)
    for x, val, idx in rows_:
        last = V.max(val[:, w], x)
    end_pass(dve, C, last)
    for x, val, idx in rows_:
        last = V.max_index(idx[:, w], val[:, w], x)
    end_pass(dve, C, last)
    if first:
        for x, val, idx in rows_:
            last = V.match_replace(x, val[:, w], x, TAKEN)
        end_pass(dve, C, last)


CHOICE_PARTS = 12


def choice_part(V, dve, C, t, part, mv, mi, wide):
    R, S = rows(t), C.sems
    m4 = mv.rearrange("p (h a) k -> p h a k", a=2)[0:R]
    f4 = C.mf[0:R].rearrange("p (h a) k -> p h a k", a=2)
    g3 = C.sel[0:R, 2, :].rearrange("p (h k) -> p h k", h=PH)
    cands = [(C.cand[0:R, k, :], C.gv[0:R, k, :], C.gi[0:R, k, :]) for k in range(PH)]
    reached, hit, hit2 = (w[0:R] for w in wide)
    flat = "p h k c -> p (h k) c"

    def by_rank(x):
        return x.unsqueeze(1).broadcast_to([P, PH * PK, PK])[0:R]

    def by_place(x):
        return x.unsqueeze(2).broadcast_to([R, PH * PK, PK])

    def by_head(x):
        return x.unsqueeze(2).broadcast_to([R, PH, PK, PK])

    if part == 0:
        V.tensor_copy(C.mf[0:R], mi[0:R])
        for a, n, at in ROWS16[:8]:
            V.tensor_tensor(C.cand[0:R, :, at:at + n], m4[:, :, 0, a:a + 1].broadcast_to([R, PH, n]),
                            m4[:, :, 1, 0:n], ALU.add)
        end_pass(dve, C, V.tensor_tensor(C.cand[0:R, :, NCAND - 8:NCAND], m4[:, :, 0, 8:16],
                                         m4[:, :, 1, 0:1].broadcast_to([R, PH, 8]), ALU.add))
        V.tensor_copy(C.dI[0:R, :, 0:1], f4[:, :, 0, 0:1])
        V.tensor_tensor(C.dI[0:R, :, 1:PK], f4[:, :, 0, 1:PK], f4[:, :, 0, 0:PK - 1], ALU.subtract)
    elif part == 1:
        best8(V, dve, C, cands, True)
    elif part == 2:
        best8(V, dve, C, cands, False)
        if t >= 1:
            dve.wait_ge(S["sT_mm"], t)
        V.tensor_tensor(g3, C.gv[0:R], C.gv[0:R, :, 0:1].broadcast_to([R, PH, PK]), ALU.subtract)\
            .then_inc(S["ex_in"], 1)
        end_pass(dve, C, V.tensor_copy(C.gf[0:R, 0, :], C.gi[0:R].rearrange("p h k -> p (h k)")))
    elif part == 3:
        end_pass(dve, C, V.tensor_tensor(reached.rearrange(flat), by_place(C.gf[0:R, 0, :]), by_rank(C.row0),
                                         ALU.is_ge))
    elif part == 4:
        V.tensor_tensor(hit2.rearrange(flat), reached.rearrange(flat), by_rank(C.step[:]), ALU.mult)\
            .then_inc(S["tk"], 1)
    elif part == 5:
        V.tensor_tensor(hit, reached, by_head(C.dI[0:R]), ALU.mult).then_inc(S["tk"], 1)
        C.passes += 2
    elif part == 6:
        dve.wait_ge(S["tk"], C.passes)
        V.reduce_sum(C.off[0:R, :], hit2.rearrange(flat), AX).then_inc(S["tk"], 1)
    elif part == 7:
        V.reduce_sum(C.sel[0:R, 0, :], hit.rearrange(flat), AX).then_inc(S["tk"], 1)
        C.passes += 2
    elif part == 8:
        dve.wait_ge(S["tk"], C.passes)
        end_pass(dve, C, V.tensor_tensor(C.gf[0:R, 1, :], C.gf[0:R, 0, :], C.off[0:R, :], ALU.subtract))
        end_pass(dve, C, V.tensor_tensor(hit.rearrange(flat), by_place(C.gf[0:R, 1, :]), by_rank(C.iota16),
                                         ALU.is_equal))
    elif part == 9:
        end_pass(dve, C, V.tensor_tensor(hit, hit, by_head(f4[:, :, 1, :]), ALU.mult))
    elif part == 10:
        end_pass(dve, C, V.reduce_sum(C.sel[0:R, 1, :], hit.rearrange(flat), AX))
    else:
        dve.wait_ge(S["ex_done"], t + 1)
        end_pass(dve, C, V.reduce_sum(C.gs[0:R, 0, :], g3, AX))
        end_pass(dve, C, V.reciprocal(C.gs[0:R, 1, :], C.gs[0:R, 0, :]))
        V.tensor_tensor(g3, g3, C.gs[0:R, 1, :].unsqueeze(2).broadcast_to([R, PH, PK]), ALU.mult)\
            .then_inc(S["sel_done"], 1)


def choice_exp(A, act, C, t):
    act.wait_ge(C.sems["ex_in"], t + 1)
    A(C.sel[0:rows(t), 2, :], C.sel[0:rows(t), 2, :], ACT.Exp).then_inc(C.sems["ex_done"], 1)


def choice_turn(nc, pe, C, t, bank):
    R = rows(t)
    pe.wait_ge(C.sems["sel_done"], t + 1)
    if t >= 1:
        pe.wait_ge(C.sems["sT_act"], 3 * t)
    for a in range(3):
        last = nc.tensor.transpose(bank[:, a * P:a * P + R], C.sel[0:R, a, :], C.ident[0:R, 0:R])
    last.then_inc(C.sems["sT_mm"], 1)


def choice_out(A, act, C, t, bank, outs):
    act.wait_ge(C.sems["sT_mm"], t + 1)
    for a, out in enumerate(outs):
        A(out[:, toks(t)], bank[:, a * P:a * P + rows(t)], ACT.Copy).then_inc(C.sems["sT_act"], 1)


def peer_select(nc, T, h, sems, C, xh, xl, IT, JT, cT):
    ctx = ExitStack()
    with ctx:
        def sb(name, shape, dt=F32):
            return ctx.enter_context(nc.sbuf_tensor(name, shape, dt))

        PS = ctx.enter_context(nc.psum_tensor("psB", [P, 8 * BANK], F32))

        def bank(b, n=BANK, at=0, p0=0, p1=P):
            return PS[p0:p1, b * BANK + at:b * BANK + at + n]

        gcol = sb("gcolB", [P, KD])
        st = sb("stB", [P, 20])
        xs = sb("xsB", [P, 2, D])
        xf = sb("xfB", [P, 2, 4, P])
        keysT = sb("keysT", [P, 2 * PH, NKEY])
        wraw = sb("wraw", [P, 2, D])
        wh = sb("wh", [P, 2, D], F32R)
        wl = sb("wl", [P, 2, D], F32R)
        qT = sb("qT", [P, 2, NTOK])
        sc = sb("sc", [P, NBLK, 2 * PH, NKEY])
        mvA = sb("mvA", [P, 2, 2 * PH, PK])
        miA = sb("miA", [P, 2, 2 * PH, PK], U32)
        wide = [sb(f"wide{i}", [P, PH, PK, PK], BF16) for i in range(3)]
        ident = C.ident

        def best_of(t):
            return (mvA[:, t], miA[:, t]) if t < 2 else (C.mv[:, t - 2], C.mi[:, t - 2])

        names = """cst_in key_in sq_done ms_done rstd_done xs_done tp_done xf_done xh_done xl_done
            wh_done wl_done q_mm q_ev s_mm s_ev""".split()
        S = {n: sems.enter_context(nc.semaphore("b_" + n)) for n in names}
        w_in = [sems.enter_context(nc.semaphore(f"b_w_in{i}")) for i in range(2)]
        NHP = 2 * PH
        HT = NTOK // 2
        block = ctx.enter_context(nc.Block())

        @block.sync
        def _(sp):
            sp.dma_start(C.cst[:], T["cst"][:, 0:256]).then_inc(S["cst_in"], 16)
            sp.dma_start(C.cst2[:], T["cst"][:, C_FIRST:C_FIRST + 2 * PK]).then_inc(S["cst_in"], 16)
            sp.dma_start(gcol[:], T["gcol"][:, 3 * KD:4 * KD]).then_inc(S["cst_in"], 16)
            sp.dma_start(keysT[:], T["keysT"]).then_inc(S["key_in"], 16)
            for u in range(NHP):
                if u >= 2:
                    sp.wait_ge(S["wl_done"], u - 1)
                sp.dma_start(wraw[:, u % 2, :], T["w_pq"][u]).then_inc(w_in[u % 2], 16)

        @block.gpsimd
        def _(pool):
            pool.memset(st[:, 19:20], -0.5).then_inc(S["ms_done"], 1)
            for t in range(NBLK):
                R = rows(t)
                pool.wait_ge(S["sq_done"], t + 1)
                nc.gpsimd.tensor_scalar(st[0:R, 5 + t:6 + t], st[0:R, t:t + 1], 1.0 / D, EPS, ALU.mult, ALU.add)\
                    .then_inc(S["ms_done"], 1)
                pool.wait_ge(S["ms_done"], t + 2)
                nc.gpsimd.tensor_tensor(st[0:R, 10 + t:11 + t], st[0:R, 5 + t:6 + t], st[0:R, 19:20], ALU.pow)\
                    .then_inc(S["rstd_done"], 1)
            for u in range(NHP):
                pool.wait_ge(S["wh_done"], u + 1)
                if u >= 2:
                    pool.wait_ge(S["q_mm"], u - 1)
                nc.gpsimd.tensor_tensor(wl[:, u % 2, :], wraw[:, u % 2, :], wh[:, u % 2, :].bitcast(F32),
                                        ALU.subtract).then_inc(S["wl_done"], 1)

        @block.scalar
        def _(act):
            A = nc.scalar.activation

            def square(t):
                R = rows(t)
                if t >= 2:
                    act.wait_ge(S["tp_done"], 2 * (t - 1))
                A(xs[0:R, t % 2, :], h[0:R, t, :], ACT.Square, accum_out=st[0:R, t:t + 1])\
                    .then_inc(S["sq_done"], 1)

            def high_w(u):
                act.wait_ge(w_in[u % 2], 16 * (u // 2 + 1))
                if u >= 2:
                    act.wait_ge(S["q_mm"], u - 1)
                A(wh[:, u % 2, :], wraw[:, u % 2, :], ACT.Copy).then_inc(S["wh_done"], 1)

            square(0)
            for t in range(NBLK):
                R = rows(t)
                if t + 1 < NBLK:
                    square(t + 1)
                if t >= 3:
                    high_w(t - 3)
                act.wait_ge(S["rstd_done"], t + 1)
                A(xs[0:R, t % 2, :], h[0:R, t, :], ACT.Copy, scale=st[0:R, 10 + t:11 + t])\
                    .then_inc(S["xs_done"], 1)
                if t >= 1:
                    for half in range(2):
                        act.wait_ge(S["xf_done"], 2 * (t - 1) + half + 1)
                        A(xh[:, 4 * half:4 * half + 4, toks(t - 1)], xf[:, half, :, 0:P], ACT.Copy)\
                            .then_inc(S["xh_done"], 1)
            for half in range(2):
                act.wait_ge(S["xf_done"], 2 * (NBLK - 1) + half + 1)
                A(xh[:, 4 * half:4 * half + 4, toks(NBLK - 1)], xf[:, half, :, 0:NS], ACT.Copy)\
                    .then_inc(S["xh_done"], 1)
            for u in range(NHP + 2):
                if 2 <= u < NHP:
                    high_w(u)
                v = u - 1
                if 0 <= v < NHP:
                    act.wait_ge(S["q_mm"], v + 1)
                    if v >= 2:
                        act.wait_ge(S["s_mm"], v - 1)
                    A(qT[:, v % 2, :].rearrange("p (a n) -> p a n", a=2),
                      bank(2 + 2 * (v % 2), 2 * BANK).rearrange("p (a n) -> p a n", a=2)[:, :, 0:HT],
                      ACT.Copy).then_inc(S["q_ev"], 1)
                v = u - 2
                if v >= 0:
                    act.wait_ge(S["s_mm"], v + 1)
                    A(sc[:, 0:4, v, :], bank(6).rearrange("p (t k) -> p t k", t=4), ACT.Copy)\
                        .then_inc(S["s_ev"], 1)
                    A(sc[0:NS, 4, v, :], bank(7, P, p1=NS), ACT.Copy).then_inc(S["s_ev"], 1)
            for t in range(2):
                choice_exp(A, act, C, t)
                choice_out(A, act, C, t, bank(0), (IT, JT, cT))

        @block.vector
        def _(dve):
            V = nc.vector
            dve.wait_ge(S["cst_in"], 48)

            def low(t, half):
                R = rows(t)
                dve.wait_ge(S["xh_done"], 2 * t + half + 1)
                dst = (slice(None), slice(4 * half, 4 * half + 4), toks(t))
                V.tensor_tensor(xl[dst], xf[:, half, :, 0:R], xh[dst].bitcast(F32), ALU.subtract)\
                    .then_inc(S["xl_done"], 1)

            for t in range(NBLK):
                R = rows(t)
                for half in range(2):
                    if t >= 1:
                        low(t - 1, half)
                        dve.wait_ge(S["xl_done"], 2 * (t - 1) + half + 1)
                    dve.wait_ge(S["tp_done"], 2 * t + half + 1)
                    V.tensor_tensor(xf[:, half, :, 0:R], bank(half, 4 * R).rearrange("p (a r) -> p a r", a=4),
                                    gcol[:, 4 * half:4 * half + 4].unsqueeze(2).broadcast_to([P, 4, R]), ALU.mult)\
                        .then_inc(S["xf_done"], 1)
            for half in range(2):
                low(NBLK - 1, half)
            V.tensor_copy(C.step[:], C.cst2[:, PK:2 * PK])
            for u in range(NHP):
                dve.wait_ge(S["s_ev"], 2 * (u + 1))
                keys = [(sc[0:rows(t), t, u, :], *(x[0:rows(t), u, :] for x in best_of(t))) for t in range(NBLK)]
                best8(V, dve, C, keys, True)
                best8(V, dve, C, keys, False)
            for t in range(2):
                for part in range(CHOICE_PARTS):
                    choice_part(V, dve, C, t, part, *best_of(t), [w[:] for w in wide])

        @block.tensor
        def _(pe):
            M = nc.tensor.matmul
            pe.wait_ge(S["cst_in"], 48)
            for t in range(NBLK):
                R = rows(t)
                pe.wait_ge(S["xs_done"], t + 1)
                for half in range(2):
                    if t >= 1:
                        pe.wait_ge(S["xf_done"], 2 * (t - 1) + half + 1)
                    for a in range(4):
                        c = 4 * half + a
                        last = nc.tensor.transpose(bank(half, R, a * R), xs[0:R, t % 2, c * P:(c + 1) * P],
                                                   ident[0:R, 0:R])
                    last.then_inc(S["tp_done"], 1)
            pe.wait_ge(S["xl_done"], 2 * NBLK)
            pe.wait_ge(S["key_in"], 16)

            def key_scores(u):
                pe.wait_ge(S["q_ev"], u + 1)
                if u >= 1:
                    pe.wait_ge(S["s_ev"], 2 * u)
                for t in range(NBLK):
                    R = rows(t)
                    last = M(PS[0:R, 6 * BANK + t * P:6 * BANK + (t + 1) * P], qT[:, u % 2, toks(t)],
                             keysT[:, u, :], start=True, stop=True)
                last.then_inc(S["s_mm"], 1)

            for u in range(NHP):
                pe.wait_ge(S["wl_done"], u + 1)
                if u >= 2:
                    pe.wait_ge(S["q_ev"], u - 1)
                for half in range(2):
                    for k in range(KD):
                        c = slice(k * P, (k + 1) * P)
                        for w, x in ((wh, xh), (wl, xh), (wh, xl)):
                            last = M(bank(2 + 2 * (u % 2) + half, HT), w[:, u % 2, c],
                                     x[:, k, half * HT:(half + 1) * HT],
                                     start=(k == 0 and w is wh and x is xh), stop=(k == KD - 1 and x is xl))
                last.then_inc(S["q_mm"], 1)
                if u >= 1:
                    key_scores(u - 1)
            key_scores(NHP - 1)
            for t in range(2):
                choice_turn(nc, pe, C, t, bank(0))


def peer_dense(nc, T, h, sems, C, xh, xl, IT, JT, cT):
    GROUPS = [(0, 2 * P, [0, 1]), (2 * P, NTOK, [2, 3, 4])]
    NGMAX = NTOK - 2 * P
    TU = BANK // NKEY
    CH = 32
    UC = CH // TU
    NU = NTOK // TU
    UP = 2 * P // TU
    NCH = NTOK // CH
    QG = NKEY // 4
    QC = 10
    Q4, Q2 = QC, QC + 18
    SPANS = [(0, q, q + 1, 0) for q in range(QC)] + \
            [(0, Q4, Q2, 4), (0, Q2, QG - 1, 2), (0, QG - 1, QG, 2),
             (1, 0, 1, 0), (1, 1, QG - 1, 0), (1, QG - 1, QG, 0)]
    U2 = UP + 4 * (Q2 - Q4)
    assert U2 + 2 * (QG - Q2) == NU
    ctx = ExitStack()
    with ctx:
        def sb(name, shape, dt=F32):
            return ctx.enter_context(nc.sbuf_tensor(name, shape, dt))

        PS = ctx.enter_context(nc.psum_tensor("psC", [P, 8 * BANK], F32))

        def bank(b, n=BANK, at=0, p0=0, p1=P):
            return PS[p0:p1, b * BANK + at:b * BANK + at + n]

        iota = C.iota
        rU = sb("rU", [P, 2, D])
        rV = sb("rV", [P, 2, D])
        Uh = sb("Uh", [P, 2, D], F32R)
        Ul = sb("Ul", [P, 2, D], F32R)
        Vh = sb("Vh", [P, 2, D], F32R)
        Vl = sb("Vl", [P, 2, D], F32R)
        ge = sb("ge", [P, NGMAX])
        wf = sb("wf", [P, NGMAX])
        Wh = sb("Wh", [P, 2, NGMAX + NS], F32R)
        Wl = sb("Wl", [P, 2, 2 * P], F32R)
        ohI = sb("ohI", [P, 4, TU, NKEY])
        ohJ = sb("ohJ", [P, 4, TU, NKEY])
        ohC = sb("ohC", [P, 4, TU, NKEY])
        gst = sb("gst", [P, 2, NKEY, CH])
        gr = sb("gr", [P, 2, NGMAX // CH, 4, CH])

        wide = [x[:].rearrange("p a t k -> p (a t k)").bitcast(BF16)[:, 0:PH * PK * PK]
                .rearrange("p (h k c) -> p h k c", k=PK, c=PK) for x in (ohI, ohJ, ohC)]
        names = """oh_done oh_mul oh_used gt_ev gw_out gw_done hU lU hV lV u_mm ge_done w_mul w_hi
            w_done v_mm y_added""".split()
        S = {n: sems.enter_context(nc.semaphore("c_" + n)) for n in names}
        rU_in = [sems.enter_context(nc.semaphore(f"c_rU{i}")) for i in range(2)]
        rV_in = [sems.enter_context(nc.semaphore(f"c_rV{i}")) for i in range(2)]
        gr_in = sems.enter_context(nc.semaphore("c_gr"))
        block = ctx.enter_context(nc.Block())

        def known_below(x, n):
            return isinstance(x, int) and x < n

        def over_quads(eng, quad):
            for g, a, b, n in SPANS:
                if b - a == 1:
                    quad(g, a, n)
                else:
                    with eng.Fori(a, b) as i:
                        quad(g, i, n)

        def unit_of(i, n, r):
            return (UP + 4 * (i - Q4) if n == 4 else U2 + 2 * (i - Q2)) + r

        def units_at(n, k):
            return [r for r in range(n) if (r // 2 if n == 4 else r) == k]

        @block.sync
        def _(sp):
            def load(s, j, k):
                if not known_below(s, 2):
                    sp.wait_ge(S["lU"], s - 1)
                sp.dma_start(rU[:, k, :], T["peer_uT"][bass.ds(j, 1), :, :].rearrange("a p c -> (a p) c"))\
                    .then_inc(rU_in[k], 16)
                if not known_below(s, 2):
                    sp.wait_ge(S["lV"], s - 1)
                sp.dma_start(rV[:, k, :], T["peer_v"][bass.ds(j, 1), :, :].rearrange("a p c -> (a p) c"))\
                    .then_inc(rV_in[k], 16)

            def load_weights(g, q):
                lo, hi, _ = GROUPS[g]
                if not known_below(QG * g + q, 2):
                    sp.wait_ge(S["w_mul"], 4 * (QG * g + q - 1))
                src = T["gates"][lo // CH:hi // CH, :, bass.ds(4 * q, 4), :].rearrange("u p j n -> p u (j n)")
                dst = gr[:, bass.ds(q % 2, 1), 0:(hi - lo) // CH, :, :].rearrange("p a u j n -> p (a u) (j n)")
                sp.dma_start(dst, src).then_inc(gr_in, 16)

            def loads(g, q, ks=range(4)):
                for k in ks:
                    load(NKEY * g + 4 * q + k, 4 * q + k, k % 2)

            loads(0, 0, (0, 1))
            sp.wait_ge(S["gw_done"], UP)
            load_weights(0, 0)
            loads(0, 0, (2, 3))
            with sp.Fori(1, QG) as i:
                load_weights(0, i)
                loads(0, i)
            loads(1, 0, (0, 1))
            sp.wait_ge(S["gw_done"], NU)
            load_weights(1, 0)
            loads(1, 0, (2, 3))
            with sp.Fori(1, QG) as i:
                load_weights(1, i)
                loads(1, i)

        @block.gpsimd
        def _(pool):
            def weigh_one_hots(u, k, slots):
                pool.wait_ge(S["oh_done"], u + 1)
                if not known_below(u, 4):
                    pool.wait_ge(S["oh_used"], u + 1 - slots)
                w = cT[:, bass.ds(TU * u, TU)].unsqueeze(2).broadcast_to([P, TU, NKEY])
                nc.gpsimd.tensor_tensor(ohC[:, k, :, :], ohJ[:, k, :, :], w, ALU.mult).then_inc(S["oh_mul"], 1)

            def store(w):
                pool.wait_ge(S["gt_ev"], UC * (w + 1))
                pool.dma_start(T["gates"][bass.ds(w, 1), :, :, :].rearrange("u p j n -> (u p) (j n)"),
                               gst[:, bass.ds(w % 2, 1), :, :].rearrange("p a j n -> p (a j n)"))\
                    .then_inc(S["gw_out"], 16)

            def stored(w):
                pool.wait_ge(S["gw_out"], 16 * (w + 1))
                pool.nop(nofuse=True).then_inc(S["gw_done"], UC)

            def chunk(w, store_last=False, slots=4):
                for r in range(UC):
                    weigh_one_hots(UC * w + r, r % slots, slots)
                    if store_last and r == 2:
                        store(w - 1)
                    if store_last and r == UC - 1:
                        stored(w - 1)

            chunk(0)
            with pool.Fori(1, UP // UC) as i:
                chunk(i, store_last=True)
            store(UP // UC - 1)
            stored(UP // UC - 1)
            pool.wait_ge(C.sems["sT_act"], 3 * NBLK)
            for a, b, slots in ((UP // UC, U2 // UC, 4), (U2 // UC, NCH, 2)):
                with pool.Fori(a, b) as i:
                    chunk(i, slots=slots)
                    store(i)
                    stored(i)

        @block.scalar
        def _(act):
            A = nc.scalar.activation

            def high_u(s, k):
                act.wait_ge(rU_in[k], 8 * (s - k) + 16)
                if not known_below(s, 2):
                    act.wait_ge(S["u_mm"], s - 1)
                A(Uh[:, k, :], rU[:, k, :], ACT.Copy).then_inc(S["hU"], 1)

            def high_v(s, k):
                act.wait_ge(rV_in[k], 8 * (s - k) + 16)
                if not known_below(s, 2):
                    act.wait_ge(S["v_mm"], s - 1)
                A(Vh[:, k, :], rV[:, k, :], ACT.Copy).then_inc(S["hV"], 1)

            def unit_out(u, k):
                if not known_below(u, 2 * UC):
                    act.wait_ge(S["gw_done"], u + 1 - 2 * UC)
                act.wait_ge(S["oh_used"], u + 1)
                act.nop(nofuse=True)
                dst = gst[:, bass.ds(u // UC % 2, 1), :, bass.ds(TU * (u % UC), TU)]
                A(dst.rearrange("p a j n -> p (a n) j"), bank(4 + k).rearrange("p (n j) -> p n j", n=TU),
                  ACT.Copy).then_inc(S["gt_ev"], 1)

            high_u(0, 0)
            high_u(1, 1)
            high_v(0, 0)
            for r in range(2 * UC):
                unit_out(r, r % 2)
            with act.Fori(1, UP // (2 * UC)) as i:
                for r in range(2 * UC):
                    unit_out(2 * UC * i + r, r % 2)

            def quad(g, i, n):
                NG = GROUPS[g][1] - GROUPS[g][0]
                end = g == 1 and isinstance(i, int) and i == QG - 1
                for k in range(4):
                    s = NKEY * g + 4 * i + k
                    act.wait_ge(S["u_mm"], s + 1)
                    if not known_below(s, 1):
                        act.wait_ge(S["w_mul"], s)
                    A(ge[:, 0:NG], bank(6 + k % 2, NG), ACT.Gelu).then_inc(S["ge_done"], 1)
                    if not (end and k >= 2):
                        high_u(s + 2, k % 2)
                    if not (end and k == 3):
                        high_v(s + 1, 1 - k % 2)
                    if known_below(s, 3 * CHOICE_PARTS + 2):
                        b, part = divmod(s, CHOICE_PARTS)
                        if part == 3 and b < 3:
                            choice_exp(A, act, C, 2 + b)
                        if part == 1 and b >= 1:
                            choice_out(A, act, C, 1 + b, bank(4), (IT, JT, cT))
                    for r in units_at(n, k - 2):
                        unit_out(unit_of(i, n, r), r % 2)

            over_quads(act, quad)

        @block.vector
        def _(dve):
            V = nc.vector

            def low_u(s, k):
                dve.wait_ge(S["hU"], s + 1)
                V.tensor_tensor(Ul[:, k, :], rU[:, k, :], Uh[:, k, :].bitcast(F32), ALU.subtract)\
                    .then_inc(S["lU"], 1)

            def low_v(s, k):
                dve.wait_ge(S["hV"], s + 1)
                V.tensor_tensor(Vl[:, k, :], rV[:, k, :], Vh[:, k, :].bitcast(F32), ALU.subtract)\
                    .then_inc(S["lV"], 1)

            def one_hots(u, k, slots=4):
                if not known_below(u, 4):
                    dve.wait_ge(S["oh_used"], u + 1 - slots)
                keys = iota.unsqueeze(1).broadcast_to([P, TU, NKEY])
                col = bass.ds(TU * u, TU)
                V.tensor_tensor(ohJ[:, k, :, :], keys, JT[:, col].unsqueeze(2).broadcast_to([P, TU, NKEY]),
                                ALU.is_equal)
                V.tensor_tensor(ohI[:, k, :, :], keys, IT[:, col].unsqueeze(2).broadcast_to([P, TU, NKEY]),
                                ALU.is_equal).then_inc(S["oh_done"], 1)

            low_u(0, 0)
            low_u(1, 1)
            low_v(0, 0)
            for r in range(4):
                one_hots(r, r)
            with dve.Fori(1, UP // 4) as i:
                for r in range(4):
                    one_hots(4 * i + r, r)

            def quad(g, i, n):
                lo, hi, blocks = GROUPS[g]
                NG = hi - lo
                end = g == 1 and isinstance(i, int) and i == QG - 1
                dve.wait_ge(gr_in, 16 * (QG * g + i + 1))
                for k in range(4):
                    s = NKEY * g + 4 * i + k
                    dve.wait_ge(S["ge_done"], s + 1)
                    if not known_below(s, 1):
                        dve.wait_ge(S["w_done"], s)
                    w = gr[:, bass.ds(i % 2, 1), 0:NG // CH, k, :].rearrange("p a u n -> p (a u) n")
                    V.tensor_tensor(wf[:, 0:NG].rearrange("p (u n) -> p u n", n=CH),
                                    ge[:, 0:NG].rearrange("p (u n) -> p u n", n=CH), w, ALU.mult)\
                        .then_inc(S["w_mul"], 1)
                    dve.wait_ge(S["w_mul"], s + 1)
                    if not known_below(s, 2):
                        dve.wait_ge(S["v_mm"], s - 1)
                    V.tensor_copy(Wh[:, k % 2, 0:NG], wf[:, 0:NG]).then_inc(S["w_hi"], 1)
                    dve.wait_ge(S["w_hi"], s + 1)
                    low = V.tensor_tensor(Wl[:, k % 2, :], wf[:, 0:2 * P], Wh[:, k % 2, 0:2 * P].bitcast(F32),
                                          ALU.subtract)
                    if NG > 2 * P:
                        low = V.tensor_tensor(Wh[:, k % 2, NG:NG + NS], wf[:, 2 * P:NG],
                                              Wh[:, k % 2, 2 * P:NG].bitcast(F32), ALU.subtract)
                    low.then_inc(S["w_done"], 1)
                    if not (end and k >= 2):
                        low_u(s + 2, k % 2)
                    if not (end and k == 3):
                        low_v(s + 1, 1 - k % 2)
                    if known_below(s, 3 * CHOICE_PARTS):
                        b, part = divmod(s, CHOICE_PARTS)
                        choice_part(V, dve, C, 2 + b, part, C.mv[:, b], C.mi[:, b], wide)
                    for r in units_at(n, k):
                        one_hots(unit_of(i, n, r), r % n, n)
                if isinstance(i, int) and (g, i) == (0, QC - 1):
                    dve.wait_ge(C.sems["sT_act"], 3 * NBLK)
                if isinstance(i, int) and i == QG - 1:
                    dve.wait_ge(S["v_mm"], NKEY * (g + 1))
                    for b, t in enumerate(blocks):
                        R = rows(t)
                        sums = PS[:, 2 * b * BANK:2 * (b + 1) * BANK]
                        V.tensor_tensor(h[0:R, t, :], sums[0:R], h[0:R, t, :], ALU.add)\
                            .then_inc(S["y_added"], 1)
                        if R < P:
                            dve.wait_ge(S["y_added"], NBLK)
                            V.tensor_tensor(h[0:R, t, :], sums[R:2 * R], h[0:R, t, :], ALU.add)

            over_quads(dve, quad)

        @block.tensor
        def _(pe):
            M = nc.tensor.matmul

            def weights(u, k):
                pe.wait_ge(S["oh_mul"], u + 1)
                if not known_below(u, 2):
                    pe.wait_ge(S["gt_ev"], u - 1)
                for a in range(TU):
                    last = M(bank(4 + k % 2, NKEY, a * NKEY), ohI[:, k, a, :], ohC[:, k, a, :], start=True, stop=True)
                last.then_inc(S["oh_used"], 1)

            for r in range(4):
                weights(r, r)
            with pe.Fori(1, UP // 4) as i:
                for r in range(4):
                    weights(4 * i + r, r)

            def up(g, s, k):
                lo, hi, _ = GROUPS[g]
                pe.wait_ge(S["lU"], s + 1)
                if not known_below(s, 2):
                    pe.wait_ge(S["ge_done"], s - 1)
                for d in range(KD):
                    c = slice(d * P, (d + 1) * P)
                    for a, x in ((Uh, xh), (Ul, xh), (Uh, xl)):
                        last = M(bank(6 + k, hi - lo), a[:, k, c], x[:, d, lo:hi],
                                 start=(d == 0 and a is Uh and x is xh), stop=(d == KD - 1 and x is xl))
                last.then_inc(S["u_mm"], 1)

            def down(g, s, k, first, final):
                pe.wait_ge(S["w_done"], s + 1)
                pe.wait_ge(S["lV"], s + 1)
                for b, t in enumerate(GROUPS[g][2]):
                    R = rows(t)
                    for n in range(2):
                        c = slice(n * 512, (n + 1) * 512)
                        if R == P:
                            parts = ((P, Wh, Vh), (P, Wl, Vh), (P, Wh, Vl))
                        else:
                            parts = ((2 * R, Wh, Vh), (R, Wh, Vl))
                        for a, (m, w, v) in enumerate(parts):
                            last = M(bank(2 * b + n, p1=m), w[:, k, b * P:b * P + m], v[:, k, c],
                                     start=(first and a == 0), stop=(final and a == len(parts) - 1),
                                     skip_group_check=True)
                last.then_inc(S["v_mm"], 1)

            def quad(g, i, n):
                s0 = NKEY * g + 4 * i
                first, final = (isinstance(i, int) and i == x for x in (0, QG - 1))
                if first:
                    up(g, s0, 0)
                for k in range(4):
                    if not (final and k == 3):
                        up(g, s0 + k + 1, 1 - k % 2)
                    if first and g == 1 and k == 0:
                        pe.wait_ge(S["y_added"], len(GROUPS[0][2]))
                        pe.wait_ge(S["gt_ev"], NU)
                    down(g, s0 + k, k % 2, first and k == 0, final and k == 3)
                    if known_below(s0 + k, 3 * CHOICE_PARTS + 1) and (s0 + k) % CHOICE_PARTS == 0 and s0 + k > 0:
                        if s0 + k == CHOICE_PARTS:
                            pe.wait_ge(S["gt_ev"], UP)
                        choice_turn(nc, pe, C, 1 + (s0 + k) // CHOICE_PARTS, bank(4))
                    for r in units_at(n, k - 1):
                        weights(unit_of(i, n, r), r)

            over_quads(pe, quad)


def final_norm(nc, T, h, sems):
    ctx = ExitStack()
    with ctx:
        def sb(name, shape, dt=F32):
            return ctx.enter_context(nc.sbuf_tensor(name, shape, dt))

        st = sb("stD", [P, 20])
        junk = sb("junk", [P, NBLK, D])
        gfin = sb("gfin", [P, D])
        y = sb("y", [P, NBLK, D])
        S = {n: sems.enter_context(nc.semaphore("d_" + n)) for n in "g_in sq ms rstd y_done y_out".split()}
        block = ctx.enter_context(nc.Block())

        @block.sync
        def _(sp):
            sp.dma_start(gfin[:], T["norm_final"].broadcast_to([P, D])).then_inc(S["g_in"], 16)
            for t in range(NBLK):
                sp.wait_ge(S["y_done"], t + 1)
                dst = T["y_p"][toks(t), :] if t < 4 else T["y_s"]
                sp.dma_start(dst, y[0:rows(t), t, :]).then_inc(S["y_out"], 16)
            sp.wait_ge(S["y_out"], 16 * NBLK)

        @block.scalar
        def _(act):
            for t in range(NBLK):
                R = rows(t)
                nc.scalar.activation(junk[0:R, t, :], h[0:R, t, :], ACT.Square, accum_out=st[0:R, t:t + 1])\
                    .then_inc(S["sq"], 1)

        @block.gpsimd
        def _(pool):
            pool.memset(st[:, 19:20], -0.5).then_inc(S["ms"], 1)
            for t in range(NBLK):
                R = rows(t)
                pool.wait_ge(S["sq"], t + 1)
                nc.gpsimd.tensor_scalar(st[0:R, 5 + t:6 + t], st[0:R, t:t + 1], 1.0 / D, EPS, ALU.mult, ALU.add)\
                    .then_inc(S["ms"], 1)
                pool.wait_ge(S["ms"], t + 2)
                nc.gpsimd.tensor_tensor(st[0:R, 10 + t:11 + t], st[0:R, 5 + t:6 + t], st[0:R, 19:20], ALU.pow)\
                    .then_inc(S["rstd"], 1)

        @block.vector
        def _(dve):
            dve.wait_ge(S["g_in"], 16)
            for t in range(NBLK):
                R = rows(t)
                dve.wait_ge(S["rstd"], t + 1)
                nc.vector.scalar_tensor_tensor(out=y[0:R, t, :], in0=h[0:R, t, :], scalar=st[0:R, 10 + t:11 + t],
                                               in1=gfin[0:R, :], op0=ALU.mult, op1=ALU.mult)\
                    .then_inc(S["y_done"], 1)


def build(nc, T):
    ctx = ExitStack()
    with ctx:
        h = ctx.enter_context(nc.sbuf_tensor("h", [P, NBLK, D], F32))
        block_a(nc, T, h, ctx)
        x = [ctx.enter_context(nc.sbuf_tensor(n, [P, KD, NTOK], F32R)) for n in ("xh", "xl")]
        IJ = [ctx.enter_context(nc.sbuf_tensor(n, [P, NTOK], F32)) for n in ("IT", "JT", "cT")]
        C = Choice(nc, ctx)
        peer_select(nc, T, h, ctx, C, *x, *IJ)
        peer_dense(nc, T, h, ctx, C, *x, *IJ)
        final_norm(nc, T, h, ctx)


HEADS = [0, 4, 1, 5, 2, 6, 3, 7]


def constants():
    c = np.zeros((P, C_ALL), np.float32)
    c[:, C_ID:C_ID + P] = np.eye(P)
    c[:, C_IOTA:C_IOTA + P] = np.arange(P)
    q, k = np.arange(P)[:, None], np.arange(P)[None, :]
    c[:, C_CAUSAL:C_CAUSAL + P] = np.where(k <= q, 0, NEG)
    q, k = np.arange(NS)[:, None], np.arange(NS)[None, :]
    c[:NS, C_NEW:C_NEW + NS] = np.where((q // NQ == k // NQ) & (k <= q), 0, NEG)
    same = np.zeros((NS, NB, 8, NQ), np.float32)
    for tok in range(NS):
        same[tok, tok // NQ, :, tok % NQ] = 1
    c[:NS, C_SAME:C_SAME + 512] = same.reshape(NS, 512)
    inv = np.float32(10000.0) ** (-np.arange(32, dtype=np.float32) / np.float32(32))
    pos = np.zeros((NBLK, P), np.float32)
    pos[:4] = np.arange(SEQ).reshape(4, P)
    pos[4, :NS] = PAST + np.arange(NS) % NQ
    first = np.array([at for _, _, at in ROWS16], np.float32)
    c[:, C_FIRST:C_FIRST + PK] = first
    c[:, C_FIRST + PK:C_FIRST + 2 * PK] = np.diff(first, prepend=0)
    ang = pos[:, :, None] * inv
    cos, sin = np.cos(ang), np.sin(ang)
    c[:, C_COS:C_COS + 320] = np.concatenate([cos, cos], -1).transpose(1, 0, 2).reshape(P, 320)
    c[:, C_SIN:C_SIN + 320] = np.concatenate([-sin, sin], -1).transpose(1, 0, 2).reshape(P, 320)
    return c


def kernel(**inputs):
    import concourse.bacc as _bacc
    from concourse.bass_utils import run_bass_kernel_spmd as _run

    x = {k: np.asarray(v) for k, v in inputs.items()}
    n_pool = x["cache_mla_ckv"].shape[1]

    def chunks(w):
        return w.reshape(-1, P, w.shape[-1]).transpose(1, 0, 2)

    w_in = x["w_in"][0]
    dq = w_in[:, DQ:DQ + 512].reshape(D, 8, 64)[:, HEADS].reshape(D, 512)
    w_in = np.concatenate([w_in[:, :DQ], dq, w_in[:, DK:]], 1)
    w_uq = x["w_uq"][0].reshape(256, 8, 96)
    w_o = x["w_o"][0]
    w_o = np.concatenate([w_o[:512], w_o[512:].reshape(8, 64, D)[HEADS].reshape(512, D)], 0)
    ckv, kr = x["cache_mla_ckv"][0], x["cache_mla_kr"][0]
    kv = x["cache_dsa_kv"][0].reshape(n_pool, PAGE, 2, 128)
    gains = [x[n][0].reshape(-1, P).T for n in ("norm_mix", "norm_mem", "mem_norm", "norm_ffn", "mla_q_norm")]
    mk = x["cache_mem_k"][0].reshape(NB, 256, 2, P).transpose(0, 3, 2, 1)
    mv = x["cache_mem_v"][0].reshape(NB, 2, P, 256).transpose(0, 2, 1, 3)
    arrays = {
        "cst": constants(),
        "x_prompt": x["x_prompt"], "x_sample": x["x_sample"], "mem_prompt": x["mem_prompt"],
        "gcol": np.concatenate(gains, 1), "mla_kv_norm": x["mla_kv_norm"], "norm_final": x["norm_final"][None],
        "page_table": x["page_table"].reshape(1, -1),
        "w_in": chunks(w_in),
        "w_uqn": chunks(w_uq[:, :, :64].reshape(256, 512)), "w_uqr": chunks(w_uq[:, :, 64:].reshape(256, 256)),
        "w_ukT": chunks(x["w_uk"][0].transpose(1, 2, 0).reshape(512, 128)),
        "w_uv": x["w_uv"][0].reshape(128, 512),
        "w_o": chunks(w_o),
        "wq_x": chunks(x["wq_x"][0]), "wkv_x": chunks(np.concatenate([x["wk_x"][0], x["wv_x"][0]], 1)),
        "wo_x": chunks(x["wo_x"][0]),
        "mem_cache": np.concatenate([mk, mv], 2),
        "ikT": x["cache_dsa_idx"][0].transpose(0, 2, 1), "krT": kr.transpose(0, 2, 1),
        "poolM": np.concatenate([ckv.transpose(0, 2, 1), ckv], 2),
        "poolD": np.concatenate([kv[:, :, 0].transpose(0, 2, 1), kv[:, :, 1]], 2),
        "w_pq": x["w_pq"][0].reshape(KD, P, 2 * PH, P).transpose(2, 1, 0, 3).reshape(2 * PH, P, D),
        "keysT": x["peer_keys"][0].reshape(2 * PH, NKEY, P).transpose(2, 0, 1),
        "peer_uT": x["peer_u"][0].reshape(NKEY, NKEY, KD, P).transpose(1, 3, 2, 0).reshape(NKEY, P, D),
        "peer_v": x["peer_v"][0].reshape(NKEY, NKEY, D).transpose(1, 0, 2),
    }
    outs = {
        "y_p": (1, SEQ, D), "y_s": (NB, NQ, D),
        "new_ckv_p": (1, 1, SEQ, 128), "new_kr_p": (1, 1, SEQ, 32), "new_kv_p": (1, 1, SEQ, 2, 2, 64),
        "new_idx_p": (1, 1, SEQ, 64), "new_mem_k_p": (1, 1, 256, 4, 64), "new_mem_v_p": (1, 1, 256, 4, 64),
        "new_ckv_s": (1, NB, NQ, 128), "new_kr_s": (1, NB, NQ, 32), "new_kv_s": (1, NB, NQ, 2, 2, 64),
        "new_idx_s": (1, NB, NQ, 64),
    }
    flat = {"y_p": (SEQ, D), "y_s": (NS, D)}
    for n, s in outs.items():
        toks_ = int(np.prod(s[:3])) if n[:3] == "new" else flat[n][0]
        flat[n] = (toks_, int(np.prod(s)) // toks_)
    nc = _bacc.Bacc("TRN2", target_bir_lowering=False, num_devices=1)
    T = {"n_pool": n_pool}
    arrays = {n: np.ascontiguousarray(a) for n, a in arrays.items()}
    for n, a in arrays.items():
        T[n] = nc.dram_tensor("in_" + n, a.shape, mybir.dt.from_np(a.dtype), kind="ExternalInput").ap()
    for n, s in flat.items():
        T[n] = nc.dram_tensor("out_" + n, s, F32, kind="ExternalOutput").ap()
    T["gates"] = nc.dram_tensor("gates", (NTOK // 32, P, NKEY, 32), F32, kind="Internal").ap()
    build(nc, T)
    r = _run(nc, [{"in_" + n: a for n, a in arrays.items()}], core_ids=[0])
    return tuple(np.asarray(r.results[0]["out_" + n]).reshape(s) for n, s in outs.items())
```
